# Optimizing a Trainium2 kernel written in Bass

```python
import jax, jax.numpy as jnp
from jax import lax
import numpy as np
import math

D_MODEL = 1024
BATCH = 1
SEQ = 256
DEPTH = 2

HEAD_DIM = 64
MIX_WIDTH = D_MODEL
FOX_HEADS = MIX_WIDTH // (4 * HEAD_DIM)
MOBA_HEADS = MIX_WIDTH // (4 * HEAD_DIM)
RWKV_HEADS = MIX_WIDTH // (2 * HEAD_DIM)
FOX_WIDTH = FOX_HEADS * HEAD_DIM
MOBA_WIDTH = MOBA_HEADS * HEAD_DIM
RWKV_WIDTH = RWKV_HEADS * HEAD_DIM
RWKV_DECAY_LORA = 64
RWKV_ICLR_LORA = 64
RWKV_GATE_LORA = 160
RWKV_GN_EPS = 64e-5
FOX_IN = 3 * FOX_WIDTH + FOX_HEADS
MOBA_IN = 3 * MOBA_WIDTH
RWKV_IN = 3 * RWKV_WIDTH + RWKV_DECAY_LORA + RWKV_ICLR_LORA + RWKV_GATE_LORA
IN_WIDTH = FOX_IN + MOBA_IN + RWKV_IN
FOX_QBLOCK = 128
MOBA_BLOCK = 256
MOBA_TOPK = 3
MOBA_QCHUNK = 32
ROPE_THETA = 500000.0
ROPE_DIM = HEAD_DIM // 4
FFN_DIM = 2816
MEM_LEN = 256
XATTN_HEADS = 4
XATTN_HEAD_DIM = 128
XATTN_WIDTH = XATTN_HEADS * XATTN_HEAD_DIM
NORM_EPS = 1e-6


def rms_norm(t, g):
    tf = t.astype(jnp.float32)
    y = tf * lax.rsqrt(jnp.mean(tf * tf, axis=-1, keepdims=True) + NORM_EPS)
    return (y * g).astype(t.dtype)

def swiglu(h, w_in, w_out):
    gate, up = jnp.split(h @ w_in, 2, axis=-1)
    return (jax.nn.silu(gate) * up) @ w_out

def split_heads(t, n_heads):
    B, S, _ = t.shape
    return t.reshape(B, S, n_heads, HEAD_DIM).transpose(0, 2, 1, 3)

def merge_heads(t):
    B, H, S, d = t.shape
    return t.transpose(0, 2, 1, 3).reshape(B, S, H * d)

def rope_tables(positions):
    inv_freq = ROPE_THETA ** (-jnp.arange(0, ROPE_DIM, 2, dtype=jnp.float32) / ROPE_DIM)
    ang = positions.astype(jnp.float32)[..., None] * inv_freq
    return jnp.cos(ang), jnp.sin(ang)

def apply_partial_rope(t, cos, sin):
    half = ROPE_DIM // 2
    x1, x2, rest = t[..., :half], t[..., half:ROPE_DIM], t[..., ROPE_DIM:]
    c, s = cos[:, None], sin[:, None]
    out = jnp.concatenate([x1 * c - x2 * s, x2 * c + x1 * s, rest.astype(jnp.float32)], axis=-1)
    return out.astype(t.dtype)

def forgetting_attention(q, k, v, log_f):
    B, H, S, d = q.shape
    c = jnp.cumsum(log_f, axis=-1)
    n_qb = S // FOX_QBLOCK
    q_blocks = q.reshape(B, H, n_qb, FOX_QBLOCK, d).transpose(2, 0, 1, 3, 4)
    c_blocks = c.reshape(B, H, n_qb, FOX_QBLOCK).transpose(2, 0, 1, 3)
    k_pos = jnp.arange(S)
    scale = d ** -0.5

    def block(args):
        i, q_i, c_i = args
        s = jnp.einsum('bhqd,bhkd->bhqk', q_i, k).astype(jnp.float32) * scale
        s = s + c_i[..., None] - c[:, :, None, :]
        q_pos = i * FOX_QBLOCK + jnp.arange(FOX_QBLOCK)
        s = jnp.where(k_pos[None, :] <= q_pos[:, None], s, -jnp.inf)
        p = jax.nn.softmax(s, axis=-1).astype(v.dtype)
        return jnp.einsum('bhqk,bhkd->bhqd', p, v)

    out = lax.map(block, (jnp.arange(n_qb), q_blocks, c_blocks))
    return out.transpose(1, 2, 0, 3, 4).reshape(B, H, S, d)

def fox_mixer(z, f_bias, q_gain, k_gain):
    q, k, v, f = jnp.split(z, [FOX_WIDTH, 2 * FOX_WIDTH, 3 * FOX_WIDTH], axis=-1)
    q = rms_norm(split_heads(q, FOX_HEADS), q_gain)
    k = rms_norm(split_heads(k, FOX_HEADS), k_gain)
    v = split_heads(v, FOX_HEADS)
    log_f = jax.nn.log_sigmoid(f.astype(jnp.float32) + f_bias).transpose(0, 2, 1)
    return merge_heads(forgetting_attention(q, k, v, log_f))

def moba_attention(q, k, v):
    B, H, S, d = q.shape
    s_pad = -(-S // MOBA_BLOCK) * MOBA_BLOCK
    pad = ((0, 0), (0, 0), (0, s_pad - S), (0, 0))
    k_pad = jnp.pad(k, pad)
    v_pad = jnp.pad(v, pad)
    n_blk = s_pad // MOBA_BLOCK
    top_k = min(MOBA_TOPK, n_blk)
    k_blk = k_pad.reshape(B, H, n_blk, MOBA_BLOCK, d)
    v_blk = v_pad.reshape(B, H, n_blk, MOBA_BLOCK, d)
    k_mean = jnp.mean(k_blk.astype(jnp.float32), axis=3)
    n_chunk = S // MOBA_QCHUNK
    q_chunks = q.reshape(B, H, n_chunk, MOBA_QCHUNK, d).transpose(2, 0, 1, 3, 4)
    b_idx = jnp.arange(B)[:, None, None, None]
    h_idx = jnp.arange(H)[None, :, None, None]
    blk_ids = jnp.arange(n_blk)
    scale = d ** -0.5

    def chunk(args):
        i, q_i = args
        q_start = i * MOBA_QCHUNK
        q_blk = q_start // MOBA_BLOCK
        gate = jnp.einsum('bhqd,bhnd->bhqn', q_i.astype(jnp.float32), k_mean)
        gate = jnp.where(blk_ids < q_blk, gate, -jnp.inf)
        _, sel = lax.top_k(gate, top_k)
        valid = sel < q_blk
        k_sel = k_blk[b_idx, h_idx, sel]
        v_sel = v_blk[b_idx, h_idx, sel]
        s_sel = jnp.einsum('bhqd,bhqnkd->bhqnk', q_i, k_sel).astype(jnp.float32) * scale
        s_sel = jnp.where(valid[..., None], s_sel, -jnp.inf)
        s_sel = s_sel.reshape(B, H, MOBA_QCHUNK, top_k * MOBA_BLOCK)
        blk_start = q_blk * MOBA_BLOCK
        k_own = lax.dynamic_slice_in_dim(k_pad, blk_start, MOBA_BLOCK, axis=2)
        v_own = lax.dynamic_slice_in_dim(v_pad, blk_start, MOBA_BLOCK, axis=2)
        s_own = jnp.einsum('bhqd,bhkd->bhqk', q_i, k_own).astype(jnp.float32) * scale
        q_pos = q_start + jnp.arange(MOBA_QCHUNK)
        k_pos = blk_start + jnp.arange(MOBA_BLOCK)
        s_own = jnp.where(k_pos[None, :] <= q_pos[:, None], s_own, -jnp.inf)
        p = jax.nn.softmax(jnp.concatenate([s_sel, s_own], axis=-1), axis=-1).astype(v.dtype)
        p_sel = p[..., :top_k * MOBA_BLOCK].reshape(B, H, MOBA_QCHUNK, top_k, MOBA_BLOCK)
        p_own = p[..., top_k * MOBA_BLOCK:]
        return (jnp.einsum('bhqnk,bhqnkd->bhqd', p_sel, v_sel)
                + jnp.einsum('bhqk,bhkd->bhqd', p_own, v_own))

    out = lax.map(chunk, (jnp.arange(n_chunk), q_chunks))
    return out.transpose(1, 2, 0, 3, 4).reshape(B, H, S, d)

def moba_mixer(z, cos, sin, q_gain, k_gain):
    q, k, v = jnp.split(z, [MOBA_WIDTH, 2 * MOBA_WIDTH], axis=-1)
    q = apply_partial_rope(rms_norm(split_heads(q, MOBA_HEADS), q_gain), cos, sin)
    k = apply_partial_rope(rms_norm(split_heads(k, MOBA_HEADS), k_gain), cos, sin)
    v = split_heads(v, MOBA_HEADS)
    return merge_heads(moba_attention(q, k, v))

def rwkv7_mixer(z, mu, w0, w2, a0, a2, g2, k_k, k_a, r_k, ln_w, ln_b):
    B, S, _ = z.shape
    zf = z.astype(jnp.float32)
    z_prev = jnp.pad(zf, ((0, 0), (1, 0), (0, 0)))[:, :S]
    zf = zf + (z_prev - zf) * mu
    W = RWKV_WIDTH
    r, k, v, w_lo, a_lo, g_lo = jnp.split(
        zf, [W, 2 * W, 3 * W, 3 * W + RWKV_DECAY_LORA, 3 * W + RWKV_DECAY_LORA + RWKV_ICLR_LORA], axis=-1)
    w_raw = w0 + jnp.tanh(w_lo) @ w2
    decay = jnp.exp(-jnp.exp(-jax.nn.softplus(-w_raw) - 0.5))
    a = jax.nn.sigmoid(a0 + a_lo @ a2)
    g = jax.nn.sigmoid(g_lo) @ g2
    kk = k * k_k
    k = k * (1.0 + (a - 1.0) * k_a)

    def hd(t):
        return t.reshape(B, S, RWKV_HEADS, HEAD_DIM)

    r, k, v, decay, a, kk = hd(r), hd(k), hd(v), hd(decay), hd(a), hd(kk)
    kk = kk / jnp.maximum(jnp.sqrt(jnp.sum(kk * kk, axis=-1, keepdims=True)), 1e-12)

    def step(state, inp):
        r_t, w_t, k_t, v_t, kk_t, a_t = inp
        sa = jnp.einsum('bhij,bhj->bhi', state, -kk_t)
        state = (state * w_t[:, :, None, :] + sa[..., None] * (kk_t * a_t)[:, :, None, :]
                 + v_t[..., None] * k_t[:, :, None, :])
        return state, jnp.einsum('bhij,bhj->bhi', state, r_t)

    xs = tuple(t.transpose(1, 0, 2, 3) for t in (r, decay, k, v, kk, a))
    state0 = jnp.zeros((B, RWKV_HEADS, HEAD_DIM, HEAD_DIM), jnp.float32)
    _, ys = lax.scan(step, state0, xs)
    y = ys.transpose(1, 0, 2, 3)
    mean = jnp.mean(y, axis=-1, keepdims=True)
    var = jnp.mean(jnp.square(y - mean), axis=-1, keepdims=True)
    y = ((y - mean) * lax.rsqrt(var + RWKV_GN_EPS)).reshape(B, S, W) * ln_w + ln_b
    bonus = (jnp.sum(r * k * r_k, axis=-1, keepdims=True) * v).reshape(B, S, W)
    return ((y + bonus) * g).astype(z.dtype)

def memory_cross_attention(h, m, w_q, w_kv, q_gain, k_gain, w_o):
    B, S, _ = h.shape
    M = m.shape[1]
    q = rms_norm((h @ w_q).reshape(B, S, XATTN_HEADS, XATTN_HEAD_DIM), q_gain)
    kv = (m @ w_kv).reshape(B, M, 2, XATTN_HEADS, XATTN_HEAD_DIM)
    k = rms_norm(kv[:, :, 0], k_gain)
    v = kv[:, :, 1]
    s = jnp.einsum('bqhd,bkhd->bhqk', q, k).astype(jnp.float32) * (XATTN_HEAD_DIM ** -0.5)
    p = jax.nn.softmax(s, axis=-1).astype(v.dtype)
    o = jnp.einsum('bhqk,bkhd->bqhd', p, v).reshape(B, S, XATTN_WIDTH)
    return o @ w_o

def first_inputs(seed: int = 0) -> dict:
    key = jax.random.key(seed)
    ks = iter(jax.random.split(key, 64))
    L, D = DEPTH, D_MODEL

    def nrm(shape, scale):
        return jax.random.normal(next(ks), shape, jnp.float32) * scale

    def gain(shape):
        return 1.0 + nrm(shape, 0.02)

    x = nrm((BATCH, SEQ, D), 1.0)
    mem = nrm((BATCH, MEM_LEN, D), 1.0)
    offset = jax.random.randint(next(ks), (BATCH, 1), 0, SEQ, dtype=jnp.int32)
    positions = (offset + jnp.arange(SEQ, dtype=jnp.int32)[None, :]).astype(jnp.int32)
    return {
        'x': x, 'mem': mem, 'positions': positions,
        'ffn1_norm': gain((L, D)),
        'ffn1_w_in': nrm((L, D, 2 * FFN_DIM), D ** -0.5),
        'ffn1_w_out': nrm((L, FFN_DIM, D), FFN_DIM ** -0.5),
        'mix_norm': gain((L, D)),
        'mix_w_in': nrm((L, D, IN_WIDTH), D ** -0.5),
        'mix_w_out': nrm((L, MIX_WIDTH, D), MIX_WIDTH ** -0.5),
        'fox_f_bias': 3.0 + nrm((L, FOX_HEADS), 0.5),
        'fox_q_gain': gain((L, HEAD_DIM)),
        'fox_k_gain': gain((L, HEAD_DIM)),
        'moba_q_gain': gain((L, HEAD_DIM)),
        'moba_k_gain': gain((L, HEAD_DIM)),
        'rwkv_mu': jax.random.uniform(next(ks), (L, RWKV_IN), jnp.float32, 0.0, 1.0),
        'rwkv_w0': nrm((L, RWKV_WIDTH), 1.0) - 1.0,
        'rwkv_w2': nrm((L, RWKV_DECAY_LORA, RWKV_WIDTH), RWKV_DECAY_LORA ** -0.5),
        'rwkv_a0': nrm((L, RWKV_WIDTH), 0.5),
        'rwkv_a2': nrm((L, RWKV_ICLR_LORA, RWKV_WIDTH), RWKV_ICLR_LORA ** -0.5),
        'rwkv_g2': nrm((L, RWKV_GATE_LORA, RWKV_WIDTH), RWKV_GATE_LORA ** -0.5),
        'rwkv_k_k': 0.85 + nrm((L, RWKV_WIDTH), 0.05),
        'rwkv_k_a': 1.0 + nrm((L, RWKV_WIDTH), 0.05),
        'rwkv_r_k': nrm((L, RWKV_HEADS, HEAD_DIM), 0.1),
        'rwkv_ln_w': gain((L, RWKV_WIDTH)),
        'rwkv_ln_b': nrm((L, RWKV_WIDTH), 0.02),
        'xattn_norm': gain((L, D)),
        'xattn_mem_norm': gain((L, D)),
        'xattn_w_q': nrm((L, D, XATTN_WIDTH), D ** -0.5),
        'xattn_w_kv': nrm((L, D, 2 * XATTN_WIDTH), D ** -0.5),
        'xattn_q_gain': gain((L, XATTN_HEAD_DIM)),
        'xattn_k_gain': gain((L, XATTN_HEAD_DIM)),
        'xattn_w_out': nrm((L, XATTN_WIDTH, D), XATTN_WIDTH ** -0.5),
        'ffn2_norm': gain((L, D)),
        'ffn2_w_in': nrm((L, D, 2 * FFN_DIM), D ** -0.5),
        'ffn2_w_out': nrm((L, FFN_DIM, D), FFN_DIM ** -0.5),
    }

def first_block(x, mem, positions, ffn1_norm, ffn1_w_in, ffn1_w_out, mix_norm, mix_w_in, mix_w_out,
              fox_f_bias, fox_q_gain, fox_k_gain, moba_q_gain, moba_k_gain,
              rwkv_mu, rwkv_w0, rwkv_w2, rwkv_a0, rwkv_a2, rwkv_g2, rwkv_k_k, rwkv_k_a, rwkv_r_k,
              rwkv_ln_w, rwkv_ln_b, xattn_norm, xattn_mem_norm, xattn_w_q, xattn_w_kv,
              xattn_q_gain, xattn_k_gain, xattn_w_out, ffn2_norm, ffn2_w_in, ffn2_w_out):
    cos, sin = rope_tables(positions)
    for l in range(DEPTH):
        x = x + 0.5 * swiglu(rms_norm(x, ffn1_norm[l]), ffn1_w_in[l], ffn1_w_out[l]).astype(x.dtype)
        z = rms_norm(x, mix_norm[l]) @ mix_w_in[l]
        z_fox, z_moba, z_rwkv = jnp.split(z, [FOX_IN, FOX_IN + MOBA_IN], axis=-1)
        y_fox = fox_mixer(z_fox, fox_f_bias[l], fox_q_gain[l], fox_k_gain[l])
        y_rwkv = rwkv7_mixer(z_rwkv, rwkv_mu[l], rwkv_w0[l], rwkv_w2[l], rwkv_a0[l], rwkv_a2[l],
                             rwkv_g2[l], rwkv_k_k[l], rwkv_k_a[l], rwkv_r_k[l], rwkv_ln_w[l], rwkv_ln_b[l])
        y_moba = moba_mixer(z_moba, cos, sin, moba_q_gain[l], moba_k_gain[l])
        y = jnp.concatenate([y_fox, y_rwkv, y_moba], axis=-1) @ mix_w_out[l]
        x = x + y.astype(x.dtype)
        x = x + memory_cross_attention(rms_norm(x, xattn_norm[l]), rms_norm(mem, xattn_mem_norm[l]),
                                       xattn_w_q[l], xattn_w_kv[l], xattn_q_gain[l], xattn_k_gain[l],
                                       xattn_w_out[l]).astype(x.dtype)
        x = x + 0.5 * swiglu(rms_norm(x, ffn2_norm[l]), ffn2_w_in[l], ffn2_w_out[l]).astype(x.dtype)
    return x


CONV_WIDTH = 512
CONV_KSIZE = 3
ATTN_HEADS = 8
ATTN_WIDTH = ATTN_HEADS * HEAD_DIM
IDX_HEADS = 8
IDX_DIM = 64
INDEX_TOPK = 256
Q_BLOCK = 128
ROPE_THETA_2 = 10000.0
POOL_WINDOWS = (2, 4, 8, 16)
POOL_GROUPS = 4
POOL_WIDTH = 512
POOL_GROUP_DIM = POOL_WIDTH // POOL_GROUPS
N_BRANCHES = 3
RMS_EPS = 1e-6

IN_SPLITS = (CONV_WIDTH, CONV_WIDTH, CONV_WIDTH, CONV_WIDTH,
             ATTN_WIDTH, ATTN_WIDTH, ATTN_WIDTH, ATTN_WIDTH,
             IDX_HEADS * IDX_DIM, IDX_DIM, IDX_HEADS,
             POOL_WIDTH, POOL_WIDTH,
             N_BRANCHES * D_MODEL)
IN_WIDTH_2 = 4 * CONV_WIDTH + 4 * ATTN_WIDTH + IDX_HEADS * IDX_DIM + IDX_DIM + IDX_HEADS + 2 * POOL_WIDTH + N_BRANCHES * D_MODEL


def rms_norm_2(x, g):
    xf = x.astype(jnp.float32)
    y = xf * lax.rsqrt(jnp.mean(xf * xf, axis=-1, keepdims=True) + RMS_EPS)
    return (y * g.astype(jnp.float32)).astype(x.dtype)

def split_columns(p):
    out = []
    off = 0
    for n in IN_SPLITS:
        out.append(p[..., off:off + n])
        off += n
    return out

def rope_tables_2(seq_len, dim):
    inv = 1.0 / (ROPE_THETA_2 ** (jnp.arange(0, dim, 2, dtype=jnp.float32) / dim))
    ang = jnp.arange(seq_len, dtype=jnp.float32)[:, None] * inv[None, :]
    return jnp.cos(ang), jnp.sin(ang)

def apply_rope(x, cos, sin):
    xf = x.astype(jnp.float32)
    half = xf.shape[-1] // 2
    x1, x2 = xf[..., :half], xf[..., half:]
    c, s = cos[None, :, None, :], sin[None, :, None, :]
    return jnp.concatenate([x1 * c - x2 * s, x2 * c + x1 * s], axis=-1).astype(x.dtype)

def short_conv_mixer(b, c, xin, gate, conv_w, w_out):
    S = xin.shape[1]
    z = c * xin
    zp = jnp.pad(z, ((0, 0), (CONV_KSIZE - 1, 0), (0, 0)))
    y = conv_w[0] * zp[:, 0:S]
    for j in range(1, CONV_KSIZE):
        y = y + conv_w[j] * zp[:, j:j + S]
    y = b * y * jax.nn.silu(gate)
    return y @ w_out

def sparse_attention_mixer(q, k, v, gate, iq, ik, iw, q_g, k_g, cos, sin, w_out):
    B, S, _ = q.shape
    q = apply_rope(rms_norm_2(q.reshape(B, S, ATTN_HEADS, HEAD_DIM), q_g), cos, sin)
    k = apply_rope(rms_norm_2(k.reshape(B, S, ATTN_HEADS, HEAD_DIM), k_g), cos, sin)
    v = v.reshape(B, S, ATTN_HEADS, HEAD_DIM)
    iq = apply_rope(iq.reshape(B, S, IDX_HEADS, IDX_DIM), cos, sin)
    ik = apply_rope(ik[:, :, None, :], cos, sin)[:, :, 0, :]
    top_k = min(INDEX_TOPK, S // 4)
    nb = S // Q_BLOCK

    def to_blocks(a):
        return jnp.swapaxes(a.reshape((B, nb, Q_BLOCK) + a.shape[2:]), 0, 1)

    starts = jnp.arange(nb, dtype=jnp.int32) * Q_BLOCK
    key_pos = jnp.arange(S, dtype=jnp.int32)

    def block_fn(args):
        qb, iqb, iwb, t0 = args
        tq = t0 + jnp.arange(Q_BLOCK, dtype=jnp.int32)
        sc = jnp.einsum('bqhd,bsd->bqhs', iqb, ik).astype(jnp.float32) * (IDX_DIM ** -0.5)
        score = jnp.einsum('bqhs,bqh->bqs', jax.nn.relu(sc), iwb.astype(jnp.float32)) * (IDX_HEADS ** -0.5)
        admissible = key_pos[None, :] <= tq[:, None]
        score = jnp.where(admissible[None], score, -jnp.inf)
        _, idx = lax.top_k(score, top_k)
        valid = idx <= tq[None, :, None]
        k_sel = jax.vmap(lambda kb, ib: kb[ib])(k, idx)
        v_sel = jax.vmap(lambda vb, ib: vb[ib])(v, idx)
        s = jnp.einsum('bqhd,bqkhd->bhqk', qb, k_sel).astype(jnp.float32) * (HEAD_DIM ** -0.5)
        s = jnp.where(valid[:, None], s, -jnp.inf)
        p = jax.nn.softmax(s, axis=-1).astype(v.dtype)
        return jnp.einsum('bhqk,bqkhd->bqhd', p, v_sel)

    o = lax.map(block_fn, (to_blocks(q), to_blocks(iq), to_blocks(iw), starts))
    o = jnp.swapaxes(o, 0, 1).reshape(B, S, ATTN_WIDTH)
    return (o * jax.nn.silu(gate)) @ w_out

def pool_mixer(u, gate, pool_w, pool_scale, w_out):
    B, S, _ = u.shape
    ug = u.reshape(B, S, POOL_GROUPS, POOL_GROUP_DIM)
    cs = jnp.cumsum(ug.astype(jnp.float32), axis=1)
    t = jnp.arange(S)
    means = []
    for gi, w in enumerate(POOL_WINDOWS):
        c = cs[:, :, gi]
        lagged = jnp.pad(c, ((0, 0), (w, 0), (0, 0)))[:, :S]
        cnt = jnp.minimum(t + 1, w).astype(jnp.float32)[None, :, None]
        means.append((c - lagged) / cnt)
    pooled = (jnp.stack(means, axis=2) - ug.astype(jnp.float32)).astype(u.dtype)
    mixed = jnp.einsum('bsgc,gcd->bsgd', pooled, pool_w).reshape(B, S, POOL_WIDTH)
    y = mixed * pool_scale * jax.nn.silu(gate)
    return y @ w_out

def second_inputs(seed: int = 0) -> dict:
    key = jax.random.key(seed)
    ks = jax.random.split(key, 13)
    f32 = jnp.float32
    L = DEPTH
    return {
        "x": jax.random.normal(ks[0], (BATCH, SEQ, D_MODEL), f32),
        "norm_g": 1.0 + 0.1 * jax.random.normal(ks[1], (L, D_MODEL), f32),
        "w_in": jax.random.normal(ks[2], (L, D_MODEL, IN_WIDTH_2), f32) * D_MODEL ** -0.5,
        "conv_w": jax.random.normal(ks[3], (L, CONV_KSIZE, CONV_WIDTH), f32) * CONV_KSIZE ** -0.5,
        "w_out_conv": jax.random.normal(ks[4], (L, CONV_WIDTH, D_MODEL), f32) * CONV_WIDTH ** -0.5,
        "q_norm_g": 1.0 + 0.1 * jax.random.normal(ks[5], (L, HEAD_DIM), f32),
        "k_norm_g": 1.0 + 0.1 * jax.random.normal(ks[6], (L, HEAD_DIM), f32),
        "w_out_attn": jax.random.normal(ks[7], (L, ATTN_WIDTH, D_MODEL), f32) * ATTN_WIDTH ** -0.5,
        "pool_w": jax.random.normal(ks[8], (L, POOL_GROUPS, POOL_GROUP_DIM, POOL_GROUP_DIM), f32) * POOL_GROUP_DIM ** -0.5,
        "pool_scale": 1.0 + 0.1 * jax.random.normal(ks[9], (L, POOL_WIDTH), f32),
        "w_out_pool": jax.random.normal(ks[10], (L, POOL_WIDTH, D_MODEL), f32) * POOL_WIDTH ** -0.5,
        "w_o": jax.random.normal(ks[11], (L, D_MODEL, D_MODEL), f32) * D_MODEL ** -0.5,
    }

def second_block(x, norm_g, w_in, conv_w, w_out_conv, q_norm_g, k_norm_g, w_out_attn, pool_w, pool_scale, w_out_pool, w_o):
    B, S, D = x.shape
    cos, sin = rope_tables_2(S, HEAD_DIM)
    for l in range(DEPTH):
        h = rms_norm_2(x, norm_g[l])
        p = h @ w_in[l]
        (cb, cc, cx, cgate, q, k, v, agate, iq, ik, iw, pu, pgate, mgate) = split_columns(p)
        y_a = short_conv_mixer(cb, cc, cx, cgate, conv_w[l], w_out_conv[l])
        y_b = sparse_attention_mixer(q, k, v, agate, iq, ik, iw, q_norm_g[l], k_norm_g[l], cos, sin, w_out_attn[l])
        y_c = pool_mixer(pu, pgate, pool_w[l], pool_scale[l], w_out_pool[l])
        g = jax.nn.sigmoid(mgate.reshape(B, S, N_BRANCHES, D))
        merged = g[:, :, 0] * y_a + g[:, :, 1] * y_b + g[:, :, 2] * y_c
        x = x + merged @ w_o[l]
    return x


def setup_inputs(seed=0):
    out = dict(first_inputs(seed))
    for name, value in second_inputs(seed + 1).items():
        if name != "x":
            out[name + "_2"] = value
    return out


def reference(
    x, mem, positions, ffn1_norm, ffn1_w_in, ffn1_w_out, mix_norm, mix_w_in, mix_w_out,
    fox_f_bias, fox_q_gain, fox_k_gain, moba_q_gain, moba_k_gain, rwkv_mu, rwkv_w0, rwkv_w2,
    rwkv_a0, rwkv_a2, rwkv_g2, rwkv_k_k, rwkv_k_a, rwkv_r_k, rwkv_ln_w, rwkv_ln_b, xattn_norm,
    xattn_mem_norm, xattn_w_q, xattn_w_kv, xattn_q_gain, xattn_k_gain, xattn_w_out, ffn2_norm,
    ffn2_w_in, ffn2_w_out, norm_g_2, w_in_2, conv_w_2, w_out_conv_2, q_norm_g_2, k_norm_g_2,
    w_out_attn_2, pool_w_2, pool_scale_2, w_out_pool_2, w_o_2,
):
    x = first_block(
        x, mem, positions, ffn1_norm, ffn1_w_in, ffn1_w_out, mix_norm, mix_w_in, mix_w_out,
        fox_f_bias, fox_q_gain, fox_k_gain, moba_q_gain, moba_k_gain, rwkv_mu, rwkv_w0, rwkv_w2,
        rwkv_a0, rwkv_a2, rwkv_g2, rwkv_k_k, rwkv_k_a, rwkv_r_k, rwkv_ln_w, rwkv_ln_b,
        xattn_norm, xattn_mem_norm, xattn_w_q, xattn_w_kv, xattn_q_gain, xattn_k_gain,
        xattn_w_out, ffn2_norm, ffn2_w_in, ffn2_w_out,
    )
    return second_block(
        x, norm_g_2, w_in_2, conv_w_2, w_out_conv_2, q_norm_g_2, k_norm_g_2, w_out_attn_2,
        pool_w_2, pool_scale_2, w_out_pool_2, w_o_2,
    )


_drawn_inputs = setup_inputs


def setup_inputs(seed=0):
    import zlib

    import numpy as np

    out = dict(_drawn_inputs(seed))
    spreads = {}
    factors = {'ffn1_norm': 2.978,
     'fox_q_gain': 8.0,
     'fox_k_gain': 8.0,
     'moba_q_gain': 8.0,
     'moba_k_gain': 8.0,
     'rwkv_k_k': 4.614,
     'rwkv_ln_w': 4.202,
     'rwkv_ln_b': 3.519,
     'xattn_norm': 8.0,
     'xattn_mem_norm': 8.0,
     'xattn_q_gain': 8.0,
     'xattn_k_gain': 8.0,
     'ffn2_norm': 3.615,
     'q_norm_g_2': 29.268,
     'k_norm_g_2': 32.713,
     'norm_g_2': 2.811,
     'pool_scale_2': 8.0}
    for name, (base, spread) in spreads.items():
        noise = np.random.default_rng([zlib.crc32(name.encode()), seed]).standard_normal(out[name].shape)
        drawn = base * np.exp(spread * noise) if base else spread * noise
        out[name] = __import__('jax').numpy.asarray(drawn.astype(out[name].dtype))
    for name, factor in factors.items():
        out[name] = (out[name] * factor).astype(out[name].dtype)
    return out
```

```python
import numpy as np

import concourse.bass as bass
from concourse import mybir

F32 = mybir.dt.float32
F32R = mybir.dt.float32r
BF16 = mybir.dt.bfloat16
I32 = mybir.dt.int32
ACT = mybir.ActivationFunctionType
ALU = mybir.AluOpType
AX = mybir.AxisListType.X

P = 128
S = 256
NT = S // P
D = 1024
DEPTH = 2
FFN = 2816
NJ = FFN // 256
RW = 512
ZR = 1824
HD = 64
RING = 4
AHEAD = 3
UNITS_FFN = 6 * NJ
ZG = 7
UNITS1 = 2 * UNITS_FFN + 4 * ZG + 8 + 8 + 4 + 4
PG = 18
UNITS2 = 4 * PG + 3 * 4 + 8
UNITS = DEPTH * (UNITS1 + UNITS2)
STREAM = UNITS + RING
assert UNITS1 % RING == 0 and UNITS2 % RING == 0
EPS = 1e-6
GN_EPS = 64e-5
NEG = -1e30
TAKEN = -3e38

ZQ, ZK, ZV, ZF, ZN = ZR, ZR + 512, ZR + 1024, ZR + 1536, ZR + 1540
PC = {n: 512 * i for i, n in enumerate(["cb", "cc", "cx", "cg", "q", "k", "v", "ag", "iq", "pu", "pg", "mg"])}
PC["ik"] = 512 * 17
PC["iw"] = PC["ik"] + 64
PN = PC["iw"] + 8

PV_FFN1, PV_MIX, PV_X, PV_MEM, PV_FFN2, PV_XQ, PV_XK, PV_N = 0, 8, 16, 24, 32, 40, 41, 42
R_MU = 0
R_W0, R_A0, R_KK, R_KA, R_RK, R_LW, R_LB, R_GQ, R_GK = (ZR + 512 * i for i in range(9))
R_FB = ZR + 512 * 9
R_N = R_FB + 4
PW_NORM, PW_CONV, PW_N = 0, 8, 20
Q_GQ, Q_GK, Q_PS, Q_N = 0, 512, 1024, 1536


def constants():
    s = np.arange(P)[:, None]
    t = np.arange(P)[None, :]
    same = (s // 64) == (t // 64)
    c = {}
    c["ident"] = (s == t)
    c["cum64"] = (s <= t) & same
    c["ones64"] = np.concatenate([(s // 64 == 0), (s // 64 == 1)], 1)
    c["cum"] = np.concatenate([(s + P * k) <= np.arange(S)[None, :] for k in range(NT)], 1)
    up_strict, up_incl = (s < t) & same, (s <= t) & same
    c["mask4"] = np.concatenate([up_strict, up_incl, up_strict, up_incl], 1)
    for lv in range(6):
        b = 1 << lv
        low = ((s // (2 * b)) == (t // (2 * b))) & ((s // b) % 2 == 1) & ((t // b) % 2 == 0)
        c[f"low{lv}"] = low
    c["lowT0"] = c["low0"].T
    c["bd"] = (s // 64 == t // 64)
    c["causal"] = np.where(t <= s, 0.0, NEG)
    c["zeropad"] = np.zeros((P, 128))
    band = np.zeros((4, S, S))
    for g, w in enumerate((2, 4, 8, 16)):
        for q in range(S):
            lo = max(0, q - w + 1)
            band[g, lo:q + 1, q] = 1.0 / min(q + 1, w)
        band[g] -= np.eye(S)
    c["band"] = band.reshape(4, NT, P, S).transpose(2, 0, 1, 3).reshape(P, -1)
    inv = (500000.0 ** (-np.arange(0, 16, 2) / 16.0)).astype(np.float32)
    c["inv"] = np.repeat(inv[None, :], P, 0)
    inv2 = np.float32(1.0) / (10000.0 ** (np.arange(0, 64, 2) / 64.0)).astype(np.float32)
    ang = (np.arange(S, dtype=np.float32)[:, None] * inv2[None, :]).astype(np.float32).astype(np.float64)
    for n, f in (("cos2", np.cos), ("sin2", np.sin)):
        c[n] = f(ang).reshape(NT, P, 32).transpose(1, 0, 2).reshape(P, -1)
    return {k: np.ascontiguousarray(v, dtype=np.float32) for k, v in c.items()}


CONST = constants()
BAND_N = 4 * NT * S
COFF, _o = {}, 0
for _k, _v in CONST.items():
    if _k != "band":
        COFF[_k] = (_o, _v.shape[1])
        _o += _v.shape[1]
CN = _o


class Token:

    def __init__(self, sem, val):
        self.sem, self.val = sem, val


class Engine:

    def __init__(self, nc, eng, name):
        self.e, self.sem, self.n, self.seen = eng, nc.alloc_semaphore(f"done_{name}"), 0, {}
        self.name = name

    def wait(self, *toks):
        for t in toks:
            if t is None:
                continue
            if isinstance(t, (list, tuple)):
                self.wait(*t)
            elif not isinstance(t.val, int):
                self.e.wait_ge(t.sem, t.val)
            elif self.seen.get(id(t.sem), 0) < t.val:
                self.seen[id(t.sem)] = t.val
                self.e.wait_ge(t.sem, t.val)

    def done(self, ins):
        self.n += 1
        ins.then_inc(self.sem, 1)
        return Token(self.sem, self.n)


class Program:
    def __init__(self, nc, a):
        self.nc, self.a = nc, a
        self.pe, self.act = Engine(nc, nc.tensor, "pe"), Engine(nc, nc.scalar, "act")
        self.dve, self.pool = Engine(nc, nc.vector, "dve"), Engine(nc, nc.gpsimd, "pool")
        self.engines = [self.pe, self.act, self.dve, self.pool]
        self.compute = tuple(e.e.engine for e in self.engines)
        self.last_v = None
        self.ev = {n: nc.alloc_semaphore(n) for n in
                   ("silu", "h_ready", "h_turned", "ht_hi", "ht_lo", "z_act", "z_dve")}
        self.dma = {n: nc.alloc_semaphore(n) for n in ("d_par", "d_rows", "d_lora", "d_mem", "d_shift1",
                                                       "d_shift1_row", "d_shift0")}
        self.dma_base = {n: 0 for n in self.dma}
        sb = nc.alloc_sbuf_tensor
        self.raw = [sb(f"raw{i}", [P, 2, 512], F32) for i in range(RING)]
        self.whi = [sb(f"whi{i}", [P, 2, 512], F32R) for i in range(RING)]
        self.wlo = [sb(f"wlo{i}", [P, 2, 512], F32R) for i in range(RING)]
        self.s_load = [nc.alloc_semaphore(f"loaded{i}") for i in range(RING)]
        self.s_hi, self.s_lo, self.s_mm = (nc.alloc_semaphore(n) for n in ("split_hi", "split_lo", "unit_used"))
        self.X = sb("x_res", [P, NT, D], F32)
        self.AHI, self.ALO = sb("a_hi", [P, 8, S], F32R), sb("a_lo", [P, 8, S], F32R)
        self.HHI, self.HLO = sb("h_hi", [P, 2, S], F32R), sb("h_lo", [P, 2, S], F32R)
        self.zero = sb("zero", [P, 512], BF16)
        self.minus_half = sb("minus_half", [P, 8], F32)
        self.C = sb("const_tables", [P, CN], F32)
        self.SM = sb("small", [P, 512], F32)
        self.arena_n = (212863 - 48 * 1024 - 8192 - 16384 - 4096 - 1024 - CN * 4 - 2048 - 1024) // 4 // 8 * 8
        self.arena = sb("arena", [P, self.arena_n], F32)
        self.top = 0
        self.PS = nc.alloc_psum_tensor("ps", [P, 8 * 512], F32)
        self.s_start = nc.alloc_semaphore("loaded_start")
        self.s_set = nc.alloc_semaphore("constants_set")
        self.s_out = nc.alloc_semaphore("stored")
        self.unit = 0
        self.scope = 0

    def V(self, method, *args, after=(), **kw):
        self.dve.wait(self.last_v, *after)
        self.last_v = self.dve.done(method(*args, **kw))
        return self.last_v

    def A(self, out, in_, func, after=(), **kw):
        self.act.wait(*after)
        return self.act.done(self.act.e.activation(out, in_, func, **kw))

    def bank(self, b, n=512, nb=1):
        return self.PS[:, b * 512:b * 512 + (n if nb == 1 else nb * 512)]

    def mem(self, *shape):
        n = int(np.prod(shape))
        v = self.arena[:, self.top:self.top + n]
        self.top += n
        assert self.top <= self.arena_n, (self.top, self.arena_n)
        if len(shape) == 1:
            return v
        names = "abcd"[:len(shape)]
        return v.rearrange(f"p ({' '.join(names)}) -> p {' '.join(names)}", **dict(zip(names, shape)))

    def c(self, name):
        o, n = COFF[name]
        return self.C[:, o:o + n]

    def event(self, name, val):
        return Token(self.ev[name], val)

    def split_next(self):
        m = self.unit + AHEAD
        i = m % RING
        n = self.scope + m
        use = self.scope_use + m // RING
        self.act.e.wait_ge(self.s_load[i], use * 16 + 16)
        self.act.e.wait_ge(self.s_mm, n + 1)
        self.act.e.activation(self.whi[i][:, :, :], self.raw[i][:, :, :], ACT.Copy).then_inc(self.s_hi, 1)
        self.dve.e.wait_ge(self.s_hi, n + 1)
        self.dve.e.tensor_tensor(self.wlo[i][:, :, :], self.raw[i][:, :, :], self.whi[i][:, :, :].bitcast(F32),
                                 ALU.subtract).then_inc(self.s_lo, 1)

    def products(self, jobs, ahi, alo, after=()):
        self.split_next()
        i = self.unit % RING
        n = self.scope + self.unit
        self.pe.wait(*after)
        self.pe.e.wait_ge(self.s_lo, n + (RING + 1))
        hi, lo = self.whi[i], self.wlo[i]
        for out, kk, kt, t, start in jobs:
            w = out.shape[1]
            a_h, a_l = ahi[:, kt, t * P:(t + 1) * P], alo[:, kt, t * P:(t + 1) * P]
            mm = self.pe.e.matmul
            mm(out, a_h, hi[:, kk, 0:w], start=start, stop=False, skip_group_check=True)
            mm(out, a_h, lo[:, kk, 0:w], start=False, stop=False, skip_group_check=True)
            last = mm(out, a_l, hi[:, kk, 0:w], start=False, stop=True, skip_group_check=True)
        last.then_inc(self.s_mm, 1)
        self.unit += 1
        return Token(self.s_mm, n + (RING + 1))

    def gemm(self, banks, nk, kt0=0, width=512, toks=None, after=()):
        for u in range(nk // 2):
            need = [toks[kt0 + 2 * u + 1]] if toks else []
            jobs = [(self.bank(banks[t], width), kk, kt0 + 2 * u + kk, t, u == 0 and kk == 0)
                    for kk in range(2) for t in range(NT)]
            tok = self.products(jobs, self.AHI, self.ALO, after=[*need, *(after if u == 0 else ())])
        return tok

    def rstd(self, out, ss, n, eps, tok):
        self.dve.wait(tok)
        t = self.dve.done(self.dve.e.tensor_scalar(out, ss, 1.0 / n, eps, ALU.mult, ALU.add))
        return self.power(out, t)

    def power(self, x, tok):
        self.pool.wait(tok)
        half = self.minus_half[:, 0:x.shape[1]]
        return self.pool.done(self.pool.e.tensor_tensor(x, x, half, ALU.pow))

    def turn(self, cols, banks, gain=None, kt0=0, ready=None, src_free=None):
        toks, left = [None] * kt0, {}
        for k, src in enumerate(cols):
            b = banks[k % len(banks)]
            self.pe.wait(ready[k] if isinstance(ready, list) else ready, left.get(b))
            for t in range(NT):
                ins = self.pe.e.transpose(self.bank(b)[:, t * P:(t + 1) * P], src[t], self.c("ident"))
            tp = self.pe.done(ins)
            self.act.wait(tp)
            ps = self.bank(b, S)
            scale = gain[:, k:k + 1] if gain is not None else 1.0
            th = self.act.done(self.act.e.activation(self.AHI[:, kt0 + k, :], ps, ACT.Copy, scale=scale))
            self.dve.wait(th)
            if gain is None:
                ins = self.dve.e.tensor_tensor(self.ALO[:, kt0 + k, :], ps, self.AHI[:, kt0 + k, :].bitcast(F32),
                                               ALU.subtract)
            else:
                ins = self.dve.e.scalar_tensor_tensor(self.ALO[:, kt0 + k, :], ps, scale,
                                                      self.AHI[:, kt0 + k, :].bitcast(F32), ALU.mult, ALU.subtract)
            left[b] = self.dve.done(ins)
            toks.append(left[b])
        return toks

    def norm_turn(self, src, gain, banks, ready):
        ss, rs = self.SM[:, 0:NT], self.SM[:, 2:2 + NT]
        tr = []
        for t in range(NT):
            self.act.wait(ready)
            ta = self.act.done(self.act.e.activation(self.XN[:, t, :], src[:, t, :], ACT.Square,
                                                     accum_out=ss[:, t:t + 1]))
            tr.append(self.rstd(rs[:, t:t + 1], ss[:, t:t + 1], D, EPS, ta))
        for t in range(NT):
            self.dve.wait(tr[t])
            tx = self.dve.done(self.dve.e.tensor_scalar(self.XN[:, t, :], src[:, t, :], rs[:, t:t + 1], None,
                                                        ALU.mult))
        return self.turn([[self.XN[:, t, k * P:(k + 1) * P] for t in range(NT)] for k in range(8)], banks, gain,
                         ready=tx)

    def add_to_x(self, banks, scale, tok):
        self.dve.wait(tok)
        for t in range(NT):
            for h in range(2):
                ins = self.dve.e.scalar_tensor_tensor(self.X[:, t, h * 512:(h + 1) * 512], self.bank(banks[t][h]),
                                                      scale, self.X[:, t, h * 512:(h + 1) * 512], ALU.mult, ALU.add)
        return self.dve.done(ins)

    def ffn_in(self, j, toks=None, first=False):
        after = [] if first else [self.event("h_ready", 2 * j)]
        for u in range(4):
            need = [toks[2 * u + 1]] if toks else []
            jobs = [(self.bank(4 + t), kk, 2 * u + kk, t, u == 0 and kk == 0) for kk in range(2) for t in range(NT)]
            tok = self.products(jobs, self.AHI, self.ALO, after=[*need, *(after if u == 0 else ())])
        for t in range(NT):
            self.act.wait(tok)
            self.act.e.activation(self.SG[:, t, :], self.bank(4 + t, 256), ACT.Silu).then_inc(self.ev["silu"], 1)
            self.dve.wait(self.event("silu", 2 * j + (t + 1)))
            self.dve.e.tensor_tensor(self.H[:, t, :], self.SG[:, t, :], self.bank(4 + t)[:, 256:512],
                                     ALU.mult).then_inc(self.ev["h_ready"], 1)

    def ffn_turn(self, j, first=False):
        self.pe.wait(self.event("h_ready", 2 * j + 2))
        if not first:
            self.pe.wait(self.event("ht_lo", 2 * j))
        for kk in range(2):
            for t in range(NT):
                ins = self.pe.e.transpose(self.bank(6 + kk)[:, t * P:(t + 1) * P],
                                          self.H[:, t, kk * P:(kk + 1) * P], self.c("ident"))
            ins.then_inc(self.ev["h_turned"], 1)
        for kk in range(2):
            self.act.wait(self.event("h_turned", 2 * j + (kk + 1)))
            self.act.e.activation(self.HHI[:, kk, :], self.bank(6 + kk, S), ACT.Copy).then_inc(self.ev["ht_hi"], 1)
            self.dve.wait(self.event("ht_hi", 2 * j + (kk + 1)))
            self.dve.e.tensor_tensor(self.HLO[:, kk, :], self.bank(6 + kk, S), self.HHI[:, kk, :].bitcast(F32),
                                     ALU.subtract).then_inc(self.ev["ht_lo"], 1)

    def ffn_out(self, j):
        for h in range(2):
            jobs = [(self.bank(2 * t + h), kk, kk, t, False) for kk in range(2) for t in range(NT)]
            tok = self.products(jobs, self.HHI, self.HLO,
                                after=[self.event("ht_lo", 2 * j + 2)] if h == 0 else ())
        return tok

    def loop(self, count, per, body):
        for e in self.engines:
            e.seen = {}
        outer, outer_use, n0, counts = self.scope, self.scope_use, self.unit, [e.n for e in self.engines]
        assert per % RING == 0
        with self.nc.Fori(0, count, engines=self.compute) as i:
            self.scope, self.scope_use = outer + i * per, outer_use + i * (per // RING)
            body(i)
            assert self.unit == n0 + per and counts == [e.n for e in self.engines]
        self.scope, self.scope_use, self.unit = outer, outer_use, n0 + count * per
        for e in self.engines:
            e.seen = {}

    def ffn(self, gain, jb, ready):
        toks = self.norm_turn(self.X, gain, [6, 7, 0, 1, 2, 3], ready)
        self.ffn_in(jb, toks, first=jb == 0)
        self.pe.wait(toks)
        for b in range(4):
            self.pe.e.matmul(self.bank(b), self.zero[:, 0:P], self.zero[:, :], start=True, stop=False,
                             skip_group_check=True)
        self.ffn_turn(jb, first=jb == 0)

        def body(i):
            for u in range(2):
                j = i * 2 + (jb + 1 + u)
                self.ffn_in(j)
                self.ffn_out(j - 1)
                self.ffn_turn(j)

        self.loop((NJ - 1) // 2, 12, body)
        tok = self.ffn_out(jb + NJ - 1)
        return self.add_to_x([[0, 1], [2, 3]], 0.5, tok)

    def column_groups(self, dst, loops, widths, toks):
        nc = self.nc
        for e, n in ((self.act, "z_act"), (self.dve, "z_dve")):
            e.e.sem_inc(self.ev[n], 2)

        def group(g, pair, width, toks=None):
            tok = self.gemm([2 * pair, 2 * pair + 1], 8, width=width, toks=toks,
                            after=[self.event("z_act", g + 1), self.event("z_dve", g + 1)])
            self.act.wait(tok)
            cols = slice(g * 512, g * 512 + width) if isinstance(g, int) else bass.ds(g * 512, width)
            self.act.e.activation(dst[:, 0, cols], self.bank(2 * pair, width), ACT.Copy).then_inc(self.ev["z_act"], 1)
            self.dve.wait(tok)
            self.dve.e.tensor_copy(dst[:, 1, cols], self.bank(2 * pair + 1, width)).then_inc(self.ev["z_dve"], 1)

        for e in self.engines:
            e.seen = {}
        self.pe.wait(toks)

        def body(i):
            for u in range(2):
                group(i * 2 + u, u, 512)

        self.loop(loops, 8, body)
        for n, w in enumerate(widths):
            group(2 * loops + n, n % 2, w)
        g = 2 * loops + len(widths)
        return [self.event("z_act", g + 2), self.event("z_dve", g + 2)]

    def head_norm(self, x, nh, hd, tmp, sm, ready, gain=None, pool=False):
        e = self.dve
        e.wait(ready)
        x3 = x.rearrange("p (h d) -> p h d", h=nh)
        t = e.done(e.e.tensor_tensor(tmp, x, x, ALU.mult))
        e.wait(t)
        t = e.done(e.e.tensor_reduce(sm, tmp.rearrange("p (h d) -> p h d", h=nh), AX, ALU.add))
        t = self.rstd(sm, sm, hd, EPS, t)
        e.wait(t)
        t = e.done(e.e.tensor_tensor(x3, x3, sm.unsqueeze(2).to_broadcast([P, nh, hd]), ALU.mult))
        if gain is not None:
            e.wait(t)
            t = e.done(e.e.tensor_tensor(x, x, gain, ALU.mult))
        return t

    def rope(self, x, nh, half, cos, sin, tmp, ready):
        e = self.dve
        e.wait(ready)
        x1, x2 = x[:, :, 0:half], x[:, :, half:2 * half]
        cb, sb = (a.unsqueeze(1).to_broadcast([P, nh, half]) for a in (cos, sin))
        v = tmp[:, 0:3 * nh * half].rearrange("p (a h d) -> p a h d", a=3, h=nh)
        e.e.tensor_tensor(v[:, 0], x2, sb, ALU.mult)
        e.e.tensor_tensor(v[:, 1], x1, sb, ALU.mult)
        e.e.tensor_tensor(v[:, 2], x2, cb, ALU.mult)
        t = e.done(e.e.tensor_tensor(x1, x1, cb, ALU.mult))
        e.wait(t)
        e.e.tensor_tensor(x1, x1, v[:, 0], ALU.subtract)
        return e.done(e.e.tensor_tensor(x2, v[:, 2], v[:, 1], ALU.add))

    def turn_plain(self, dst, src, n, b, ready, gain=None, free=None, on=None):
        self.pe.wait(ready, free)
        for k in range(n):
            ins = self.pe.e.transpose(self.bank(b)[:, k * P:(k + 1) * P], src[:, k * P:(k + 1) * P], self.c("ident"))
        tp = self.pe.done(ins)
        e = on or self.act
        e.wait(tp)
        v = self.bank(b, n * P).rearrange("p (k c) -> p k c", k=n)
        if e is self.act:
            return e.done(e.e.activation(dst, v, ACT.Copy, scale=gain if gain is not None else 1.0))
        if gain is not None:
            return e.done(e.e.tensor_scalar(dst, v, gain, None, ALU.mult))
        return e.done(e.e.tensor_copy(dst, v))

    def softmax_pv(self, qt, nh, hd, SB, nk, v_of, out, PT, tok, free, banks_t, bank_o):
        dve, act, pe = self.dve, self.act, self.pe
        mx, sm = self.SM[:, 32:32 + nh], self.SM[:, 48:48 + nh]
        dve.wait(tok)
        t = dve.done(dve.e.tensor_reduce(mx, SB, AX, ALU.max))
        dve.wait(t)
        t = dve.done(dve.e.tensor_scalar(mx, mx, -1.0, None, ALU.mult))
        act.wait(t)
        te = []
        for h in range(nh):
            te.append(act.done(act.e.activation(SB[:, h, :], SB[:, h, :], ACT.Exp, bias=mx[:, h:h + 1],
                                                accum_out=sm[:, h:h + 1])))
        dve.wait(te[-1])
        tr = dve.done(dve.e.reciprocal(sm, sm))
        nkt = nk // P
        per = 4
        todo = [(h, k) for h in range(nh) for k in range(nkt)]
        left, ready = {}, {}
        for g in range(0, len(todo), per):
            b = banks_t[(g // per) % len(banks_t)]
            part = todo[g:g + per]
            pe.wait(te[part[-1][0]], left.get(b), free)
            for n, (h, k) in enumerate(part):
                ins = pe.e.transpose(self.bank(b)[:, n * P:(n + 1) * P], SB[:, h, k * P:(k + 1) * P], self.c("ident"))
            tp = pe.done(ins)
            e = dve if (g // per) % 2 else act
            e.wait(tp)
            dst = PT[:, g * P:(g + len(part)) * P]
            if e is act:
                left[b] = act.done(act.e.activation(dst, self.bank(b, len(part) * P), ACT.Copy))
            else:
                left[b] = dve.done(dve.e.tensor_copy(dst, self.bank(b, len(part) * P)))
            for h, k in part:
                ready[h, k] = left[b]
        for h in range(nh):
            for k in range(nkt):
                pe.wait(ready[h, k])
                n = todo.index((h, k))
                ins = pe.e.matmul(self.bank(bank_o)[:, h * hd:(h + 1) * hd], PT[:, n * P:(n + 1) * P], v_of(h, k),
                                  start=(k == 0), stop=(k == nkt - 1), skip_group_check=True)
        tp = pe.done(ins)
        dve.wait(tp, tr)
        o3 = self.bank(bank_o, nh * hd).rearrange("p (h d) -> p h d", h=nh)
        return dve.done(dve.e.tensor_tensor(out.rearrange("p (h d) -> p h d", h=nh), o3,
                                            sm.unsqueeze(2).to_broadcast([P, nh, hd]), ALU.mult)), tp



    def load(self, name, dst, src):
        assert name not in self.loaded
        self.loaded[name] = True
        self.nc.scalar.dma_start(dst, src).then_inc(self.dma[name], 16)
        return Token(self.dma[name], self.layer_no * 16 + (self.dma_base[name] + 16))

    def attention(self, par, rows):
        Z, mark = self.Z, self.top
        dve, act, pe = self.dve, self.act, self.pe
        v = self.dve.e
        QT, KT, SB, PT = self.mem(4, S), self.mem(4, S), self.mem(8, S), self.mem(16 * P)
        tmp, LF = self.mem(512), self.mem(NT, 4)
        CS = self.mem(NT, 2, 8)
        sm = self.SM[:, 16:24]
        aux = self.mem(80)
        f = aux[:, 0:8].rearrange("p (t h) -> p t h", t=NT)
        ab = aux[:, 8:16].rearrange("p (t h) -> p t h", t=NT)
        fb = rows[:, R_FB:R_FB + 4].unsqueeze(1).to_broadcast([P, NT, 4])
        self.V(v.tensor_tensor, f, Z[:, :, ZF:ZF + 4], fb, ALU.add, after=[self.z_ready, par])
        t = self.V(v.scalar_tensor_tensor, ab, f, -1.0, f, ALU.mult, ALU.max)
        t = self.A(ab, ab, ACT.Exp, after=[t], scale=-1.0)
        t = self.A(ab, ab, ACT.Ln, after=[t], bias=1.0)
        self.V(v.scalar_tensor_tensor, LF, f, 0.0, ab, ALU.min, ALU.subtract, after=[t])
        self.V(v.tensor_scalar, LF, LF, float(HD) ** 0.5, None, ALU.mult)
        LN = self.mem(NT, 4)
        t_lf = self.V(v.tensor_scalar, LN, LF, -1.0, None, ALU.mult)
        pos = self.mem(NT)
        self.V(v.tensor_copy, pos, self.POS)
        ang, n = aux[:, 16:48].rearrange("p (t a d) -> p t a d", t=NT, a=2), aux[:, 48:80].rearrange(
            "p (t a d) -> p t a d", t=NT, a=2)
        for t_ in range(NT):
            for a in range(2):
                self.V(v.tensor_scalar, ang[:, t_, a, :], self.c("inv"), pos[:, t_:t_ + 1], None, ALU.mult)
        big = float(1.5 * 2 ** 23)
        for a, quarter in ((0, 0.25), (1, 0.0)):
            self.V(v.tensor_scalar, n[:, :, a, :], ang[:, :, a, :], float(1 / (2 * np.pi)), quarter, ALU.mult, ALU.add)
        self.V(v.tensor_scalar, n, n, big, None, ALU.add)
        self.V(v.tensor_scalar, n, n, big, None, ALU.subtract)
        for part in TWO_PI:
            self.V(v.scalar_tensor_tensor, ang, n, -part, ang, ALU.mult, ALU.add)
        self.V(v.tensor_scalar, ang[:, :, 0, :], ang[:, :, 0, :], float(np.pi / 2), None, ALU.add)
        t = self.V(v.tensor_scalar, ang, ang, PI_IN, -PI_IN, ALU.min, ALU.max)
        t_cs = self.A(CS, ang, ACT.Sin, after=[t])
        tq = []
        for t_ in range(NT):
            for src, gain, dst in ((ZQ, R_GQ, QT), (ZK, R_GK, KT)):
                x = Z[:, t_, src:src + 512]
                t = self.head_norm(x, 8, HD, tmp, sm, [self.z_ready, self.last_v], rows[:, gain:gain + 512])
                t = self.rope(x[:, 256:512].rearrange("p (h d) -> p h d", h=4), 4, 8, CS[:, t_, 0, :], CS[:, t_, 1, :],
                              tmp, [t, t_cs])
                self.last_v = t
                b = 4 + len(tq)
                tq.append(self.turn_plain(dst[:, :, t_ * P:(t_ + 1) * P], x, 4, b, t))
        free = None
        scale = float(HD) ** -0.5
        for qt in range(NT):
            nk = P * (qt + 1)
            qs = slice(qt * P, (qt + 1) * P)
            banks = {}
            pe.wait(tq, t_lf, free)
            for h in range(8):
                b, slot = 4 + 2 * (h // 4) + h % 2, (h // 2) % 2
                hp, po = h // 2, HD * (h % 2)
                out = self.bank(b)[:, slot * S:slot * S + nk]
                fox = h < 4
                ins = pe.e.matmul(out, QT[po:po + HD, hp, qs], KT[po:po + HD, hp, 0:nk], start=True, stop=not fox,
                                  skip_group_check=True)
                if fox:
                    for st in range(qt + 1):
                        cum = self.c("cum")[:, st * S:(st + 1) * S]
                        pe.e.matmul(out, cum[:, qs], LF[:, st, h:h + 1].to_broadcast([P, nk]), start=False,
                                    stop=False, skip_group_check=True)
                        ins = pe.e.matmul(out, LN[:, st, h:h + 1].to_broadcast([P, P]), cum[:, 0:nk], start=False,
                                          stop=st == qt, skip_group_check=True)
            tp = pe.done(ins)
            for b in range(4):
                ps = self.bank(4 + b).rearrange("p (s k) -> p s k", s=2)
                h0 = 4 * (b // 2) + b % 2
                dst = SB[:, h0:h0 + 3:2, :]
                mask = self.c("causal").unsqueeze(1).to_broadcast([P, 2, P])
                dve.wait(tp, free)
                dve.e.scalar_tensor_tensor(dst[:, :, nk - P:nk], ps[:, :, nk - P:nk], scale, mask, ALU.mult, ALU.add)
                if qt:
                    dve.e.tensor_scalar(dst[:, :, 0:P], ps[:, :, 0:P], scale, None, ALU.mult)
            self.last_v = t_s = self.mark_dve()
            t_o, free = self.softmax_pv(qt, 8, HD, SB[:, :, 0:nk], nk,
                                        lambda h, k: Z[:, k, ZV + h * HD:ZV + (h + 1) * HD],
                                        Z[:, qt, ZQ:ZQ + 512], PT, t_s, free, [0, 1, 2], 3)
            self.last_v = t_o
        self.top = mark
        return t_o

    def rwkv(self, par, rows, lora, start):
        Z, mark = self.Z, self.top
        dve, act, pe, pool = self.dve, self.act, self.pe, self.pool
        v = self.dve.e
        ZS = self.mem(ZR)
        T1, T2, T3 = (ZS[:, i * 512:(i + 1) * 512] for i in range(3))
        T4, T5, T6, T7, T8 = (self.mem(512) for _ in range(5))
        TA = self.mem(4, 4, P)
        MK = self.mem(8, 4, P)
        RHS, ST = self.mem(512), self.mem(4, P)
        mk0 = MK.rearrange("p a b c -> p (a b c)")
        L, LT = mk0[:, 0:288], mk0[:, 512:512 + 384].rearrange("p (k c) -> p k c", k=3)
        ZS2 = self.XN.rearrange("p a b -> p (a b)")[:, 0:ZR]
        xn = self.XN.rearrange("p a b -> p (a b)")
        TI, TIT = (xn[:, i * 1024:(i + 1) * 1024].rearrange("p (h c) -> p h c", h=8) for i in range(2))
        hh = [self.H.rearrange("p a b -> p (a b)"), self.SG.rearrange("p a b -> p (a b)")]
        XG = [x.rearrange("p (h c) -> p h c", h=4) for x in hh]
        U, WCM = rows[:, 0:512], rows[:, 512:1536].rearrange("p (c h d) -> p c h d", c=2, h=4)
        sm = self.SM[:, 0:8]
        sm2, sm3, WC, MU = self.SM[:, 8:16], self.SM[:, 16:24], self.SM[:, 24:32], self.SM[:, 64:72]
        act.wait(start, self.z_ready)
        shifted = [self.load("d_shift1", ZS2[1:P, :], Z[0:P - 1, 1, 0:ZR]),
                   self.load("d_shift1_row", ZS2[0:1, :], Z[P - 1:P, 0, 0:ZR])]
        dve.wait(start)
        t = self.V(v.memset, ZS[0:1, :], 0.0)
        act.wait(t)
        shifted.append(self.load("d_shift0", ZS[1:P, :], Z[0:P - 1, 0, 0:ZR]))
        mu = rows[:, R_MU:R_MU + ZR]
        for t_, z in ((1, ZS2), (0, ZS)):
            zt = Z[:, t_, 0:ZR]
            self.V(v.tensor_tensor, z, z, zt, ALU.subtract, after=[*shifted, par])
            self.V(v.tensor_tensor, z, z, mu, ALU.mult)
            self.V(v.tensor_tensor, zt, zt, z, ALU.add)
        self.V(v.memset, ST, 0.0)
        decay = -float(np.exp(-0.5))
        h3 = lambda x: x.rearrange("p (h d) -> p h d", h=8)
        bc = lambda s: s.unsqueeze(2).to_broadcast([P, 8, HD])
        for t_ in range(NT):
            r, k, val = (Z[:, t_, i * 512:(i + 1) * 512] for i in range(3))
            zl = Z[:, t_, 3 * 512:ZR]
            t0 = self.last_v
            self.A(L[:, 0:64], zl[:, 0:64], ACT.Tanh, after=[t0])
            self.A(L[:, 64:128], zl[:, 64:128], ACT.Copy)
            ta = self.A(L[:, 128:288], zl[:, 128:288], ACT.Sigmoid)
            pe.wait(ta, t0)
            for i, w in enumerate((128, 128, 32)):
                ins = pe.e.transpose(self.bank(0)[0:w, i * P:(i + 1) * P], L[:, i * P:i * P + w], self.c("ident"))
            tp = pe.done(ins)
            self.A(LT[:, 0:2, :], self.bank(0, 256).rearrange("p (k c) -> p k c", k=2), ACT.Copy, after=[tp])
            ta = self.A(LT[0:32, 2, :], self.bank(0)[0:32, 256:384], ACT.Copy)
            pe.wait(ta, lora)
            W = self.LORA
            pe.e.matmul(self.bank(1), LT[0:64, 0, :], W[0:64, 0, :], start=True, stop=True)
            pe.e.matmul(self.bank(2), LT[64:128, 0, :], W[64:128, 0, :], start=True, stop=True)
            pe.e.matmul(self.bank(3), LT[:, 1, :], W[:, 1, :], start=True, stop=False)
            tp = pe.done(pe.e.matmul(self.bank(3), LT[0:32, 2, :], W[0:32, 2, :], start=False, stop=True))
            self.V(v.tensor_tensor, T1, self.bank(1), rows[:, R_W0:R_W0 + 512], ALU.add, after=[tp])
            t = self.V(v.tensor_tensor, T5, self.bank(2), rows[:, R_A0:R_A0 + 512], ALU.add)
            self.A(T1, T1, ACT.Sigmoid, after=[t])
            t_a = self.A(T5, T5, ACT.Sigmoid)
            t_g = self.A(T6, self.bank(3), ACT.Copy)
            t_ld = self.V(v.tensor_scalar, T1, T1, decay, None, ALU.mult, after=[t_a])
            pe.wait(t_ld)
            tp = pe.done(pe.e.matmul(self.bank(1), self.c("cum64"), T1, start=True, stop=True))
            for hp in range(4):
                ins = pe.e.matmul(self.bank(2)[:, 2 * hp:2 * hp + 2], T1[:, hp * P:(hp + 1) * P], self.c("ones64"),
                                  start=True, stop=True, skip_group_check=True)
            tw = pe.done(ins)
            t_cx = self.V(v.tensor_tensor, T4, self.bank(1), T1, ALU.subtract, after=[tp])
            self.A(T2, self.bank(1), ACT.Exp, after=[tp, t_cx])
            self.A(T3, self.bank(1), ACT.Exp, scale=-1.0)
            self.A(T4, T4, ACT.Exp)
            t_e = self.A(WC, self.bank(2, 8), ACT.Exp, after=[tw])
            self.V(v.tensor_tensor, T7, k, rows[:, R_KK:R_KK + 512], ALU.mult)
            self.V(v.tensor_tensor, T8, T7, T7, ALU.mult)
            self.V(v.tensor_reduce, sm, h3(T8), AX, ALU.add)
            t = self.V(v.tensor_scalar, sm, sm, 1e-24, None, ALU.max)
            t = self.power(sm, t)
            self.V(v.tensor_tensor, h3(T7), h3(T7), bc(sm), ALU.mult, after=[t])
            self.V(v.scalar_tensor_tensor, T8, T5, -1.0, rows[:, R_KA:R_KA + 512], ALU.add, ALU.mult)
            self.V(v.scalar_tensor_tensor, k, T8, 1.0, k, ALU.add, ALU.mult)
            self.V(v.tensor_tensor, T8, r, k, ALU.mult)
            self.V(v.tensor_tensor, T8, T8, rows[:, R_RK:R_RK + 512], ALU.mult)
            self.V(v.tensor_reduce, sm2, h3(T8), AX, ALU.add)
            self.V(v.tensor_tensor, T2, r, T2, ALU.mult, after=[t_e])
            t_at = self.V(v.scalar_tensor_tensor, T4, T7, -1.0, T4, ALU.mult, ALU.mult)
            self.V(v.tensor_tensor, T8, k, T3, ALU.mult)
            self.V(v.tensor_tensor, T7, T7, T5, ALU.mult)
            t_bt = self.V(v.tensor_tensor, T3, T7, T3, ALU.mult)
            for c in range(2):
                wc = WC.rearrange("p (h c) -> p c h", c=2)[:, c, :].unsqueeze(2).to_broadcast([P, 4, P])
                self.V(v.tensor_tensor, WCM[:, c], wc, self.c("bd").unsqueeze(1).to_broadcast([P, 4, P]), ALU.mult)
            tt = [self.turn_plain(TA[:, i], src, 4, 4 + i, t_bt) for i, src in enumerate((T4, T2, T3, T8))]
            t_mk = []
            for h in range(8):
                hp, po = h // 2, HD * (h % 2)
                b = h % 4
                pe.wait(tt, t_cx, t_e, t_g, t_mk[h - 4] if h >= 4 else self.last_v)
                out = self.bank(b)
                pe.e.matmul(out[:, 0:256], TA[po:po + HD, 2, hp, :], TA[po:po + HD, 0:2, hp, :], start=True, stop=True,
                            skip_group_check=True)
                ins = pe.e.matmul(out[:, 256:512], TA[po:po + HD, 3, hp, :], TA[po:po + HD, 0:2, hp, :], start=True,
                                  stop=True, skip_group_check=True)
                tp = pe.done(ins)
                t_mk.append(self.V(v.tensor_tensor, MK[:, h].rearrange("p a c -> p (a c)"), out, self.c("mask4"),
                                   ALU.mult, after=[tp]))
            b4 = lambda n: self.c(n).unsqueeze(1).to_broadcast([P, 4, P])
            p4 = lambda b: self.bank(b).rearrange("p (h c) -> p h c", h=4)
            for g in range(2):
                for i in range(4):
                    h = 2 * i + g
                    ins = pe.e.matmul(p4(4 + g)[:, i, :], TA[HD * g:HD * (g + 1), 0, i, :],
                                      TA[HD * g:HD * (g + 1), 2, i, :], start=True, stop=True, skip_group_check=True)
                tp = pe.done(ins)
                self.V(v.tensor_tensor, TI[:, g::2, :], p4(4 + g), b4("low0"), ALU.mult, after=[tp])
                self.V(v.tensor_tensor, TI[:, g::2, :], TI[:, g::2, :], b4("ident"), ALU.add)
                self.V(v.tensor_tensor, TIT[:, g::2, :], MK[:, g::2, 0, :], b4("lowT0"), ALU.mult)
                self.V(v.tensor_tensor, TIT[:, g::2, :], TIT[:, g::2, :], b4("ident"), ALU.add)
            ready = [self.last_v, self.last_v]
            for lv in range(1, 6):
                tx = []
                for g in range(2):
                    pe.wait(ready[g])
                    for i in range(4):
                        h = 2 * i + g
                        ins = pe.e.matmul(p4(3 * g)[:, i, :], MK[:, h, 0, :], TI[:, h, :], start=True, stop=True,
                                          skip_group_check=True)
                    tp = pe.done(ins)
                    tx.append(self.V(v.tensor_tensor, XG[g], p4(3 * g), b4(f"low{lv}"), ALU.mult, after=[tp]))
                ready = []
                for g in range(2):
                    pe.wait(tx[g])
                    for i in range(4):
                        h = 2 * i + g
                        ins = pe.e.matmul(p4(3 * g + 1)[:, i, :], XG[g][:, i, :], TIT[:, h, :], start=True, stop=True,
                                          skip_group_check=True)
                        if lv < 5:
                            ins = pe.e.matmul(p4(3 * g + 2)[:, i, :], TIT[:, h, :], XG[g][:, i, :], start=True,
                                              stop=True, skip_group_check=True)
                    tp = pe.done(ins)
                    t = self.V(v.tensor_tensor, TIT[:, g::2, :], TIT[:, g::2, :], p4(3 * g + 1), ALU.add, after=[tp])
                    if lv < 5:
                        t = self.V(v.tensor_tensor, TI[:, g::2, :], TI[:, g::2, :], p4(3 * g + 2), ALU.add)
                    ready.append(t)
            y = self.bank(7)
            for c in range(2):
                co = slice(HD * c, HD * (c + 1))
                pe.wait(self.last_v)
                for hp in range(4):
                    cols = slice(hp * P, (hp + 1) * P)
                    pe.e.matmul(self.bank(6)[co, cols], TA[:, 0, hp, co], ST[:, hp, :], start=hp == 0, stop=False,
                                skip_group_check=True)
                    pe.e.matmul(y[co, cols], TA[:, 1, hp, co], ST[:, hp, :], start=hp == 0, stop=False,
                                skip_group_check=True)
                for h in range(8):
                    hc = slice(h * HD, (h + 1) * HD)
                    ins = pe.e.matmul(self.bank(6)[co, hc], MK[:, h, 2, co], val[:, hc], start=False, stop=True,
                                      skip_group_check=True)
                tp = pe.done(ins)
                if c == 0:
                    t = self.V(v.memset, RHS[HD:P, :], 0.0)
                    t = self.V(v.memset, U[HD:P, :], 0.0)
                t = self.V(v.tensor_copy, RHS[co, :], self.bank(6)[co, :], after=[tp])
                pe.wait(t)
                for h in range(8):
                    hc = slice(h * HD, (h + 1) * HD)
                    ins = pe.e.matmul(self.bank(5)[co, hc], TIT[:, h, co], RHS[:, hc], start=True, stop=True,
                                      skip_group_check=True)
                tp = pe.done(ins)
                t = self.V(v.tensor_copy, U[co, :], self.bank(5)[co, :], after=[tp])
                pe.wait(t)
                for hp in range(4):
                    cols = slice(hp * P, (hp + 1) * P)
                    pe.e.matmul(self.bank(4)[:, cols], T3[co, cols], U[co, cols], start=True, stop=False,
                                skip_group_check=True)
                    ins = pe.e.matmul(self.bank(4)[:, cols], T8[co, cols], val[co, cols], start=False, stop=True,
                                      skip_group_check=True)
                tp = pe.done(ins)
                self.V(v.tensor_tensor, ST, ST, p4(4), ALU.add, after=[tp])
                self.V(v.tensor_tensor, ST, ST, WCM[:, c], ALU.mult)
            for h in range(8):
                hc = slice(h * HD, (h + 1) * HD)
                pe.e.matmul(y[:, hc], MK[:, h, 1, :], U[:, hc], start=False, stop=False, skip_group_check=True)
                ins = pe.e.matmul(y[:, hc], MK[:, h, 3, :], val[:, hc], start=False, stop=True, skip_group_check=True)
            tp = pe.done(ins)
            y3 = h3(y)
            self.V(v.tensor_reduce, MU, y3, AX, ALU.add, after=[tp])
            self.V(v.tensor_scalar, MU, MU, 1.0 / HD, None, ALU.mult)
            self.V(v.tensor_tensor, h3(r), y3, bc(MU), ALU.subtract)
            self.V(v.tensor_tensor, T2, r, r, ALU.mult)
            self.V(v.tensor_reduce, sm3, h3(T2), AX, ALU.add)
            t = self.rstd(sm3, sm3, HD, GN_EPS, self.last_v)
            self.V(v.tensor_tensor, h3(r), h3(r), bc(sm3), ALU.mult, after=[t])
            self.V(v.tensor_tensor, r, r, rows[:, R_LW:R_LW + 512], ALU.mult)
            self.V(v.tensor_tensor, r, r, rows[:, R_LB:R_LB + 512], ALU.add)
            self.V(v.tensor_tensor, h3(T2), h3(val), bc(sm2), ALU.mult)
            self.V(v.tensor_tensor, r, r, T2, ALU.add)
            t = self.V(v.tensor_tensor, r, r, T6, ALU.mult, after=[t_g])
        self.top = mark
        return t

    def mark_dve(self):
        return self.dve.done(self.dve.e.memset(self.SM[:, 100:101], 0.0))

    def cross_attention(self, par):
        Z, mark = self.Z, self.top
        dve, act, pe = self.dve, self.act, self.pe
        v = self.dve.e
        pv = self.PV
        MEM, Q, K, VV = (self.mem(NT, n) for n in (D, 512, 512, 512))
        QT, KT, tmp = self.mem(4, S), self.mem(4, S), self.mem(512)
        SB, PT, O = self.mem(4, S), self.mem(8 * P), self.mem(NT, 512)
        sm = self.SM[:, 0:4]
        self.act.wait(self.x_ready)
        t_mem = self.load("d_mem", MEM, self.a["mem"].rearrange("(t p) d -> p t d", p=P))
        toks = self.norm_turn(self.X, pv[:, PV_X:PV_X + 8], [4, 5, 6, 7], self.x_ready)
        tok = self.gemm([0, 1], 8, toks=toks)
        t_q = [self.A(Q[:, t, :], self.bank(t), ACT.Copy, after=[tok]) for t in range(NT)][-1]
        toks = self.norm_turn(MEM, pv[:, PV_MEM:PV_MEM + 8], [4, 5, 6, 7], t_mem)
        tok = self.gemm([2, 3], 8, toks=toks)
        t_k = [self.A(K[:, t, :], self.bank(2 + t), ACT.Copy, after=[tok]) for t in range(NT)][-1]
        tok = self.gemm([0, 1], 8, after=[t_q])
        t_v = [self.A(VV[:, t, :], self.bank(t), ACT.Copy, after=[tok]) for t in range(NT)][-1]
        tq = []
        b = 4
        for x, gain, dst, tok in ((Q, PV_XQ, QT, t_q), (K, PV_XK, KT, t_k)):
            for t_ in range(NT):
                t = self.head_norm(x[:, t_, :], 4, P, tmp, sm, [tok, *toks, self.last_v])
                self.last_v = t
                tq.append(self.turn_plain(dst[:, :, t_ * P:(t_ + 1) * P], x[:, t_, :], 4, b, t,
                                          gain=pv[:, gain:gain + 1]))
                b += 1
        free = None
        for qt in range(NT):
            pe.wait(tq, free)
            for h in range(4):
                ins = pe.e.matmul(self.bank(4 + h // 2)[:, (h % 2) * S:(h % 2 + 1) * S],
                                  QT[:, h, qt * P:(qt + 1) * P], KT[:, h, :], start=True, stop=True,
                                  skip_group_check=True)
            tp = pe.done(ins)
            t = self.V(v.tensor_scalar, SB.rearrange("p h k -> p (h k)"), self.bank(4, nb=2), float(P) ** -0.5, None,
                       ALU.mult, after=[tp, free])
            t_o, free = self.softmax_pv(qt, 4, P, SB, S, lambda h, k: VV[:, k, h * P:(h + 1) * P], O[:, qt, :], PT,
                                        t, [free, t_v], [2, 3], 1 - qt)
            self.last_v = t_o
        toks = self.turn([[O[:, t, k * P:(k + 1) * P] for t in range(NT)] for k in range(4)], [4, 5, 6, 7],
                         ready=self.last_v)
        self.gemm([0, 1], 4, toks=toks)
        tok = self.gemm([2, 3], 4)
        self.top = mark
        return self.add_to_x([[0, 2], [1, 3]], 1.0, tok)

    def block1(self, stop=None):
        a, nc = self.a, self.nc
        self.top = 0
        self.XN, self.H, self.SG = self.mem(NT, D), self.mem(NT, 256), self.mem(NT, 256)
        rows, self.LORA, pv, self.Z = self.mem(R_N), self.mem(3, 512), self.mem(48), self.mem(NT, ZN)
        self.PV = pv
        self.layer0 = 0

        def layer(l):
            par = self.load("d_par", pv[:, 0:PV_N], a["pv1"][bass.ds(l, 1)].rearrange("a p n -> p (a n)"))
            t_rows = self.load("d_rows", rows, a["rows1"][bass.ds(l, 1)].rearrange("a b n -> (a b) n").to_broadcast(
                [P, R_N]))
            lora = self.load("d_lora", self.LORA, a["lora"][bass.ds(l, 1)].rearrange("a k p n -> p (a k) n"))
            t = self.ffn(pv[:, PV_FFN1:PV_FFN1 + 8], 0, [self.start, par])
            toks = self.norm_turn(self.X, pv[:, PV_MIX:PV_MIX + 8], [4, 5, 6, 7], t)
            self.z_ready = self.column_groups(self.Z, 3, [ZN - 6 * 512], [t, *toks])
            self.last_v = t_o = self.attention(t_rows, rows)
            t_r = self.rwkv(t_rows, rows, lora, t_o)
            src = [ZQ, ZQ + 128] + [128 * i for i in range(4)] + [ZQ + 256, ZQ + 384]
            toks = self.turn([[self.Z[:, t, c:c + P] for t in range(NT)] for c in src], [4, 5, 6, 7], ready=t_r)
            self.gemm([0, 1], 8, toks=toks)
            tok = self.gemm([2, 3], 8)
            self.x_ready = self.add_to_x([[0, 2], [1, 3]], 1.0, tok)
            t = self.cross_attention(par)
            t = self.ffn(pv[:, PV_FFN2:PV_FFN2 + 8], NJ, t)

        self.layers(UNITS1, layer)

    def layers(self, per, layer):
        base = self.done_units
        sems = [self.pe.sem.num, self.act.sem.num, self.dve.sem.num, self.pool.sem.num] + [s.num for s in
                                                                                           self.ev.values()]
        lo, hi = min(sems), max(sems)
        assert hi - lo + 1 == len(sems)
        with self.nc.Fori(0, DEPTH, engines=self.compute) as l:
            for e in self.engines:
                e.n, e.seen = 0, {}
            self.last_v = None
            self.unit, self.scope = 0, base + l * per
            self.scope_use = base // RING + l * (per // RING)
            self.layer_no = l
            self.loaded = {}
            layer(l)
            assert self.unit == per, (self.unit, per)
            self.nc.multi_engine_barrier(list(self.compute), sems_to_clear=range(lo, hi + 1))
        self.done_units += DEPTH * per
        for name in self.loaded:
            self.dma_base[name] += 16 * DEPTH
        for e in self.engines:
            e.n, e.seen = 0, {}
        self.last_v = None

    def block2(self):
        a = self.a
        dve, act, pe = self.dve, self.act, self.pe
        v = self.dve.e
        self.top = 0
        self.XN = self.mem(NT, D)
        Pm, rows, PW, pv, band = self.mem(NT, PN), self.mem(Q_N), self.mem(4, P), self.mem(24), self.mem(4, NT, S)
        rest = self.top
        t_band = self.load_band(band)

        def col(t, name, n=512):
            return Pm[:, t, PC[name]:PC[name] + n]

        def layer(l):
            par = self.load("d_par", pv[:, 0:PW_N], a["pv2"][bass.ds(l, 1)].rearrange("a p n -> p (a n)"))
            t_rows = self.load("d_rows", rows, a["rows2"][bass.ds(l, 1)].rearrange("a b n -> (a b) n").to_broadcast(
                [P, Q_N]))
            t_pw = self.load("d_lora", PW, a["poolw"][bass.ds(l, 1)].rearrange("a g p n -> p (a g) n"))
            toks = self.norm_turn(self.X, pv[:, PW_NORM:PW_NORM + 8], [4, 5, 6, 7], par)
            ready = self.column_groups(Pm, 8, [512, 72], toks)
            self.last_v = None
            for t in range(NT):
                act.wait(ready)
                for n, w in (("cg", 512), ("ag", 512), ("pg", 512)):
                    t_silu = self.A(col(t, n), col(t, n), ACT.Silu)
            for t in range(NT):
                t_sig = self.A(col(t, "mg", 3 * D), col(t, "mg", 3 * D), ACT.Sigmoid)
            merged = [col(t, "mg", D) for t in range(NT)]
            self.top = rest
            ZT, BG, cv = self.mem(4, S + 2), self.mem(4, S), self.mem(4, S)
            self.V(v.memset, ZT[:, :, 0:2], 0.0, after=[ready])
            tz = []
            for t in range(NT):
                t1 = self.V(v.tensor_tensor, col(t, "cc"), col(t, "cc"), col(t, "cx"), ALU.mult)
                tz.append(self.turn_plain(ZT[:, :, 2 + t * P:2 + (t + 1) * P], col(t, "cc"), 4, 4 + t, t1))
                t1 = self.V(v.tensor_tensor, col(t, "cb"), col(t, "cb"), col(t, "cg"), ALU.mult, after=[t_silu])
                tz.append(self.turn_plain(BG[:, :, t * P:(t + 1) * P], col(t, "cb"), 4, 6 + t, t1))
            toks = []
            for k in range(4):
                w = [pv[:, PW_CONV + 3 * k + j:PW_CONV + 3 * k + j + 1] for j in range(3)]
                y = cv[:, k, :]
                self.V(v.tensor_scalar, y, ZT[:, k, 0:S], w[0], None, ALU.mult, after=[*tz, par])
                self.V(v.scalar_tensor_tensor, y, ZT[:, k, 1:S + 1], w[1], y, ALU.mult, ALU.add)
                self.V(v.scalar_tensor_tensor, y, ZT[:, k, 2:S + 2], w[2], y, ALU.mult, ALU.add)
                t1 = self.V(v.tensor_tensor, y, y, BG[:, k, :], ALU.mult)
                t1 = self.A(self.AHI[:, k, :], y, ACT.Copy, after=[t1])
                toks.append(self.V(v.tensor_tensor, self.ALO[:, k, :], y, self.AHI[:, k, :].bitcast(F32),
                                   ALU.subtract, after=[t1]))
            self.gemm([0, 1], 4, toks=toks)
            tok = self.gemm([2, 3], 4)
            for t in range(NT):
                for h in range(2):
                    m = merged[t][:, h * 512:(h + 1) * 512]
                    self.V(v.tensor_tensor, m, self.bank(2 * h + t), m, ALU.mult, after=[tok, t_sig])
            POT = cv
            for g in range(4):
                pe.wait(tz, toks, t_band, self.last_v)
                for s in range(NT):
                    ins = pe.e.matmul(self.bank(4 + g, S), col(s, "pu")[:, g * P:(g + 1) * P], band[:, g, s, :],
                                      start=s == 0, stop=s == 1)
                tp = pe.done(ins)
                tg = self.A(POT[:, g, :], self.bank(4 + g, S), ACT.Copy, after=[tp])
            pe.wait(tg, t_pw)
            for t in range(NT):
                for g in range(4):
                    ins = pe.e.matmul(self.bank(4 + t)[:, g * P:(g + 1) * P], POT[:, g, t * P:(t + 1) * P], PW[:, g, :],
                                      start=True, stop=True, skip_group_check=True)
            tp = pe.done(ins)
            for t in range(NT):
                self.V(v.tensor_tensor, col(t, "pu"), self.bank(4 + t), rows[:, Q_PS:Q_PS + 512], ALU.mult,
                       after=[tp, t_rows])
                t1 = self.V(v.tensor_tensor, col(t, "pu"), col(t, "pu"), col(t, "pg"), ALU.mult)
            toks = self.turn([[col(t, "pu")[:, k * P:(k + 1) * P] for t in range(NT)] for k in range(4)],
                             [4, 5, 6, 7], kt0=4, ready=t1)
            self.gemm([0, 1], 4, kt0=4, toks=toks, after=[self.last_v])
            tok = self.gemm([2, 3], 4, kt0=4)
            self.merge(merged, col, 2, tok, self.pool_tmp(cv))
            t_o = self.sparse_attention(Pm, col, rows, t_rows, rest)
            toks = self.turn([[col(t, "q")[:, k * P:(k + 1) * P] for t in range(NT)] for k in range(4)],
                             [4, 5, 6, 7], ready=t_o)
            self.gemm([0, 1], 4, toks=toks, after=[self.last_v])
            tok = self.gemm([2, 3], 4)
            self.top = rest
            t1 = self.merge(merged, col, 1, tok, self.mem(512))
            toks = self.turn([[merged[t][:, k * P:(k + 1) * P] for t in range(NT)] for k in range(8)], [4, 5, 6, 7],
                             ready=t1)
            self.gemm([0, 1], 8, toks=toks)
            tok = self.gemm([2, 3], 8)
            self.add_to_x([[0, 2], [1, 3]], 1.0, tok)

        self.layers(UNITS2, layer)

    def pool_tmp(self, cv):
        return cv.rearrange("p a b -> p (a b)")[:, 0:512]

    def merge(self, merged, col, branch, tok, tmp):
        v = self.dve.e
        for t in range(NT):
            for h in range(2):
                g = col(t, "mg", 3 * D)[:, branch * D + h * 512:branch * D + (h + 1) * 512]
                m = merged[t][:, h * 512:(h + 1) * 512]
                self.V(v.tensor_tensor, g, self.bank(2 * h + t), g, ALU.mult, after=[tok])
                last = self.V(v.tensor_tensor, m, m, g, ALU.add)
        return last

    def load_band(self, band):
        self.nc.gpsimd.dma_start(band.rearrange("p g s t -> p (g s t)"), self.a["band"]).then_inc(self.s_start, 16)
        return Token(self.s_start, 48 + 16)

    def sparse_attention(self, Pm, col, rows, t_rows, rest):
        dve, act, pe = self.dve, self.act, self.pe
        v = self.dve.e
        self.top = rest
        xn = self.XN.rearrange("p a b -> p (a b)")
        QT, KT = (xn[:, i * 1024:(i + 1) * 1024].rearrange("p (h k) -> p h k", h=4) for i in range(2))
        IQT, IKT, SB, PT = self.mem(4, S), self.mem(S), self.mem(8, S), self.mem(16 * P)
        score, M2, SC = self.mem(S), self.mem(S), self.SM[:, 128:384]
        tmp = SB.rearrange("p a b -> p (a b)")
        IK2 = self.SM[:, 384:512]
        sm = self.SM[:, 0:8]
        cos, sin = (self.c(n).rearrange("p (t d) -> p t d", t=NT) for n in ("cos2", "sin2"))
        tq = []
        h8 = lambda x: x.rearrange("p (h d) -> p h d", h=8)
        b = 0
        for t in range(NT):
            t1 = self.rope(h8(col(t, "iq")), 8, 32, cos[:, t, :], sin[:, t, :], tmp, [self.last_v])
            tq.append(self.turn_plain(IQT[:, :, t * P:(t + 1) * P], col(t, "iq"), 4, 4 + b, t1, free=tq[-1:]))
            ik = col(t, "ik", 64)
            t1 = self.rope(ik.unsqueeze(1), 1, 32, cos[:, t, :], sin[:, t, :], tmp, [t1])
            self.last_v = t1
            for c in range(2):
                t1 = self.V(v.tensor_copy, IK2[:, c * 64:(c + 1) * 64], ik, after=tq)
            tq.append(self.turn_plain(IKT[:, t * P:(t + 1) * P].unsqueeze(1), IK2, 1, 5 + b, t1))
            for name, gain, dst in (("q", Q_GQ, QT), ("k", Q_GK, KT)):
                x = col(t, name)
                t1 = self.head_norm(x, 8, HD, tmp[:, 0:512], sm, [self.last_v, t_rows], rows[:, gain:gain + 512])
                t1 = self.rope(h8(x), 8, 32, cos[:, t, :], sin[:, t, :], tmp, [t1])
                self.last_v = t1
                b ^= 2
                tq.append(self.turn_plain(dst[:, :, t * P:(t + 1) * P], x, 4, 4 + b, t1, free=tq[-1:]))
        free = None
        for qt in range(NT):
            nk = P * (qt + 1)
            qs = slice(qt * P, (qt + 1) * P)

            def scores(A, B):
                pe.wait(tq, free, self.last_v)
                for h in range(8):
                    bk, slot, po = 4 + 2 * (h // 4) + h % 2, (h // 2) % 2, HD * (h % 2)
                    ins = pe.e.matmul(self.bank(bk)[:, slot * S:slot * S + nk], A[po:po + HD, h // 2, qs],
                                      B(h)[po:po + HD, 0:nk], start=True, stop=True, skip_group_check=True)
                return pe.done(ins)

            tp = scores(IQT, lambda h: IKT)
            act.wait(free, self.last_v)
            for bk in range(4):
                h0 = 4 * (bk // 2) + bk % 2
                t1 = self.A(SB[:, h0:h0 + 3:2, 0:nk], self.bank(4 + bk).rearrange("p (s k) -> p s k", s=2)[:, :, 0:nk],
                            ACT.Relu, after=[tp], scale=HD ** -0.5)
            iw = col(qt, "iw", 8)
            sc = score[:, 0:nk]
            self.V(v.tensor_scalar, sc, SB[:, 0, 0:nk], iw[:, 0:1], None, ALU.mult, after=[t1])
            for h in range(1, 8):
                self.V(v.scalar_tensor_tensor, sc, SB[:, h, 0:nk], iw[:, h:h + 1], sc, ALU.mult, ALU.add)
            self.V(v.tensor_scalar, sc, sc, 8 ** -0.5, None, ALU.mult)
            self.V(v.tensor_tensor, sc[:, nk - P:nk], sc[:, nk - P:nk], self.c("causal"), ALU.add)
            top8 = self.SM[:, 104:112]
            work = [sc, SC[:, 0:nk]]
            for n in range(8):
                self.V(v.max, top8, work[n % 2])
                self.V(v.match_replace, work[1 - n % 2], top8, work[n % 2], TAKEN)
            m2 = M2[:, 0:nk]
            self.V(v.tensor_scalar, m2, sc, -2e38, NEG, ALU.is_gt, ALU.mult)
            self.V(v.tensor_tensor, m2[:, nk - P:nk], m2[:, nk - P:nk], self.c("causal"), ALU.add)
            tp = scores(QT, lambda h: KT[:, h // 2, :])
            for bk in range(4):
                h0 = 4 * (bk // 2) + bk % 2
                self.V(v.scalar_tensor_tensor, SB[:, h0:h0 + 3:2, 0:nk],
                       self.bank(4 + bk).rearrange("p (s k) -> p s k", s=2)[:, :, 0:nk], HD ** -0.5,
                       m2.unsqueeze(1).to_broadcast([P, 2, nk]), ALU.mult, ALU.add, after=[tp])
            t_o, free = self.softmax_pv(qt, 8, HD, SB[:, :, 0:nk], nk, lambda h, k: col(k, "v")[:, h * HD:(h + 1) * HD],
                                        col(qt, "q"), PT, self.last_v, free, [0, 1, 2], 3)
            self.last_v = t_o
            t_o = self.V(v.tensor_tensor, col(qt, "q"), col(qt, "q"), col(qt, "ag"), ALU.mult)
        return t_o

    def build(self):
        nc, a = self.nc, self.a
        self.POS = nc.alloc_sbuf_tensor("positions", [P, NT], I32)[:, :]
        nc.gpsimd.dma_start(self.X[:, :, :], a["x"].rearrange("(t p) d -> p t d", p=P)).then_inc(self.s_start, 16)
        nc.gpsimd.dma_start(self.C[:, :], a["consts"]).then_inc(self.s_start, 16)
        nc.gpsimd.dma_start(self.POS, a["pos"]).then_inc(self.s_start, 16)
        self.start = Token(self.s_start, 48)
        self.done_units = 0
        nc.tensor.sem_inc(self.s_mm, RING)
        nc.vector.sem_inc(self.s_lo, RING)
        nc.vector.memset(self.zero[:, :], 0.0)
        nc.vector.memset(self.minus_half[:, :], -0.5)
        z = nc.vector.memset(self.SM[:, :], 0.0)
        z.then_inc(self.s_set, 1)
        for e in self.engines:
            e.e.wait_ge(self.s_start, 48)
            e.e.wait_ge(self.s_set, 1)
        with nc.Fori(0, STREAM // RING, engines=(nc.sync.engine,)) as i:
            for u in range(RING):
                nc.sync.wait_ge(self.s_lo, i * RING + (u + 1))
                nc.sync.dma_start(self.raw[u][:, :, :],
                                  a["stream"][bass.ds(i * RING + u, 1)].rearrange("a p (k n) -> p (a k) n", k=2)
                                  ).then_inc(self.s_load[u], 16)
        self.unit = -AHEAD
        self.scope, self.scope_use = 0, 0
        for _ in range(AHEAD):
            self.split_next()
            self.unit += 1
        self.block1()
        self.block2()
        nc.sync.wait_ge(self.s_load[RING - 1], 16 * (STREAM // RING))
        nc.vector.drain().then_inc(self.s_out, 1)
        nc.scalar.wait_ge(self.s_out, 1)
        nc.scalar.dma_start(a["out"].rearrange("(t p) d -> p t d", p=P), self.X[:, :, :]).then_inc(self.s_out, 16)
        nc.scalar.wait_ge(self.s_out, 17)


def two_pi_parts():
    rest, parts = 2 * np.pi, []
    for bits in (2.0 ** 6, 2.0 ** 17):
        parts.append(float(np.floor(rest * bits) / bits))
        rest -= parts[-1]
    return parts + [float(np.float32(rest))]


TWO_PI = two_pi_parts()
PI_IN = float(np.nextafter(np.float32(np.pi), np.float32(0)))


def units(w, cols=None):
    k, n = w.shape
    pad = -n % 512
    if pad:
        w = np.concatenate([w, np.zeros((k, pad), w.dtype)], 1)
    return w.reshape(k // 256, 2, P, (n + pad) // 512, 512).transpose(3, 0, 2, 1, 4).reshape(-1, P, 1024)


def ffn_units(w_in, w_out):
    both = np.stack([w_in[:, :FFN].reshape(D, NJ, 256), w_in[:, FFN:].reshape(D, NJ, 256)], 2)
    both = both.reshape(4, 2, P, NJ, 512).transpose(3, 0, 2, 1, 4).reshape(NJ, 4, P, 1024)
    out = w_out.reshape(NJ, 2, P, 2, 512).transpose(0, 3, 2, 1, 4).reshape(NJ, 2, P, 1024)
    seq = [both[0]]
    for j in range(1, NJ):
        seq += [both[j], out[j - 1]]
    return np.concatenate(seq + [out[NJ - 1]])


def kernel(**inputs):
    import concourse.bacc as bacc
    from concourse.bass_utils import run_bass_kernel_spmd as run

    n = {k: np.asarray(v) for k, v in inputs.items()}
    seq, pv1, rows1, lora, pv2, rows2, poolw = [], [], [], [], [], [], []
    for l in range(DEPTH):
        w = n["mix_w_in"][l]
        f0, m0, r0 = 0, 772, 1540
        w = np.concatenate([w[:, r0:], w[:, 0:256], w[:, m0:m0 + 256], w[:, 256:512], w[:, m0 + 256:m0 + 512],
                            w[:, 512:768], w[:, m0 + 512:m0 + 768], w[:, 768:772]], 1)
        seq += [ffn_units(n["ffn1_w_in"][l], n["ffn1_w_out"][l]), units(w), units(n["mix_w_out"][l]),
                units(n["xattn_w_q"][l]), units(n["xattn_w_kv"][l]), units(n["xattn_w_out"][l]),
                ffn_units(n["ffn2_w_in"][l], n["ffn2_w_out"][l])]
        pv1.append(np.concatenate([n[k][l].reshape(8, P).T for k in
                                   ("ffn1_norm", "mix_norm", "xattn_norm", "xattn_mem_norm", "ffn2_norm")]
                                  + [n[k][l].reshape(P, 1) for k in ("xattn_q_gain", "xattn_k_gain")], 1))
        four = lambda g: [n[g][l]] * 4
        rows1.append(np.concatenate([n["rwkv_mu"][l], n["rwkv_w0"][l], n["rwkv_a0"][l], n["rwkv_k_k"][l],
                                     n["rwkv_k_a"][l], n["rwkv_r_k"][l].reshape(-1), n["rwkv_ln_w"][l],
                                     n["rwkv_ln_b"][l], *four("fox_q_gain"), *four("moba_q_gain"),
                                     *four("fox_k_gain"), *four("moba_k_gain"), n["fox_f_bias"][l]])[None])
        g2 = n["rwkv_g2"][l]
        lora.append(np.stack([np.concatenate([n["rwkv_w2"][l], n["rwkv_a2"][l]]), g2[:P],
                              np.concatenate([g2[P:], np.zeros((P - 32, 512), g2.dtype)])]))
    for l in range(DEPTH):
        w = n["w_in_2"][l]
        w = np.concatenate([w[:, :4608], w[:, 4680:], w[:, 4608:4680]], 1)
        seq += [units(w), units(n["w_out_conv_2"][l]), units(n["w_out_pool_2"][l]), units(n["w_out_attn_2"][l]),
                units(n["w_o_2"][l])]
        pv2.append(np.concatenate([n["norm_g_2"][l].reshape(8, P).T,
                                   n["conv_w_2"][l].reshape(3, 4, P).transpose(2, 1, 0).reshape(P, 12)], 1))
        rows2.append(np.concatenate([np.tile(n["q_norm_g_2"][l], 8), np.tile(n["k_norm_g_2"][l], 8),
                                     n["pool_scale_2"][l]])[None])
        poolw.append(n["pool_w_2"][l])
    stream = np.concatenate(seq + [np.zeros((RING, P, 1024), np.float32)])
    assert stream.shape[0] == STREAM, (stream.shape, STREAM)
    arrays = {"stream": stream, "pv1": np.stack(pv1), "rows1": np.stack(rows1), "lora": np.stack(lora),
              "pv2": np.stack(pv2), "rows2": np.stack(rows2), "poolw": np.stack(poolw),
              "consts": np.concatenate([v for k, v in CONST.items() if k != "band"], 1), "band": CONST["band"],
              "x": n["x"][0], "mem": n["mem"][0], "pos": n["positions"].reshape(NT, P).T}
    arrays = {k: np.ascontiguousarray(v) for k, v in arrays.items()}
    nc = bacc.Bacc("TRN2", target_bir_lowering=False, num_devices=1)
    aps = {k: nc.dram_tensor(k, list(v.shape), I32 if k == "pos" else F32, kind="ExternalInput").ap()
           for k, v in arrays.items()}
    aps["out"] = nc.dram_tensor("out", [S, D], F32, kind="ExternalOutput").ap()
    Program(nc, aps).build()
    r = run(nc, [arrays], core_ids=[0])
    return r.results[0]["out"].reshape(1, S, D)
```

```python
import numpy as np

import concourse.bass as bass
from concourse import mybir

F32 = mybir.dt.float32
F32R = mybir.dt.float32r
BF16 = mybir.dt.bfloat16
I32 = mybir.dt.int32
ACT = mybir.ActivationFunctionType
ALU = mybir.AluOpType
AX = mybir.AxisListType.X

P = 128
S = 256
NT = S // P
D = 1024
DEPTH = 2
FFN = 2816
NJ = FFN // 256
RW = 512
ZR = 1824
HD = 64
RING = 4
AHEAD = 3
UNITS_FFN = 6 * NJ
ZG = 7
UNITS1 = 2 * UNITS_FFN + 4 * ZG + 8 + 8 + 4 + 4
PG = 18
UNITS2 = 4 * PG + 3 * 4 + 8
UNITS = DEPTH * (UNITS1 + UNITS2)
STREAM = UNITS + RING
assert UNITS1 % RING == 0 and UNITS2 % RING == 0
EPS = 1e-6
GN_EPS = 64e-5
NEG = -1e30
TAKEN = -3e38

ZQ, ZK, ZV, ZF, ZN = ZR, ZR + 512, ZR + 1024, ZR + 1536, ZR + 1540
PC = {n: 512 * i for i, n in enumerate(["q", "k", "v", "iq", "ik"])}
PC["iw"] = PC["ik"] + 64
P2 = PC["iw"] + 8
PC.update({n: P2 + 512 * i for i, n in enumerate(["pu", "pg", "cb", "cc", "cx", "cg", "ag", "mg"])})
PN = PC["mg"] + 3 * D

RWKV_WORDS = 4096 + 3 * 512 + 2048 + 2 * 512
PV_FFN1, PV_MIX, PV_X, PV_MEM, PV_FFN2, PV_XQ, PV_XK, PV_N = 0, 8, 16, 24, 32, 40, 41, 42
R_MU = 0
R_W0, R_A0, R_KK, R_KA, R_RK, R_LW, R_LB, R_GQ, R_GK = (ZR + 512 * i for i in range(9))
R_FB = ZR + 512 * 9
R_N = R_FB + 4
PW_NORM, PW_CONV, PW_N = 0, 8, 20
Q_GQ, Q_GK, Q_PS, Q_N = 0, 512, 1024, 1536


def constants():
    s = np.arange(P)[:, None]
    t = np.arange(P)[None, :]
    same = (s // 64) == (t // 64)
    c = {}
    c["ident"] = (s == t)
    c["cum64"] = (s <= t) & same
    c["ones64"] = np.concatenate([(s // 64 == 0), (s // 64 == 1)], 1)
    c["cum"] = np.concatenate([(s + P * k) <= np.arange(S)[None, :] for k in range(NT)], 1)
    up_strict, up_incl = (s < t) & same, (s <= t) & same
    c["mask4"] = np.concatenate([up_strict, up_incl, up_strict, up_incl], 1)
    for lv in range(6):
        b = 1 << lv
        low = ((s // (2 * b)) == (t // (2 * b))) & ((s // b) % 2 == 1) & ((t // b) % 2 == 0)
        c[f"low{lv}"] = low
    c["lowT0"] = c["low0"].T
    c["bd"] = (s // 64 == t // 64)
    c["causal"] = np.where(t <= s, 0.0, NEG)
    band = np.zeros((4, S, S))
    for g, w in enumerate((2, 4, 8, 16)):
        for q in range(S):
            lo = max(0, q - w + 1)
            band[g, lo:q + 1, q] = 1.0 / min(q + 1, w)
        band[g] -= np.eye(S)
    c["band"] = band.reshape(4, NT, P, S).transpose(2, 0, 1, 3).reshape(P, -1)
    inv = (500000.0 ** (-np.arange(0, 16, 2) / 16.0)).astype(np.float32)
    c["inv"] = np.repeat(inv[None, :], P, 0)
    inv2 = np.float32(1.0) / (10000.0 ** (np.arange(0, 64, 2) / 64.0)).astype(np.float32)
    ang = (np.arange(S, dtype=np.float32)[:, None] * inv2[None, :]).astype(np.float32).astype(np.float64)
    for n, f in (("cos2", np.cos), ("sin2", np.sin)):
        c[n] = f(ang).reshape(NT, P, 32).transpose(1, 0, 2).reshape(P, -1)
    return {k: np.ascontiguousarray(v, dtype=np.float32) for k, v in c.items()}


CONST = constants()
BAND_N = 4 * NT * S
COFF, _o = {}, 0
for _k, _v in CONST.items():
    if _k != "band":
        COFF[_k] = (_o, _v.shape[1])
        _o += _v.shape[1]
CN = _o


class Token:

    def __init__(self, sem, val):
        self.sem, self.val = sem, val


class Engine:

    def __init__(self, nc, eng, name):
        self.e, self.sem, self.n, self.seen = eng, nc.alloc_semaphore(f"done_{name}"), 0, {}
        self.name = name

    def wait(self, *toks):
        for t in toks:
            if t is None:
                continue
            if isinstance(t, (list, tuple)):
                self.wait(*t)
            elif not isinstance(t.val, int):
                self.e.wait_ge(t.sem, t.val)
            elif self.seen.get(id(t.sem), 0) < t.val:
                self.seen[id(t.sem)] = t.val
                self.e.wait_ge(t.sem, t.val)

    def done(self, ins):
        self.n += 1
        ins.then_inc(self.sem, 1)
        return Token(self.sem, self.n)


class Program:
    def __init__(self, nc, a):
        self.nc, self.a = nc, a
        self.pe, self.act = Engine(nc, nc.tensor, "pe"), Engine(nc, nc.scalar, "act")
        self.dve, self.pool = Engine(nc, nc.vector, "dve"), Engine(nc, nc.gpsimd, "pool")
        self.engines = [self.pe, self.act, self.dve, self.pool]
        self.compute = tuple(e.e.engine for e in self.engines)
        self.last_v = None
        self.rs, self.t_rs = {}, {}
        self.ev = {n: nc.alloc_semaphore(n) for n in
                   ("silu", "h_ready", "h_turned", "ht_hi", "ht_lo", "z_act", "z_dve")}
        self.dma = {n: nc.alloc_semaphore(n) for n in ("d_par", "d_rows", "d_lora", "d_mem", "d_shift1",
                                                       "d_shift1_row", "d_shift0")}
        self.dma_base = {n: 0 for n in self.dma}
        sb = nc.alloc_sbuf_tensor
        self.raw = [sb(f"raw{i}", [P, 2, 512], F32) for i in range(RING)]
        self.whi = [sb(f"whi{i}", [P, 2, 512], F32R) for i in range(RING)]
        self.wlo = [sb(f"wlo{i}", [P, 2, 512], F32R) for i in range(RING)]
        self.s_load = [nc.alloc_semaphore(f"loaded{i}") for i in range(RING)]
        self.s_hi, self.s_lo, self.s_mm = (nc.alloc_semaphore(n) for n in ("split_hi", "split_lo", "unit_used"))
        self.X = sb("x_res", [P, NT, D], F32)
        self.AHI, self.ALO = sb("a_hi", [P, 8, S], F32R), sb("a_lo", [P, 8, S], F32R)
        self.HHI, self.HLO = sb("h_hi", [P, 2, S], F32R), sb("h_lo", [P, 2, S], F32R)
        self.zero = sb("zero", [P, 512], BF16)
        self.minus_half = sb("minus_half", [P, 16], F32)
        self.C = sb("const_tables", [P, CN], F32)
        self.SM = sb("small", [P, 512], F32)
        self.arena_n = (212863 - 48 * 1024 - 8192 - 16384 - 4096 - 1024 - CN * 4 - 2048 - 1056) // 4 // 8 * 8
        self.arena = sb("arena", [P, self.arena_n], F32)
        self.top = 0
        self.PS = nc.alloc_psum_tensor("ps", [P, 8 * 512], F32)
        self.s_start = nc.alloc_semaphore("loaded_start")
        self.s_set = nc.alloc_semaphore("constants_set")
        self.s_out = nc.alloc_semaphore("stored")
        self.unit = 0
        self.scope = 0

    def V(self, method, *args, after=(), **kw):
        self.dve.wait(self.last_v, *after)
        self.last_v = self.dve.done(method(*args, **kw))
        return self.last_v

    def A(self, out, in_, func, after=(), **kw):
        self.act.wait(*after)
        return self.act.done(self.act.e.activation(out, in_, func, **kw))

    def bank(self, b, n=512, nb=1):
        return self.PS[:, b * 512:b * 512 + (n if nb == 1 else nb * 512)]

    def mem(self, *shape):
        n = int(np.prod(shape))
        v = self.arena[:, self.top:self.top + n]
        self.top += n
        assert self.top <= self.arena_n, (self.top, self.arena_n)
        if len(shape) == 1:
            return v
        names = "abcd"[:len(shape)]
        return v.rearrange(f"p ({' '.join(names)}) -> p {' '.join(names)}", **dict(zip(names, shape)))

    def c(self, name):
        o, n = COFF[name]
        return self.C[:, o:o + n]

    def event(self, name, val):
        return Token(self.ev[name], val)

    def split_next(self):
        m = self.unit + AHEAD
        i = m % RING
        n = self.scope + m
        use = self.scope_use + m // RING
        self.act.e.wait_ge(self.s_load[i], use * 16 + 16)
        self.act.e.wait_ge(self.s_mm, n + 1)
        self.act.e.activation(self.whi[i][:, :, :], self.raw[i][:, :, :], ACT.Copy).then_inc(self.s_hi, 1)
        self.dve.e.wait_ge(self.s_hi, n + 1)
        self.dve.e.tensor_tensor(self.wlo[i][:, :, :], self.raw[i][:, :, :], self.whi[i][:, :, :].bitcast(F32),
                                 ALU.subtract).then_inc(self.s_lo, 1)

    def products(self, jobs, ahi, alo, after=()):
        self.split_next()
        i = self.unit % RING
        n = self.scope + self.unit
        self.pe.wait(*after)
        self.pe.e.wait_ge(self.s_lo, n + (RING + 1))
        hi, lo = self.whi[i], self.wlo[i]
        for out, kk, kt, t, start in jobs:
            w = out.shape[1]
            a_h, a_l = ahi[:, kt, t * P:(t + 1) * P], alo[:, kt, t * P:(t + 1) * P]
            mm = self.pe.e.matmul
            mm(out, a_h, hi[:, kk, 0:w], start=start, stop=False, skip_group_check=True)
            mm(out, a_h, lo[:, kk, 0:w], start=False, stop=False, skip_group_check=True)
            last = mm(out, a_l, hi[:, kk, 0:w], start=False, stop=True, skip_group_check=True)
        last.then_inc(self.s_mm, 1)
        self.unit += 1
        return Token(self.s_mm, n + (RING + 1))

    def gemm(self, *args, **kw):
        return self.drain(self.gemm_steps(*args, **kw))

    def drain(self, steps):
        while True:
            try:
                next(steps)
            except StopIteration as end:
                return end.value

    def gemm_steps(self, banks, nk, kt0=0, width=512, toks=None, after=(), first=True):
        for u in range(nk // 2):
            need = [toks[kt0 + 2 * u + 1]] if toks else []
            jobs = [(self.bank(banks[t], width), kk, kt0 + 2 * u + kk, t, first and u == 0 and kk == 0)
                    for kk in range(2) for t in range(NT)]
            tok = self.products(jobs, self.AHI, self.ALO, after=[*need, *(after if u == 0 else ())])
            yield 2.6
        return tok

    def rstd(self, out, ss, n, eps, tok):
        self.dve.wait(tok)
        t = self.dve.done(self.dve.e.tensor_scalar(out, ss, 1.0 / n, eps, ALU.mult, ALU.add))
        return self.power(out, t)

    def power(self, x, tok):
        self.pool.wait(tok)
        half = self.minus_half[:, 0:x.shape[1]]
        return self.pool.done(self.pool.e.tensor_tensor(x, x, half, ALU.pow))

    def turn(self, cols, banks, gain=None, kt0=0, ready=None):
        toks, left = [None] * kt0, {}
        for k, src in enumerate(cols):
            b = banks[k % len(banks)]
            self.pe.wait(ready[k] if isinstance(ready, list) else ready, left.get(b))
            for t in range(NT):
                ins = self.pe.e.transpose(self.bank(b)[:, t * P:(t + 1) * P], src[t], self.c("ident"))
            tp = self.pe.done(ins)
            self.act.wait(tp)
            ps = self.bank(b, S)
            scale = gain[:, k:k + 1] if gain is not None else 1.0
            th = self.act.done(self.act.e.activation(self.AHI[:, kt0 + k, :], ps, ACT.Copy, scale=scale))
            self.dve.wait(th)
            if gain is None:
                ins = self.dve.e.tensor_tensor(self.ALO[:, kt0 + k, :], ps, self.AHI[:, kt0 + k, :].bitcast(F32),
                                               ALU.subtract)
            else:
                ins = self.dve.e.scalar_tensor_tensor(self.ALO[:, kt0 + k, :], ps, scale,
                                                      self.AHI[:, kt0 + k, :].bitcast(F32), ALU.mult, ALU.subtract)
            left[b] = self.dve.done(ins)
            toks.append(left[b])
        return toks

    def norm_turn(self, src, gain, banks, halves, slot=0, junk=None):
        toks = self.turn([[src[:, t, k * P:(k + 1) * P] for t in range(NT)] for k in range(8)], banks, gain,
                         ready=[halves[k // 4] for k in range(8)])
        rs, ss = (self.SM[:, o:o + NT] for o in (72 + 4 * slot, 74 + 4 * slot))
        ta = None
        for t in range(NT):
            out = self.XN[:, t, :] if junk is None else junk
            ta = self.A(out, src[:, t, :], ACT.Square, after=[*halves, ta], accum_out=ss[:, t:t + 1])
        self.rs[slot] = [rs[:, t:t + 1] for t in range(NT)]
        self.t_rs[slot] = self.rstd(rs, ss, D, EPS, ta)
        return toks

    def add_half(self, h, banks, scale, tok):
        self.dve.wait(tok)
        for t in range(NT):
            x = self.X[:, t, h * 512:(h + 1) * 512]
            ins = self.dve.e.scalar_tensor_tensor(x, self.bank(banks[t]), scale, x, ALU.mult, ALU.add)
        return self.dve.done(ins)

    def project(self, nk, toks, after=()):
        halves = []
        for h in range(2):
            tok = self.gemm([2 * h, 2 * h + 1], nk, toks=toks, after=after)
            halves.append(self.add_half(h, [2 * h, 2 * h + 1], 1.0, tok))
        return halves

    def ffn_in(self, j, toks=None):
        after = [] if toks else [self.event("h_ready", 2 * j)]
        for u in range(4):
            need = [toks[2 * u + 1]] if toks else []
            jobs = [(self.bank(4 + t), kk, 2 * u + kk, t, u == 0 and kk == 0) for kk in range(2) for t in range(NT)]
            tok = self.products(jobs, self.AHI, self.ALO, after=[*need, *(after if u == 0 else ())])
        if toks:
            self.act.wait(self.t_rs[0])
            self.dve.wait(self.t_rs[0])
        for t in range(NT):
            self.act.wait(tok)
            self.act.e.activation(self.SG[:, t, :], self.bank(4 + t, 256), ACT.Silu,
                                  scale=self.rs[0][t]).then_inc(self.ev["silu"], 1)
            self.dve.wait(self.event("silu", 2 * j + (t + 1)))
            self.dve.e.scalar_tensor_tensor(self.H[:, t, :], self.bank(4 + t)[:, 256:512], self.rs[0][t],
                                            self.SG[:, t, :], ALU.mult, ALU.mult).then_inc(self.ev["h_ready"], 1)

    def ffn_turn(self, j, first=False):
        self.pe.wait(self.event("h_ready", 2 * j + 2))
        if not first:
            self.pe.wait(self.event("ht_lo", 2 * j))
        for kk in range(2):
            for t in range(NT):
                ins = self.pe.e.transpose(self.bank(6 + kk)[:, t * P:(t + 1) * P],
                                          self.H[:, t, kk * P:(kk + 1) * P], self.c("ident"))
            ins.then_inc(self.ev["h_turned"], 1)
        for kk in range(2):
            self.act.wait(self.event("h_turned", 2 * j + (kk + 1)))
            self.act.e.activation(self.HHI[:, kk, :], self.bank(6 + kk, S), ACT.Copy).then_inc(self.ev["ht_hi"], 1)
            self.dve.wait(self.event("ht_hi", 2 * j + (kk + 1)))
            self.dve.e.tensor_tensor(self.HLO[:, kk, :], self.bank(6 + kk, S), self.HHI[:, kk, :].bitcast(F32),
                                     ALU.subtract).then_inc(self.ev["ht_lo"], 1)

    def ffn_out(self, j):
        toks = []
        for h in range(2):
            jobs = [(self.bank(2 * t + h), kk, kk, t, False) for kk in range(2) for t in range(NT)]
            toks.append(self.products(jobs, self.HHI, self.HLO,
                                      after=[self.event("ht_lo", 2 * j + 2)] if h == 0 else ()))
        return toks

    def loop(self, count, per, body):
        for e in self.engines:
            e.seen = {}
        outer, outer_use, n0, counts = self.scope, self.scope_use, self.unit, [e.n for e in self.engines]
        assert per % RING == 0
        with self.nc.Fori(0, count, engines=self.compute) as i:
            self.scope, self.scope_use = outer + i * per, outer_use + i * (per // RING)
            body(i)
            assert self.unit == n0 + per and counts == [e.n for e in self.engines]
        self.scope, self.scope_use, self.unit = outer, outer_use, n0 + count * per
        for e in self.engines:
            e.seen = {}

    def ffn(self, gain, jb, halves):
        toks = self.norm_turn(self.X, gain, [6, 7, 0, 1, 2, 3], halves)
        self.ffn_in(jb, toks)
        self.pe.wait(toks)
        for b in range(4):
            self.pe.e.matmul(self.bank(b), self.zero[:, 0:P], self.zero[:, :], start=True, stop=False,
                             skip_group_check=True)
        self.ffn_turn(jb, first=jb == 0)

        def body(i):
            for u in range(2):
                j = i * 2 + (jb + 1 + u)
                self.ffn_in(j)
                self.ffn_out(j - 1)
                self.ffn_turn(j)

        self.loop((NJ - 1) // 2, 12, body)
        toks = self.ffn_out(jb + NJ - 1)
        return [self.add_half(h, [h, 2 + h], 0.5, toks[h]) for h in range(2)]

    def column_group(self, dst, g, col, width, banks, before, toks=(), func=None):
        tok = yield from self.gemm_steps(
            banks, 8, width=width, after=[*toks, self.event("z_act", before + 2), self.event("z_dve", before + 2)])
        cols = slice(col, col + width) if isinstance(col, int) else bass.ds(col, width)
        self.act.wait(tok)
        self.act.e.activation(dst[:, 0, cols], self.bank(banks[0], width), func or ACT.Copy,
                              scale=self.rs[0][0]).then_inc(self.ev["z_act"], 1)
        if func is None:
            self.dve.wait(tok)
            self.dve.e.tensor_scalar(dst[:, 1, cols], self.bank(banks[1], width), self.rs[0][1], None,
                                     ALU.mult).then_inc(self.ev["z_dve"], 1)
        else:
            self.act.e.activation(dst[:, 1, cols], self.bank(banks[1], width), func,
                                  scale=self.rs[0][1]).then_inc(self.ev["z_dve"], 1)
        return [self.event("z_act", g + 3), self.event("z_dve", g + 3)]

    def column_loop(self, dst, count, toks):
        for e, n in ((self.act, "z_act"), (self.dve, "z_dve")):
            e.e.sem_inc(self.ev[n], 2)
        self.pe.wait(toks)
        self.act.wait(self.t_rs[0])
        self.dve.wait(self.t_rs[0])

        def body(i):
            for u in range(2):
                g = i * 2 + u
                self.drain(self.column_group(dst, g, g * 512, 512, [2 * u, 2 * u + 1], g - 1))

        self.loop(count, 8, body)
        return [self.event("z_act", 2 * count + 2), self.event("z_dve", 2 * count + 2)]

    def weave(self, *threads):
        clocks = [[0.0, n, t] for n, t in enumerate(threads)]
        while clocks:
            now = min(clocks, key=lambda c: (c[0], c[1]))
            try:
                now[0] += next(now[2])
            except StopIteration:
                clocks.remove(now)

    def head_norm(self, x, nh, hd, tmp, sm, ready, gain=None):
        e = self.dve
        e.wait(ready)
        x3 = x.rearrange("p (h d) -> p h d", h=nh)
        t = e.done(e.e.tensor_tensor(tmp, x, x, ALU.mult))
        e.wait(t)
        t = e.done(e.e.tensor_reduce(sm, tmp.rearrange("p (h d) -> p h d", h=nh), AX, ALU.add))
        t = self.rstd(sm, sm, hd, EPS, t)
        yield 1.5 + nh * hd / 500
        e.wait(t)
        t = e.done(e.e.tensor_tensor(x3, x3, sm.unsqueeze(2).to_broadcast([P, nh, hd]), ALU.mult))
        if gain is not None:
            e.wait(t)
            t = e.done(e.e.tensor_tensor(x, x, gain, ALU.mult))
        return t

    def rope(self, x, nh, half, cos, sin, tmp, ready):
        e = self.dve
        e.wait(ready)
        x1, x2 = x[:, :, 0:half], x[:, :, half:2 * half]
        cb, sb = (a.unsqueeze(1).to_broadcast([P, nh, half]) for a in (cos, sin))
        v = tmp[:, 0:3 * nh * half].rearrange("p (a h d) -> p a h d", a=3, h=nh)
        e.e.tensor_tensor(v[:, 0], x2, sb, ALU.mult)
        e.e.tensor_tensor(v[:, 1], x1, sb, ALU.mult)
        e.e.tensor_tensor(v[:, 2], x2, cb, ALU.mult)
        t = e.done(e.e.tensor_tensor(x1, x1, cb, ALU.mult))
        e.wait(t)
        e.e.tensor_tensor(x1, x1, v[:, 0], ALU.subtract)
        return e.done(e.e.tensor_tensor(x2, v[:, 2], v[:, 1], ALU.add))

    def turn_plain(self, dst, src, n, b, ready, gain=None, free=None, on=None):
        self.pe.wait(ready, free)
        for k in range(n):
            ins = self.pe.e.transpose(self.bank(b)[:, k * P:(k + 1) * P], src[:, k * P:(k + 1) * P], self.c("ident"))
        tp = self.pe.done(ins)
        e = on or self.act
        e.wait(tp)
        v = self.bank(b, n * P).rearrange("p (k c) -> p k c", k=n)
        if e is self.act:
            return e.done(e.e.activation(dst, v, ACT.Copy, scale=gain if gain is not None else 1.0))
        if gain is not None:
            return e.done(e.e.tensor_scalar(dst, v, gain, None, ALU.mult))
        return e.done(e.e.tensor_copy(dst, v))

    def softmax_pv(self, nh, hd, SB, nk, v_of, out, PT, tok, free, banks_t, bank_o, res):
        dve, act, pe = self.dve, self.act, self.pe
        mx, sm = self.SM[:, 32:32 + nh], self.SM[:, 48:48 + nh]
        dve.wait(tok)
        t = dve.done(dve.e.tensor_reduce(mx, SB, AX, ALU.max))
        dve.wait(t)
        t = dve.done(dve.e.tensor_scalar(mx, mx, -1.0, None, ALU.mult))
        act.wait(t)
        te = []
        for h in range(nh):
            te.append(act.done(act.e.activation(SB[:, h, :], SB[:, h, :], ACT.Exp, bias=mx[:, h:h + 1],
                                                accum_out=sm[:, h:h + 1])))
            yield 0.45
        dve.wait(te[-1])
        tr = dve.done(dve.e.reciprocal(sm, sm))
        nkt = nk // P
        per = 4
        todo = [(h, k) for h in range(nh) for k in range(nkt)]
        left, ready = {}, {}
        for g in range(0, len(todo), per):
            b = banks_t[(g // per) % len(banks_t)]
            part = todo[g:g + per]
            pe.wait(te[part[-1][0]], left.get(b), free)
            for n, (h, k) in enumerate(part):
                ins = pe.e.transpose(self.bank(b)[:, n * P:(n + 1) * P], SB[:, h, k * P:(k + 1) * P], self.c("ident"))
            tp = pe.done(ins)
            e = dve if (g // per) % 2 else act
            e.wait(tp)
            dst = PT[:, g * P:(g + len(part)) * P]
            if e is act:
                left[b] = act.done(act.e.activation(dst, self.bank(b, len(part) * P), ACT.Copy))
            else:
                left[b] = dve.done(dve.e.tensor_copy(dst, self.bank(b, len(part) * P)))
            for h, k in part:
                ready[h, k] = left[b]
            yield 0.8
        for h in range(nh):
            for k in range(nkt):
                pe.wait(ready[h, k])
                n = todo.index((h, k))
                ins = pe.e.matmul(self.bank(bank_o)[:, h * hd:(h + 1) * hd], PT[:, n * P:(n + 1) * P], v_of(h, k),
                                  start=(k == 0), stop=(k == nkt - 1), skip_group_check=True)
            if h < nh - 1 and h % 4 == 3:
                yield 0.8
        tp = pe.done(ins)
        dve.wait(tp, tr)
        o3 = self.bank(bank_o, nh * hd).rearrange("p (h d) -> p h d", h=nh)
        self.last_v = dve.done(dve.e.tensor_tensor(out.rearrange("p (h d) -> p h d", h=nh), o3,
                                                   sm.unsqueeze(2).to_broadcast([P, nh, hd]), ALU.mult))
        res[:] = [self.last_v, tp]
        yield 0.8



    def load(self, name, dst, src):
        assert name not in self.loaded
        self.loaded[name] = True
        self.nc.scalar.dma_start(dst, src).then_inc(self.dma[name], 16)
        return Token(self.dma[name], self.layer_no * 16 + (self.dma_base[name] + 16))

    def attention(self, par, rows, t_z, banks):
        Z = self.Z
        act, pe = self.act, self.pe
        v = self.dve.e
        even, odd, bt = banks
        QT, KT, SB, PT = self.mem(2, S), self.mem(2, S), self.mem(4, S), self.mem(8 * P)
        for t_ in range(NT):
            self.last_v = yield from self.head_norm(Z[:, t_, ZQ:ZQ + 1024], 16, HD, SB.rearrange("p h k -> p (h k)"),
                                                    self.SM[:, 112:128], [self.last_v, t_z, par],
                                                    rows[:, R_GQ:R_GQ + 1024])
            yield 2
        tmp = SB.rearrange("p h k -> p (h k)")
        LF, LN, CS, pos, aux = self.mem(NT, 4), self.mem(NT, 4), self.mem(NT, 2, 8), self.mem(NT), self.mem(80)
        f = aux[:, 0:8].rearrange("p (t h) -> p t h", t=NT)
        ab = aux[:, 8:16].rearrange("p (t h) -> p t h", t=NT)
        fb = rows[:, R_FB:R_FB + 4].unsqueeze(1).to_broadcast([P, NT, 4])
        self.V(v.tensor_tensor, f, Z[:, :, ZF:ZF + 4], fb, ALU.add, after=[t_z, par])
        t = self.V(v.scalar_tensor_tensor, ab, f, -1.0, f, ALU.mult, ALU.max)
        t = self.A(ab, ab, ACT.Exp, after=[t], scale=-1.0)
        t = self.A(ab, ab, ACT.Ln, after=[t], bias=1.0)
        yield 2
        self.V(v.scalar_tensor_tensor, LF, f, 0.0, ab, ALU.min, ALU.subtract, after=[t])
        self.V(v.tensor_scalar, LF, LF, float(HD) ** 0.5, None, ALU.mult)
        t_lf = self.V(v.tensor_scalar, LN, LF, -1.0, None, ALU.mult)
        self.V(v.tensor_copy, pos, self.POS)
        ang, n = (aux[:, o:o + 32].rearrange("p (t a d) -> p t a d", t=NT, a=2) for o in (16, 48))
        for t_ in range(NT):
            for a in range(2):
                self.V(v.tensor_scalar, ang[:, t_, a, :], self.c("inv"), pos[:, t_:t_ + 1], None, ALU.mult)
        yield 1
        to_int = float(1.5 * 2 ** 23)
        for a, quarter in ((0, 0.25), (1, 0.0)):
            self.V(v.tensor_scalar, n[:, :, a, :], ang[:, :, a, :], float(1 / (2 * np.pi)), quarter, ALU.mult, ALU.add)
        self.V(v.tensor_scalar, n, n, to_int, None, ALU.add)
        self.V(v.tensor_scalar, n, n, to_int, None, ALU.subtract)
        for part in TWO_PI:
            self.V(v.scalar_tensor_tensor, ang, n, -part, ang, ALU.mult, ALU.add)
        self.V(v.tensor_scalar, ang[:, :, 0, :], ang[:, :, 0, :], float(np.pi / 2), None, ALU.add)
        t = self.V(v.tensor_scalar, ang, ang, PI_IN, -PI_IN, ALU.min, ALU.max)
        t_cs = self.A(CS, ang, ACT.Sin, after=[t])
        yield 2
        scale = float(HD) ** -0.5
        free = None
        for fox in (True, False):
            off = 0 if fox else 256
            tq, t_r = [], self.last_v
            if not fox:
                for t_ in range(NT):
                    for src in (ZQ + off, ZK + off):
                        self.last_v = t_r = self.rope(Z[:, t_, src:src + 256].rearrange("p (h d) -> p h d", h=4), 4, 8,
                                                      CS[:, t_, 0, :], CS[:, t_, 1, :], tmp,
                                                      [self.last_v, t_cs, free])
                    yield 1.2
            for t_ in range(NT):
                for src, dst in ((ZQ, QT), (ZK, KT)):
                    b = banks[len(tq) % 2]
                    tq.append(self.turn_plain(dst[:, :, t_ * P:(t_ + 1) * P], Z[:, t_, src + off:src + off + 256], 2,
                                              b, [t_r, free], free=tq[-2:]))
                    yield 0.5
            for qt in range(NT):
                nk = P * (qt + 1)
                qs = slice(qt * P, (qt + 1) * P)
                pe.wait(tq, t_lf, free, self.last_v)
                for h in range(4):
                    hp, po = h // 2, HD * (h % 2)
                    out = self.bank((even, odd)[h % 2])[:, hp * S:hp * S + nk]
                    ins = pe.e.matmul(out, QT[po:po + HD, hp, qs], KT[po:po + HD, hp, 0:nk], start=True, stop=not fox,
                                      skip_group_check=True)
                    if fox:
                        for st in range(qt + 1):
                            cum = self.c("cum")[:, st * S:(st + 1) * S]
                            pe.e.matmul(out, cum[:, qs], LF[:, st, h:h + 1].to_broadcast([P, nk]), start=False,
                                        stop=False, skip_group_check=True)
                            ins = pe.e.matmul(out, LN[:, st, h:h + 1].to_broadcast([P, P]), cum[:, 0:nk],
                                              start=False, stop=st == qt, skip_group_check=True)
                    if h < 3:
                        yield 0.5
                tp = pe.done(ins)
                for g in range(2):
                    ps = self.bank((even, odd)[g]).rearrange("p (s k) -> p s k", s=2)
                    dst = SB[:, g::2, :]
                    mask = self.c("causal").unsqueeze(1).to_broadcast([P, 2, P])
                    t_s = self.V(v.scalar_tensor_tensor, dst[:, :, nk - P:nk], ps[:, :, nk - P:nk], scale, mask,
                                 ALU.mult, ALU.add, after=[tp, free])
                    if qt:
                        t_s = self.V(v.tensor_scalar, dst[:, :, 0:P], ps[:, :, 0:P], scale, None, ALU.mult)
                yield 1
                res = []
                yield from self.softmax_pv(4, HD, SB[:, :, 0:nk], nk,
                                           lambda h, k: Z[:, k, ZV + off + h * HD:ZV + off + (h + 1) * HD],
                                           Z[:, qt, ZQ + off:ZQ + off + 256], PT, t_s, free, [bt, odd], even, res)
                self.t_att, free = res

    def rwkv(self, par, rows, lora, t_z, banks, base):
        Z, act, pe = self.Z, self.act, self.pe
        v = self.dve.e
        B0, B1, B2, B3, B4 = banks
        side_top, self.top = self.top, base
        shared = self.mem(4096)
        ZS = shared[:, 0:ZR]
        T1, T2, T4, T5, T7 = (shared[:, i * 512:(i + 1) * 512] for i in range(5))
        T3, T6, T8 = (self.mem(512) for _ in range(3))
        TA = self.mem(4, 4, P)
        MK = shared.rearrange("p (h a c) -> p h a c", h=8, a=4)
        RHS, ST = self.mem(512), self.mem(4, P)
        mk0 = shared[:, 2560:4096]
        assert self.top == base + RWKV_WORDS
        self.top = side_top
        L, LT = mk0[:, 0:288], mk0[:, 512:512 + 384].rearrange("p (k c) -> p k c", k=3)
        ZS2 = self.XN.rearrange("p a b -> p (a b)")[:, 0:ZR]
        xn = self.XN.rearrange("p a b -> p (a b)")
        TI, TIT = (xn[:, i * 1024:(i + 1) * 1024].rearrange("p (h c) -> p h c", h=8) for i in range(2))
        hh = [self.H.rearrange("p a b -> p (a b)"), self.SG.rearrange("p a b -> p (a b)")]
        XG = [x.rearrange("p (h c) -> p h c", h=4) for x in hh]
        U, WCM = rows[:, 0:512], rows[:, 512:1536].rearrange("p (c h d) -> p c h d", c=2, h=4)
        sm = self.SM[:, 0:8]
        sm2, sm3, WC, MU = self.SM[:, 8:16], self.SM[:, 16:24], self.SM[:, 24:32], self.SM[:, 64:72]
        act.wait(t_z)
        shifted = [self.load("d_shift1", ZS2[1:P, :], Z[0:P - 1, 1, 0:ZR]),
                   self.load("d_shift1_row", ZS2[0:1, :], Z[P - 1:P, 0, 0:ZR])]
        t = self.V(v.memset, ZS[0:1, :], 0.0, after=[t_z])
        act.wait(t)
        shifted.append(self.load("d_shift0", ZS[1:P, :], Z[0:P - 1, 0, 0:ZR]))
        mu = rows[:, R_MU:R_MU + ZR]
        for t_, z in ((1, ZS2), (0, ZS)):
            zt = Z[:, t_, 0:ZR]
            self.V(v.tensor_tensor, z, z, zt, ALU.subtract, after=[*shifted, par])
            self.V(v.tensor_tensor, z, z, mu, ALU.mult)
            self.V(v.tensor_tensor, zt, zt, z, ALU.add)
            yield 6
        self.V(v.memset, ST, 0.0)
        decay = -float(np.exp(-0.5))
        h3 = lambda x: x.rearrange("p (h d) -> p h d", h=8)
        bc = lambda s: s.unsqueeze(2).to_broadcast([P, 8, HD])
        for t_ in range(NT):
            r, k, val = (Z[:, t_, i * 512:(i + 1) * 512] for i in range(3))
            zl = Z[:, t_, 3 * 512:ZR]
            t0 = self.last_v
            self.A(L[:, 0:64], zl[:, 0:64], ACT.Tanh, after=[t0])
            self.A(L[:, 64:128], zl[:, 64:128], ACT.Copy)
            ta = self.A(L[:, 128:288], zl[:, 128:288], ACT.Sigmoid)
            yield 1.5
            pe.wait(ta, t0)
            for i, w in enumerate((128, 128, 32)):
                ins = pe.e.transpose(self.bank(B0)[0:w, i * P:(i + 1) * P], L[:, i * P:i * P + w], self.c("ident"))
            tp = pe.done(ins)
            self.A(LT[:, 0:2, :], self.bank(B0, 256).rearrange("p (k c) -> p k c", k=2), ACT.Copy, after=[tp])
            ta = self.A(LT[0:32, 2, :], self.bank(B0)[0:32, 256:384], ACT.Copy)
            yield 2.5
            pe.wait(ta, lora)
            W = self.LORA
            pe.e.matmul(self.bank(B1), LT[0:64, 0, :], W[0:64, 0, :], start=True, stop=True)
            pe.e.matmul(self.bank(B2), LT[64:128, 0, :], W[64:128, 0, :], start=True, stop=True)
            pe.e.matmul(self.bank(B3), LT[:, 1, :], W[:, 1, :], start=True, stop=False)
            tp = pe.done(pe.e.matmul(self.bank(B3), LT[0:32, 2, :], W[0:32, 2, :], start=False, stop=True))
            yield 3.5
            self.V(v.tensor_tensor, T1, self.bank(B1), rows[:, R_W0:R_W0 + 512], ALU.add, after=[tp])
            t = self.V(v.tensor_tensor, T5, self.bank(B2), rows[:, R_A0:R_A0 + 512], ALU.add)
            self.A(T1, T1, ACT.Sigmoid, after=[t])
            t_a = self.A(T5, T5, ACT.Sigmoid)
            t_g = self.A(T6, self.bank(B3), ACT.Copy)
            yield 2.5
            t_ld = self.V(v.tensor_scalar, T1, T1, decay, None, ALU.mult, after=[t_a])
            yield 1
            pe.wait(t_ld)
            tp = pe.done(pe.e.matmul(self.bank(B1), self.c("cum64"), T1, start=True, stop=True))
            for hp in range(4):
                ins = pe.e.matmul(self.bank(B2)[:, 2 * hp:2 * hp + 2], T1[:, hp * P:(hp + 1) * P], self.c("ones64"),
                                  start=True, stop=True, skip_group_check=True)
            tw = pe.done(ins)
            t_cx = self.V(v.tensor_tensor, T4, self.bank(B1), T1, ALU.subtract, after=[tp])
            self.A(T2, self.bank(B1), ACT.Exp, after=[tp, t_cx])
            self.A(T3, self.bank(B1), ACT.Exp, scale=-1.0)
            self.A(T4, T4, ACT.Exp)
            t_e = self.A(WC, self.bank(B2, 8), ACT.Exp, after=[tw])
            yield 2
            self.V(v.tensor_tensor, T7, k, rows[:, R_KK:R_KK + 512], ALU.mult)
            self.V(v.tensor_tensor, T8, T7, T7, ALU.mult)
            self.V(v.tensor_reduce, sm, h3(T8), AX, ALU.add)
            t = self.V(v.tensor_scalar, sm, sm, 1e-24, None, ALU.max)
            t = self.power(sm, t)
            self.V(v.tensor_tensor, h3(T7), h3(T7), bc(sm), ALU.mult, after=[t])
            self.V(v.scalar_tensor_tensor, T8, T5, -1.0, rows[:, R_KA:R_KA + 512], ALU.add, ALU.mult)
            self.V(v.scalar_tensor_tensor, k, T8, 1.0, k, ALU.add, ALU.mult)
            self.V(v.tensor_tensor, T8, r, k, ALU.mult)
            self.V(v.tensor_tensor, T8, T8, rows[:, R_RK:R_RK + 512], ALU.mult)
            self.V(v.tensor_reduce, sm2, h3(T8), AX, ALU.add)
            yield 8
            self.V(v.tensor_tensor, T2, r, T2, ALU.mult, after=[t_e])
            t_at = self.V(v.scalar_tensor_tensor, T4, T7, -1.0, T4, ALU.mult, ALU.mult)
            self.V(v.tensor_tensor, T8, k, T3, ALU.mult)
            self.V(v.tensor_tensor, T7, T7, T5, ALU.mult)
            t_bt = self.V(v.tensor_tensor, T3, T7, T3, ALU.mult)
            for c in range(2):
                wc = WC.rearrange("p (h c) -> p c h", c=2)[:, c, :].unsqueeze(2).to_broadcast([P, 4, P])
                self.V(v.tensor_tensor, WCM[:, c], wc, self.c("bd").unsqueeze(1).to_broadcast([P, 4, P]), ALU.mult)
            yield 4.5
            tt = [self.turn_plain(TA[:, i], src, 4, b, t_bt, free=[t_g, t_e, t_cx])
                  for i, (src, b) in enumerate(((T4, B0), (T2, B4), (T3, B3), (T8, B1)))]
            yield 2.5
            t_mk = []
            for h in range(8):
                hp, po = h // 2, HD * (h % 2)
                b = banks[h % 5]
                pe.wait(tt, t_mk[h - 5] if h >= 5 else None)
                out = self.bank(b)
                pe.e.matmul(out[:, 0:256], TA[po:po + HD, 2, hp, :], TA[po:po + HD, 0:2, hp, :], start=True, stop=True,
                            skip_group_check=True)
                ins = pe.e.matmul(out[:, 256:512], TA[po:po + HD, 3, hp, :], TA[po:po + HD, 0:2, hp, :], start=True,
                                  stop=True, skip_group_check=True)
                tp = pe.done(ins)
                t_mk.append(self.V(v.tensor_tensor, MK[:, h].rearrange("p a c -> p (a c)"), out, self.c("mask4"),
                                   ALU.mult, after=[tp]))
                yield 0.9
            b4 = lambda n: self.c(n).unsqueeze(1).to_broadcast([P, 4, P])
            p4 = lambda b: self.bank(b).rearrange("p (h c) -> p h c", h=4)
            for g in range(2):
                nb = (B3, B4)[g]
                pe.wait(t_mk)
                for i in range(4):
                    h = 2 * i + g
                    ins = pe.e.matmul(p4(nb)[:, i, :], TA[HD * g:HD * (g + 1), 0, i, :],
                                      TA[HD * g:HD * (g + 1), 2, i, :], start=True, stop=True, skip_group_check=True)
                tp = pe.done(ins)
                self.V(v.tensor_tensor, TI[:, g::2, :], p4(nb), b4("low0"), ALU.mult, after=[tp])
                self.V(v.tensor_tensor, TI[:, g::2, :], TI[:, g::2, :], b4("ident"), ALU.add)
                self.V(v.tensor_tensor, TIT[:, g::2, :], MK[:, g::2, 0, :], b4("lowT0"), ALU.mult)
                self.V(v.tensor_tensor, TIT[:, g::2, :], TIT[:, g::2, :], b4("ident"), ALU.add)
                yield 2.5
            ready = [self.last_v, self.last_v]
            xb, tb = (B0, B2), (B1, B3)
            for lv in range(1, 6):
                tx = []
                for g in range(2):
                    pe.wait(ready[g])
                    for i in range(4):
                        h = 2 * i + g
                        ins = pe.e.matmul(p4(xb[g])[:, i, :], MK[:, h, 0, :], TI[:, h, :], start=True, stop=True,
                                          skip_group_check=True)
                    tp = pe.done(ins)
                    tx.append(self.V(v.tensor_tensor, XG[g], p4(xb[g]), b4(f"low{lv}"), ALU.mult, after=[tp]))
                    yield 0.9
                ready = []
                for g in range(2):
                    pe.wait(tx[g])
                    for i in range(4):
                        h = 2 * i + g
                        ins = pe.e.matmul(p4(xb[g])[:, i, :], XG[g][:, i, :], TIT[:, h, :], start=True, stop=True,
                                          skip_group_check=True)
                        if lv < 5:
                            ins = pe.e.matmul(p4(tb[g])[:, i, :], TIT[:, h, :], XG[g][:, i, :], start=True,
                                              stop=True, skip_group_check=True)
                    tp = pe.done(ins)
                    t = self.V(v.tensor_tensor, TIT[:, g::2, :], TIT[:, g::2, :], p4(xb[g]), ALU.add, after=[tp])
                    if lv < 5:
                        t = self.V(v.tensor_tensor, TI[:, g::2, :], TI[:, g::2, :], p4(tb[g]), ALU.add)
                    ready.append(t)
                    yield 1.8
            y = self.bank(B4)
            self.V(v.memset, RHS[HD:P, :], 0.0)
            t = self.V(v.memset, U[HD:P, :], 0.0)
            for c in range(2):
                co = slice(HD * c, HD * (c + 1))
                pe.wait(self.last_v)
                for hp in range(4):
                    cols = slice(hp * P, (hp + 1) * P)
                    pe.e.matmul(self.bank(B0)[co, cols], TA[:, 0, hp, co], ST[:, hp, :], start=hp == 0, stop=False,
                                skip_group_check=True)
                    pe.e.matmul(y[co, cols], TA[:, 1, hp, co], ST[:, hp, :], start=hp == 0, stop=False,
                                skip_group_check=True)
                for h in range(8):
                    hc = slice(h * HD, (h + 1) * HD)
                    ins = pe.e.matmul(self.bank(B0)[co, hc], MK[:, h, 2, co], val[:, hc], start=False, stop=True,
                                      skip_group_check=True)
                tp = pe.done(ins)
                yield 2.5
                t = self.A(RHS[co, :], self.bank(B0)[co, :], ACT.Copy, after=[tp, t])
                yield 0.7
                pe.wait(t)
                for h in range(8):
                    hc = slice(h * HD, (h + 1) * HD)
                    ins = pe.e.matmul(self.bank(B1)[co, hc], TIT[:, h, co], RHS[:, hc], start=True, stop=True,
                                      skip_group_check=True)
                tp = pe.done(ins)
                yield 1.2
                t = self.A(U[co, :], self.bank(B1)[co, :], ACT.Copy, after=[tp])
                yield 0.7
                pe.wait(t)
                for hp in range(4):
                    cols = slice(hp * P, (hp + 1) * P)
                    pe.e.matmul(self.bank(B2)[:, cols], T3[co, cols], U[co, cols], start=True, stop=False,
                                skip_group_check=True)
                    ins = pe.e.matmul(self.bank(B2)[:, cols], T8[co, cols], val[co, cols], start=False, stop=True,
                                      skip_group_check=True)
                tp = pe.done(ins)
                yield 1.8
                self.V(v.tensor_tensor, ST, ST, p4(B2), ALU.add, after=[tp])
                self.V(v.tensor_tensor, ST, ST, WCM[:, c], ALU.mult)
                yield 1.4
            for h in range(8):
                hc = slice(h * HD, (h + 1) * HD)
                pe.e.matmul(y[:, hc], MK[:, h, 1, :], U[:, hc], start=False, stop=False, skip_group_check=True)
                ins = pe.e.matmul(y[:, hc], MK[:, h, 3, :], val[:, hc], start=False, stop=True, skip_group_check=True)
            tp = pe.done(ins)
            y3 = h3(y)
            yield 2
            self.V(v.tensor_reduce, MU, y3, AX, ALU.add, after=[tp])
            self.V(v.tensor_scalar, MU, MU, 1.0 / HD, None, ALU.mult)
            self.V(v.tensor_tensor, h3(r), y3, bc(MU), ALU.subtract)
            self.V(v.tensor_tensor, T2, r, r, ALU.mult)
            self.V(v.tensor_reduce, sm3, h3(T2), AX, ALU.add)
            t = self.rstd(sm3, sm3, HD, GN_EPS, self.last_v)
            self.V(v.tensor_tensor, h3(r), h3(r), bc(sm3), ALU.mult, after=[t])
            self.V(v.tensor_tensor, r, r, rows[:, R_LW:R_LW + 512], ALU.mult)
            self.V(v.tensor_tensor, r, r, rows[:, R_LB:R_LB + 512], ALU.add)
            yield 6
            self.V(v.tensor_tensor, h3(T2), h3(val), bc(sm2), ALU.mult)
            self.V(v.tensor_tensor, r, r, T2, ALU.add)
            self.t_rwkv = self.V(v.tensor_tensor, r, r, T6, ALU.mult, after=[t_g])
            yield 2

    def memory_kv(self, par, banks):
        pv, act = self.PV, self.act
        self.KT = self.mem(4, S)
        K, VV = self.mem(NT, 512), self.mem(NT, 512)
        MEM = self.arena[:, self.top - 2048:self.top].rearrange("p (t d) -> p t d", t=NT)
        kt = self.KT.rearrange("p h k -> p (h k)")
        self.VV = VV
        act.wait(self.t_att)
        t_mem = self.load("d_mem", MEM, self.a["mem"].rearrange("(t p) d -> p t d", p=P))
        yield 4
        toks = self.norm_turn(MEM, pv[:, PV_MEM:PV_MEM + 8], banks, [t_mem, t_mem], slot=1, junk=kt)
        rs = self.rs[1]
        yield 6
        b = banks[:2]
        tok = yield from self.gemm_steps(b, 8, toks=toks, after=[toks])
        t_k = [self.A(K[:, t, :], self.bank(b[t]), ACT.Copy, after=[tok, self.t_rs[1]], scale=rs[t])
               for t in range(NT)][-1]
        tok = yield from self.gemm_steps(b, 8, after=[t_k])
        self.t_v = [self.A(VV[:, t, :], self.bank(b[t]), ACT.Copy, after=[tok], scale=rs[t]) for t in range(NT)][-1]
        self.t_kt = []
        tmp, sm = self.Z[:, 0, ZK:ZK + 512], self.SM[:, 116:120]
        for t_ in range(NT):
            self.last_v = t = yield from self.head_norm(K[:, t_, :], 4, P, tmp, sm, [t_k, self.last_v])
            yield 1
            self.t_kt.append(self.turn_plain(self.KT[:, :, t_ * P:(t_ + 1) * P], K[:, t_, :], 4, banks[2], t,
                                             gain=pv[:, PV_XK:PV_XK + 1], free=self.t_kt[-1:]))

    def cross_attention(self, halves):
        mark = self.top
        act, pe = self.act, self.pe
        v = self.dve.e
        pv = self.PV
        Q = self.mem(NT, 512)
        QT, tmp = self.mem(4, S), self.mem(512)
        SB, PT, O = self.mem(4, S), self.mem(8 * P), self.mem(NT, 512)
        sm = self.SM[:, 0:4]
        toks = self.norm_turn(self.X, pv[:, PV_X:PV_X + 8], [4, 5, 6, 7], halves)
        tok = self.gemm([0, 1], 8, toks=toks)
        t_q = [self.A(Q[:, t, :], self.bank(t), ACT.Copy, after=[tok, self.t_rs[0]], scale=self.rs[0][t])
               for t in range(NT)]
        tq = []
        for t_ in range(NT):
            t = self.drain(self.head_norm(Q[:, t_, :], 4, P, tmp, sm, [t_q[t_], *toks, self.last_v]))
            self.last_v = t
            tq.append(self.turn_plain(QT[:, :, t_ * P:(t_ + 1) * P], Q[:, t_, :], 4, 4 + t_, t,
                                      gain=pv[:, PV_XQ:PV_XQ + 1]))
        free = None
        for qt in range(NT):
            pe.wait(tq, self.t_kt, free)
            for h in range(4):
                ins = pe.e.matmul(self.bank(6 + h // 2)[:, (h % 2) * S:(h % 2 + 1) * S],
                                  QT[:, h, qt * P:(qt + 1) * P], self.KT[:, h, :], start=True, stop=True,
                                  skip_group_check=True)
            tp = pe.done(ins)
            t = self.V(v.tensor_scalar, SB.rearrange("p h k -> p (h k)"), self.bank(6, nb=2), float(P) ** -0.5, None,
                       ALU.mult, after=[tp, free])
            res = []
            self.drain(self.softmax_pv(4, P, SB, S, lambda h, k: self.VV[:, k, h * P:(h + 1) * P], O[:, qt, :], PT,
                                       t, [free, self.t_v], [2, 3], 1 - qt, res))
            free = res[1]
        toks = self.turn([[O[:, t, k * P:(k + 1) * P] for t in range(NT)] for k in range(4)], [4, 5, 6, 7],
                         ready=self.last_v)
        self.top = mark
        return self.project(4, toks, after=[self.last_v])

    def block1(self):
        a = self.a
        self.top = 0
        self.XN, self.H, self.SG = self.mem(NT, D), self.mem(NT, 256), self.mem(NT, 256)
        rows, self.LORA, pv, self.Z = self.mem(R_N), self.mem(3, 512), self.mem(48), self.mem(NT, ZN)
        self.PV = pv
        fixed = self.top

        def sources(first):
            return [[self.Z[:, t, first + k * P:first + (k + 1) * P] for t in range(NT)] for k in range(4)]

        def side(par, t_rows, toks, mark):
            widths = [512, 512, ZN - 6 * 512]
            for n, w in enumerate(widths):
                g = 4 + n
                t_z = yield from self.column_group(self.Z, g, 512 * g, w, [0, 1], g)
            yield from self.attention(t_rows, rows, t_z, [0, 1, 2])
            self.top = mark
            yield from self.memory_kv(par, [0, 1, 2])
            self.t_turned = self.turn(sources(ZQ), [2], ready=(self.t_att, self.t_kt))
            yield 3
            yield from self.gemm_steps([0, 1], 4, toks=self.t_turned, after=[self.t_v])

        def layer(l):
            par = self.load("d_par", pv[:, 0:PV_N], a["pv1"][bass.ds(l, 1)].rearrange("a p n -> p (a n)"))
            t_rows = self.load("d_rows", rows, a["rows1"][bass.ds(l, 1)].rearrange("a b n -> (a b) n").to_broadcast(
                [P, R_N]))
            lora = self.load("d_lora", self.LORA, a["lora"][bass.ds(l, 1)].rearrange("a k p n -> p (a k) n"))
            halves = self.ffn(pv[:, PV_FFN1:PV_FFN1 + 8], 0, [par, par])
            toks = self.norm_turn(self.X, pv[:, PV_MIX:PV_MIX + 8], [4, 5, 6, 7], halves)
            t_z = self.column_loop(self.Z, 2, [*halves, *toks])
            self.top = fixed + RWKV_WORDS
            rec = self.rwkv(t_rows, rows, lora, [*t_z, *toks], [3, 4, 5, 6, 7], fixed)
            self.weave(rec, side(par, t_rows, toks, fixed + RWKV_WORDS))
            self.gemm([2, 3], 4, toks=self.t_turned, after=[self.t_kt, self.t_turned])
            toks = self.turn(sources(0), [4, 5, 6, 7], kt0=4, ready=(self.t_rwkv,))
            halves = []
            for h in range(2):
                tok = self.gemm([2 * h, 2 * h + 1], 4, kt0=4, toks=toks, first=False)
                halves.append(self.add_half(h, [2 * h, 2 * h + 1], 1.0, tok))
            self.top = fixed
            halves = self.cross_attention(halves)
            self.ffn(pv[:, PV_FFN2:PV_FFN2 + 8], NJ, halves)

        self.layers(UNITS1, layer)

    def layers(self, per, layer):
        base = self.done_units
        sems = [self.pe.sem.num, self.act.sem.num, self.dve.sem.num, self.pool.sem.num] + [s.num for s in
                                                                                           self.ev.values()]
        lo, hi = min(sems), max(sems)
        assert hi - lo + 1 == len(sems)
        with self.nc.Fori(0, DEPTH, engines=self.compute) as l:
            for e in self.engines:
                e.n, e.seen = 0, {}
            self.last_v = None
            self.unit, self.scope = 0, base + l * per
            self.scope_use = base // RING + l * (per // RING)
            self.layer_no = l
            self.loaded = {}
            layer(l)
            assert self.unit == per, (self.unit, per)
            self.nc.multi_engine_barrier(list(self.compute), sems_to_clear=range(lo, hi + 1))
        self.done_units += DEPTH * per
        for name in self.loaded:
            self.dma_base[name] += 16 * DEPTH
        for e in self.engines:
            e.n, e.seen = 0, {}
        self.last_v = None

    def block2(self):
        a = self.a
        pe = self.pe
        v = self.dve.e
        self.top = 0
        self.XN = self.mem(NT, D)
        Pm, rows, PW, pv, band = self.mem(NT, PN), self.mem(Q_N), self.mem(4, P), self.mem(24), self.mem(4, NT, S)
        rest = self.top
        t_band = self.load_band(band)

        def col(t, name, n=512, skip=0):
            return Pm[:, t, PC[name] + skip:PC[name] + skip + n]

        def by_feature(t, name):
            return col(t, name, 1024).rearrange("p (k s) -> p k s", k=4)

        merged = [col(t, "mg", D) for t in range(NT)]
        ZT, BG, CV = by_feature(0, "cx"), by_feature(1, "cx"), by_feature(0, "cb")
        POT = col(1, "mg", 1024, 2 * D).rearrange("p (k s) -> p k s", k=4)

        def conv_and_pool(ready, par, t_rows, t_pw, b):
            left = None
            for g2 in range(2):
                pe.wait(ready["pu"], t_band, left)
                for g in range(2 * g2, 2 * g2 + 2):
                    for s in range(NT):
                        ins = pe.e.matmul(self.bank(b)[:, (g % 2) * S:(g % 2 + 1) * S],
                                          col(s, "pu")[:, g * P:(g + 1) * P], band[:, g, s, :], start=s == 0,
                                          stop=s == 1, skip_group_check=True)
                tp = pe.done(ins)
                left = self.A(POT[:, 2 * g2:2 * g2 + 2, :], self.bank(b).rearrange("p (k s) -> p k s", k=2), ACT.Copy,
                              after=[tp])
            yield 4
            for t in range(NT):
                pe.wait(left, t_pw)
                for g in range(4):
                    ins = pe.e.matmul(self.bank(b)[:, g * P:(g + 1) * P], POT[:, g, t * P:(t + 1) * P], PW[:, g, :],
                                      start=True, stop=True, skip_group_check=True)
                tp = pe.done(ins)
                left = self.V(v.tensor_tensor, col(t, "pu"), self.bank(b), rows[:, Q_PS:Q_PS + 512], ALU.mult,
                              after=[tp, t_rows, *ready["pg"]])
                self.t_pool = self.V(v.tensor_tensor, col(t, "pu"), col(t, "pu"), col(t, "pg"), ALU.mult)
                yield 1.5
            yield 0
            t_in = []
            for t in range(NT):
                self.V(v.tensor_tensor, col(t, "cc"), col(t, "cc"), col(t, "cx"), ALU.mult, after=[ready["cg"]])
                t_in = self.V(v.tensor_tensor, col(t, "cb"), col(t, "cb"), col(t, "cg"), ALU.mult)
            yield 2
            for dst, src in ((ZT, "cc"), (BG, "cb")):
                for t in range(NT):
                    left = self.turn_plain(dst[:, :, t * P:(t + 1) * P], col(t, src), 4, b, [t_in, left])
                    yield 1.5
            for k in range(4):
                w = [pv[:, PW_CONV + 3 * k + j:PW_CONV + 3 * k + j + 1] for j in range(3)]
                self.V(v.tensor_scalar, CV[:, k, :], ZT[:, k, :], w[2], None, ALU.mult, after=[left, par])
                for j in (1, 2):
                    y = CV[:, k, j:]
                    self.V(v.scalar_tensor_tensor, y, ZT[:, k, 0:S - j], w[2 - j], y, ALU.mult, ALU.add)
            self.t_conv = self.V(v.tensor_tensor, CV, CV, BG, ALU.mult)
            self.t_branch = left
            yield 3

        def side(toks, par, t_rows, t_pw):
            silu = {"pg", "cg", "ag"}
            ready = {}
            extras = conv_and_pool(ready, par, t_rows, t_pw, 2)
            names = ["pu", "pg", "cb", "cc", "cx", "cg", "ag"] + ["mg"] * 6
            for n, name in enumerate(names):
                g = 5 + n
                func = ACT.Silu if name in silu else ACT.Sigmoid if name == "mg" else None
                ready[name] = yield from self.column_group(Pm, g, P2 + 512 * n, 512, [0, 1], g, func=func)
                if n:
                    yield next(extras, 0)
            t1 = self.A(self.AHI[:, 0:4, :], CV, ACT.Copy, after=[self.t_conv, *ready["mg"]])
            t1 = self.V(v.tensor_tensor, self.ALO[:, 0:4, :], CV, self.AHI[:, 0:4, :].bitcast(F32), ALU.subtract,
                        after=[t1])
            left = ready["mg"]
            for h in range(2):
                tok = yield from self.gemm_steps([0, 1], 4, toks=[t1] * 4, after=[left])
                left = self.merge(merged, col, 0, h, [0, 1], tok)
                yield 0
            toks = self.turn([[col(t, "pu")[:, k * P:(k + 1) * P] for t in range(NT)] for k in range(4)],
                             [2], kt0=4, ready=(self.t_pool, self.t_branch))
            yield 3
            for h in range(2):
                tok = yield from self.gemm_steps([0, 1], 4, kt0=4, toks=toks, after=[left])
                left = self.merge(merged, col, 2, h, [0, 1], tok)
            self.t_side = left

        def layer(l):
            par = self.load("d_par", pv[:, 0:PW_N], a["pv2"][bass.ds(l, 1)].rearrange("a p n -> p (a n)"))
            t_rows = self.load("d_rows", rows, a["rows2"][bass.ds(l, 1)].rearrange("a b n -> (a b) n").to_broadcast(
                [P, Q_N]))
            t_pw = self.load("d_lora", PW, a["poolw"][bass.ds(l, 1)].rearrange("a g p n -> p (a g) n"))
            toks = self.norm_turn(self.X, pv[:, PW_NORM:PW_NORM + 8], [4, 5, 6, 7], [par, par])
            self.column_loop(Pm, 2, toks)
            t_q = self.drain(self.column_group(Pm, 4, PC["ik"], 72, [0, 1], 4))
            self.top = rest
            self.weave(self.sparse_attention(Pm, col, rows, t_rows, [*t_q, *toks], [3, 4, 5, 6, 7]),
                       side(toks, par, t_rows, t_pw))
            for t in range(NT):
                t1 = self.V(v.tensor_tensor, col(t, "q"), col(t, "q"), col(t, "ag"), ALU.mult, after=[self.t_side])
            toks = self.turn([[col(t, "q")[:, k * P:(k + 1) * P] for t in range(NT)] for k in range(4)],
                             [4, 5, 6, 7], ready=t1)
            ready = []
            for h in range(2):
                banks = [2 * h, 2 * h + 1]
                tok = self.gemm(banks, 4, toks=toks, after=[t1])
                ready += [self.merge(merged, col, 1, h, banks, tok)] * 4
            toks = self.turn([[merged[t][:, k * P:(k + 1) * P] for t in range(NT)] for k in range(8)], [4, 5, 6, 7],
                             ready=ready)
            self.project(8, toks, after=[ready[-1]])

        self.layers(UNITS2, layer)

    def merge(self, merged, col, branch, h, banks, tok):
        v = self.dve.e
        for t in range(NT):
            g = col(t, "mg", 512, branch * D + h * 512)
            last = self.V(v.tensor_tensor, g, self.bank(banks[t]), g, ALU.mult, after=[tok])
            if branch:
                m = merged[t][:, h * 512:(h + 1) * 512]
                last = self.V(v.tensor_tensor, m, m, g, ALU.add)
        return last

    def load_band(self, band):
        self.nc.gpsimd.dma_start(band.rearrange("p g s t -> p (g s t)"), self.a["band"]).then_inc(self.s_start, 16)
        return Token(self.s_start, 48 + 16)

    def sparse_attention(self, Pm, col, rows, t_rows, t_p, banks):
        dve, act, pe = self.dve, self.act, self.pe
        v = self.dve.e
        bt, s_banks = banks[0], banks[1:]
        xn = self.XN.rearrange("p a b -> p (a b)")
        QT, KT = (xn[:, i * 1024:(i + 1) * 1024].rearrange("p (h k) -> p h k", h=4) for i in range(2))
        IQT, IKT, SB, PT = self.mem(4, S), self.mem(S), self.mem(8, S), self.mem(16 * P)
        score, M2, SC = self.mem(S), self.mem(S), self.SM[:, 128:384]
        tmp = SB.rearrange("p a b -> p (a b)")
        IK2 = self.SM[:, 384:512]
        sm = self.SM[:, 0:16]
        cos, sin = (self.c(n).rearrange("p (t d) -> p t d", t=NT) for n in ("cos2", "sin2"))
        tq = []
        h8 = lambda x: x.rearrange("p (h d) -> p h d", h=8)
        for t in range(NT):
            t1 = self.rope(h8(col(t, "iq")), 8, 32, cos[:, t, :], sin[:, t, :], tmp, [self.last_v, t_p])
            self.last_v = t1
            yield 2
            tq.append(self.turn_plain(IQT[:, :, t * P:(t + 1) * P], col(t, "iq"), 4, s_banks[0], t1, free=tq[-1:]))
            ik = col(t, "ik", 64)
            t1 = self.rope(ik.unsqueeze(1), 1, 32, cos[:, t, :], sin[:, t, :], tmp, [self.last_v])
            self.last_v = t1
            for c in range(2):
                t1 = self.V(v.tensor_copy, IK2[:, c * 64:(c + 1) * 64], ik, after=tq)
            yield 1.5
            tq.append(self.turn_plain(IKT[:, t * P:(t + 1) * P].unsqueeze(1), IK2, 1, s_banks[1], t1))
        for t in range(NT):
            x = col(t, "q", 1024)
            t1 = yield from self.head_norm(x, 16, HD, tmp[:, 0:1024], sm, [self.last_v, t_rows],
                                           rows[:, Q_GQ:Q_GQ + 1024])
            t1 = self.rope(x.rearrange("p (h d) -> p h d", h=16), 16, 32, cos[:, t, :], sin[:, t, :], tmp,
                           [t1, self.last_v])
            self.last_v = t1
            yield 6
            for name, dst, b in (("q", QT, s_banks[2]), ("k", KT, s_banks[3])):
                tq.append(self.turn_plain(dst[:, :, t * P:(t + 1) * P], col(t, name), 4, b, t1, free=tq[-2:]))
            yield 1
        free = None
        last = t1

        def scores(A, B):
            pe.wait(tq, free, last)
            for h in range(8):
                bk, slot, po = s_banks[2 * (h // 4) + h % 2], (h // 2) % 2, HD * (h % 2)
                ins = pe.e.matmul(self.bank(bk)[:, slot * S:slot * S + nk], A[po:po + HD, h // 2, qs],
                                  B(h)[po:po + HD, 0:nk], start=True, stop=True, skip_group_check=True)
            return pe.done(ins)

        for qt in range(NT):
            nk = P * (qt + 1)
            qs = slice(qt * P, (qt + 1) * P)
            tp = scores(IQT, lambda h: IKT)
            yield 2
            act.wait(free, last)
            for n, bk in enumerate(s_banks):
                h0 = 4 * (n // 2) + n % 2
                t1 = self.A(SB[:, h0:h0 + 3:2, 0:nk], self.bank(bk).rearrange("p (s k) -> p s k", s=2)[:, :, 0:nk],
                            ACT.Relu, after=[tp], scale=HD ** -0.5)
            iw = col(qt, "iw", 8)
            sc = score[:, 0:nk]
            self.V(v.tensor_scalar, sc, SB[:, 0, 0:nk], iw[:, 0:1], None, ALU.mult, after=[t1])
            for h in range(1, 8):
                self.V(v.scalar_tensor_tensor, sc, SB[:, h, 0:nk], iw[:, h:h + 1], sc, ALU.mult, ALU.add)
            yield 4
            self.V(v.tensor_scalar, sc, sc, 8 ** -0.5, None, ALU.mult)
            self.V(v.tensor_tensor, sc[:, nk - P:nk], sc[:, nk - P:nk], self.c("causal"), ALU.add)
            top8 = self.SM[:, 104:112]
            work = [sc, SC[:, 0:nk]]
            for n in range(8):
                self.V(v.max, top8, work[n % 2])
                self.V(v.match_replace, work[1 - n % 2], top8, work[n % 2], TAKEN)
                yield 1
            m2 = M2[:, 0:nk]
            self.V(v.tensor_scalar, m2, sc, -2e38, NEG, ALU.is_gt, ALU.mult)
            t_m = self.V(v.tensor_tensor, m2[:, nk - P:nk], m2[:, nk - P:nk], self.c("causal"), ALU.add)
            last = t1
            tp = scores(QT, lambda h: KT[:, h // 2, :])
            yield 2
            for n, bk in enumerate(s_banks):
                h0 = 4 * (n // 2) + n % 2
                t1 = self.V(v.scalar_tensor_tensor, SB[:, h0:h0 + 3:2, 0:nk],
                            self.bank(bk).rearrange("p (s k) -> p s k", s=2)[:, :, 0:nk], HD ** -0.5,
                            m2.unsqueeze(1).to_broadcast([P, 2, nk]), ALU.mult, ALU.add, after=[tp, t_m])
            yield 2
            res = []
            yield from self.softmax_pv(8, HD, SB[:, :, 0:nk], nk, lambda h, k: col(k, "v")[:, h * HD:(h + 1) * HD],
                                       col(qt, "q"), PT, t1, [free, t1], [bt, *s_banks[1:]], s_banks[0], res)
            last, free = res

    def build(self):
        nc, a = self.nc, self.a
        self.POS = nc.alloc_sbuf_tensor("positions", [P, NT], I32)[:, :]
        nc.gpsimd.dma_start(self.X[:, :, :], a["x"].rearrange("(t p) d -> p t d", p=P)).then_inc(self.s_start, 16)
        nc.gpsimd.dma_start(self.C[:, :], a["consts"]).then_inc(self.s_start, 16)
        nc.gpsimd.dma_start(self.POS, a["pos"]).then_inc(self.s_start, 16)
        self.start = Token(self.s_start, 48)
        self.done_units = 0
        nc.tensor.sem_inc(self.s_mm, RING)
        nc.vector.sem_inc(self.s_lo, RING)
        nc.vector.memset(self.zero[:, :], 0.0)
        nc.vector.memset(self.minus_half[:, :], -0.5)
        z = nc.vector.memset(self.SM[:, :], 0.0)
        z.then_inc(self.s_set, 1)
        for e in self.engines:
            e.e.wait_ge(self.s_start, 48)
            e.e.wait_ge(self.s_set, 1)
        with nc.Fori(0, STREAM // RING, engines=(nc.sync.engine,)) as i:
            for u in range(RING):
                nc.sync.wait_ge(self.s_lo, i * RING + (u + 1))
                nc.sync.dma_start(self.raw[u][:, :, :],
                                  a["stream"][bass.ds(i * RING + u, 1)].rearrange("a p (k n) -> p (a k) n", k=2)
                                  ).then_inc(self.s_load[u], 16)
        self.unit = -AHEAD
        self.scope, self.scope_use = 0, 0
        for _ in range(AHEAD):
            self.split_next()
            self.unit += 1
        self.block1()
        self.block2()
        nc.sync.wait_ge(self.s_load[RING - 1], 16 * (STREAM // RING))
        nc.vector.drain().then_inc(self.s_out, 1)
        nc.scalar.wait_ge(self.s_out, 1)
        nc.scalar.dma_start(a["out"].rearrange("(t p) d -> p t d", p=P), self.X[:, :, :]).then_inc(self.s_out, 16)
        nc.scalar.wait_ge(self.s_out, 17)


def two_pi_parts():
    rest, parts = 2 * np.pi, []
    for bits in (2.0 ** 6, 2.0 ** 17):
        parts.append(float(np.floor(rest * bits) / bits))
        rest -= parts[-1]
    return parts + [float(np.float32(rest))]


TWO_PI = two_pi_parts()
PI_IN = float(np.nextafter(np.float32(np.pi), np.float32(0)))


def units(w, cols=None):
    k, n = w.shape
    pad = -n % 512
    if pad:
        w = np.concatenate([w, np.zeros((k, pad), w.dtype)], 1)
    return w.reshape(k // 256, 2, P, (n + pad) // 512, 512).transpose(3, 0, 2, 1, 4).reshape(-1, P, 1024)


def ffn_units(w_in, w_out):
    both = np.stack([w_in[:, :FFN].reshape(D, NJ, 256), w_in[:, FFN:].reshape(D, NJ, 256)], 2)
    both = both.reshape(4, 2, P, NJ, 512).transpose(3, 0, 2, 1, 4).reshape(NJ, 4, P, 1024)
    out = w_out.reshape(NJ, 2, P, 2, 512).transpose(0, 3, 2, 1, 4).reshape(NJ, 2, P, 1024)
    seq = [both[0]]
    for j in range(1, NJ):
        seq += [both[j], out[j - 1]]
    return np.concatenate(seq + [out[NJ - 1]])


def kernel(**inputs):
    import concourse.bacc as bacc
    from concourse.bass_utils import run_bass_kernel_spmd as run

    n = {k: np.asarray(v) for k, v in inputs.items()}
    seq, pv1, rows1, lora, pv2, rows2, poolw = [], [], [], [], [], [], []
    for l in range(DEPTH):
        w = n["mix_w_in"][l]
        f0, m0, r0 = 0, 772, 1540
        w = np.concatenate([w[:, r0:], w[:, 0:256], w[:, m0:m0 + 256], w[:, 256:512], w[:, m0 + 256:m0 + 512],
                            w[:, 512:768], w[:, m0 + 512:m0 + 768], w[:, 768:772]], 1)
        w_o = n["mix_w_out"][l]
        w_o = units(np.concatenate([w_o[:256], w_o[768:], w_o[256:768]]))
        seq += [ffn_units(n["ffn1_w_in"][l], n["ffn1_w_out"][l]), units(w), units(n["xattn_w_kv"][l]),
                w_o[[0, 1, 4, 5, 2, 3, 6, 7]], units(n["xattn_w_q"][l]), units(n["xattn_w_out"][l]),
                ffn_units(n["ffn2_w_in"][l], n["ffn2_w_out"][l])]
        pv1.append(np.concatenate([n[k][l].reshape(8, P).T for k in
                                   ("ffn1_norm", "mix_norm", "xattn_norm", "xattn_mem_norm", "ffn2_norm")]
                                  + [n[k][l].reshape(P, 1) for k in ("xattn_q_gain", "xattn_k_gain")], 1))
        four = lambda g: [n[g][l]] * 4
        rows1.append(np.concatenate([n["rwkv_mu"][l], n["rwkv_w0"][l], n["rwkv_a0"][l], n["rwkv_k_k"][l],
                                     n["rwkv_k_a"][l], n["rwkv_r_k"][l].reshape(-1), n["rwkv_ln_w"][l],
                                     n["rwkv_ln_b"][l], *four("fox_q_gain"), *four("moba_q_gain"),
                                     *four("fox_k_gain"), *four("moba_k_gain"), n["fox_f_bias"][l]])[None])
        g2 = n["rwkv_g2"][l]
        lora.append(np.stack([np.concatenate([n["rwkv_w2"][l], n["rwkv_a2"][l]]), g2[:P],
                              np.concatenate([g2[P:], np.zeros((P - 32, 512), g2.dtype)])]))
    for l in range(DEPTH):
        w = n["w_in_2"][l]
        q0, i0, p0, c0 = 2048, 4608, 4680, 0
        rest = np.concatenate([w[:, p0:p0 + 1024], w[:, c0:q0], w[:, q0 + 1536:q0 + 2048], w[:, p0 + 1024:]], 1)
        seq += [units(np.concatenate([w[:, q0:q0 + 1536], w[:, i0 - 512:i0]], 1)), units(w[:, i0:p0]), units(rest),
                units(n["w_out_conv_2"][l]), units(n["w_out_pool_2"][l]), units(n["w_out_attn_2"][l]),
                units(n["w_o_2"][l])]
        pv2.append(np.concatenate([n["norm_g_2"][l].reshape(8, P).T,
                                   n["conv_w_2"][l].reshape(3, 4, P).transpose(2, 1, 0).reshape(P, 12)], 1))
        rows2.append(np.concatenate([np.tile(n["q_norm_g_2"][l], 8), np.tile(n["k_norm_g_2"][l], 8),
                                     n["pool_scale_2"][l]])[None])
        poolw.append(n["pool_w_2"][l])
    stream = np.concatenate(seq + [np.zeros((RING, P, 1024), np.float32)])
    assert stream.shape[0] == STREAM, (stream.shape, STREAM)
    arrays = {"stream": stream, "pv1": np.stack(pv1), "rows1": np.stack(rows1), "lora": np.stack(lora),
              "pv2": np.stack(pv2), "rows2": np.stack(rows2), "poolw": np.stack(poolw),
              "consts": np.concatenate([v for k, v in CONST.items() if k != "band"], 1), "band": CONST["band"],
              "x": n["x"][0], "mem": n["mem"][0], "pos": n["positions"].reshape(NT, P).T}
    arrays = {k: np.ascontiguousarray(v) for k, v in arrays.items()}
    nc = bacc.Bacc("TRN2", target_bir_lowering=False, num_devices=1)
    aps = {k: nc.dram_tensor(k, list(v.shape), I32 if k == "pos" else F32, kind="ExternalInput").ap()
           for k, v in arrays.items()}
    aps["out"] = nc.dram_tensor("out", [S, D], F32, kind="ExternalOutput").ap()
    Program(nc, aps).build()
    r = run(nc, [arrays], core_ids=[0])
    return r.results[0]["out"].reshape(1, S, D)
```

```python
import numpy as np

import concourse.bass as bass
from concourse import mybir

F32 = mybir.dt.float32
F32R = mybir.dt.float32r
BF16 = mybir.dt.bfloat16
I32 = mybir.dt.int32
ACT = mybir.ActivationFunctionType
ALU = mybir.AluOpType
AX = mybir.AxisListType.X

P = 128
S = 256
NT = S // P
D = 1024
DEPTH = 2
FFN = 2816
NJ = FFN // 256
RW = 512
ZR = 1824
HD = 64
RING = 4
AHEAD = 3
UNITS_FFN = 6 * NJ
ZG = 7
UNITS1 = 2 * UNITS_FFN + 4 * ZG + 8 + 8 + 4 + 4
PG = 18
UNITS2 = 4 * PG + 3 * 4 + 8
UNITS = DEPTH * (UNITS1 + UNITS2)
STREAM = UNITS + RING
assert UNITS1 % RING == 0 and UNITS2 % RING == 0
EPS = 1e-6
GN_EPS = 64e-5
NEG = -1e30
TAKEN = -3e38

ZQ, ZK, ZV, ZF, ZN = ZR, ZR + 512, ZR + 1024, ZR + 1536, ZR + 1540
PC = {n: 512 * i for i, n in enumerate(["q", "k", "v", "iq", "ik"])}
PC["iw"] = PC["ik"] + 64
P2 = PC["iw"] + 8
PC.update({n: P2 + 512 * i for i, n in enumerate(["pu", "pg", "cb", "cc", "cx", "cg", "ag", "mg"])})
PN = PC["mg"] + 3 * D

RWKV_WORDS = 2560 + 3 * 512 + 2048 + 2 * 512
PV_FFN1, PV_MIX, PV_X, PV_MEM, PV_FFN2, PV_XQ, PV_XK, PV_N = 0, 8, 16, 24, 32, 40, 41, 42
R_MU = 0
R_W0, R_A0, R_KK, R_KA, R_RK, R_LW, R_LB, R_GQ, R_GK = (ZR + 512 * i for i in range(9))
R_FB = ZR + 512 * 9
R_N = R_FB + 4
PW_NORM, PW_CONV, PW_N = 0, 8, 20
Q_GQ, Q_GK, Q_PS, Q_N = 0, 512, 1024, 1536


def constants():
    s = np.arange(P)[:, None]
    t = np.arange(P)[None, :]
    same = (s // 64) == (t // 64)
    c = {}
    c["ident"] = (s == t)
    c["cum64"] = (s <= t) & same
    c["ones64"] = np.concatenate([(s // 64 == 0), (s // 64 == 1)], 1)
    c["cum"] = np.concatenate([(s + P * k) <= np.arange(S)[None, :] for k in range(NT)], 1)
    i, j = s % 64, np.arange(64)[None, :]
    c["ident64"] = i == j
    c["mask4"] = np.concatenate([i < j, i <= j, i < j, i <= j], 1)
    for lv in range(6):
        b = 1 << lv
        c[f"low{lv}"] = ((i // (2 * b)) == (j // (2 * b))) & ((i // b) % 2 == 1) & ((j // b) % 2 == 0)
    c["lowT0"] = ((i // 2) == (j // 2)) & (i % 2 == 0) & (j % 2 == 1)
    c["bd"] = (s // 64 == t // 64)
    c["causal"] = np.where(t <= s, 0.0, NEG)
    band = np.zeros((4, S, S))
    for g, w in enumerate((2, 4, 8, 16)):
        for q in range(S):
            lo = max(0, q - w + 1)
            band[g, lo:q + 1, q] = 1.0 / min(q + 1, w)
        band[g] -= np.eye(S)
    c["band"] = band.reshape(4, NT, P, S).transpose(2, 0, 1, 3).reshape(P, -1)
    inv = (500000.0 ** (-np.arange(0, 16, 2) / 16.0)).astype(np.float32)
    c["inv"] = np.repeat(inv[None, :], P, 0)
    inv2 = np.float32(1.0) / (10000.0 ** (np.arange(0, 64, 2) / 64.0)).astype(np.float32)
    ang = (np.arange(S, dtype=np.float32)[:, None] * inv2[None, :]).astype(np.float32).astype(np.float64)
    for n, f in (("cos2", np.cos), ("sin2", np.sin)):
        c[n] = f(ang).reshape(NT, P, 32).transpose(1, 0, 2).reshape(P, -1)
    return {k: np.ascontiguousarray(v, dtype=np.float32) for k, v in c.items()}


CONST = constants()
BAND_N = 4 * NT * S
COFF, _o = {}, 0
for _k, _v in CONST.items():
    if _k != "band":
        COFF[_k] = (_o, _v.shape[1])
        _o += _v.shape[1]
CN = _o


class Token:

    def __init__(self, sem, val):
        self.sem, self.val = sem, val


class Engine:

    def __init__(self, nc, eng, name):
        self.e, self.sem, self.n, self.seen = eng, nc.alloc_semaphore(f"done_{name}"), 0, {}
        self.name = name

    def wait(self, *toks):
        for t in toks:
            if t is None:
                continue
            if isinstance(t, (list, tuple)):
                self.wait(*t)
            elif not isinstance(t.val, int):
                self.e.wait_ge(t.sem, t.val)
            elif self.seen.get(id(t.sem), 0) < t.val:
                self.seen[id(t.sem)] = t.val
                self.e.wait_ge(t.sem, t.val)

    def done(self, ins):
        self.n += 1
        ins.then_inc(self.sem, 1)
        return Token(self.sem, self.n)


class Program:
    def __init__(self, nc, a):
        self.nc, self.a = nc, a
        self.pe, self.act = Engine(nc, nc.tensor, "pe"), Engine(nc, nc.scalar, "act")
        self.dve, self.pool = Engine(nc, nc.vector, "dve"), Engine(nc, nc.gpsimd, "pool")
        self.engines = [self.pe, self.act, self.dve, self.pool]
        self.compute = tuple(e.e.engine for e in self.engines)
        self.last_v = None
        self.rs, self.t_rs = {}, {}
        self.ev = {n: nc.alloc_semaphore(n) for n in
                   ("silu", "h_ready", "h_turned", "ht_hi", "ht_lo", "z_act", "z_dve")}
        self.dma = {n: nc.alloc_semaphore(n) for n in ("d_par", "d_rows", "d_lora", "d_mem", "d_shift1",
                                                       "d_shift1_row", "d_shift0")}
        self.dma_base = {n: 0 for n in self.dma}
        sb = nc.alloc_sbuf_tensor
        self.raw = [sb(f"raw{i}", [P, 2, 512], F32) for i in range(RING)]
        self.whi = [sb(f"whi{i}", [P, 2, 512], F32R) for i in range(RING)]
        self.wlo = [sb(f"wlo{i}", [P, 2, 512], F32R) for i in range(RING)]
        self.s_load = [nc.alloc_semaphore(f"loaded{i}") for i in range(RING)]
        self.s_hi, self.s_lo, self.s_mm = (nc.alloc_semaphore(n) for n in ("split_hi", "split_lo", "unit_used"))
        self.X = sb("x_res", [P, NT, D], F32)
        self.AHI, self.ALO = sb("a_hi", [P, 8, S], F32R), sb("a_lo", [P, 8, S], F32R)
        self.HHI, self.HLO = sb("h_hi", [P, 2, S], F32R), sb("h_lo", [P, 2, S], F32R)
        self.zero = sb("zero", [P, 512], BF16)
        self.minus_half = sb("minus_half", [P, 16], F32)
        self.C = sb("const_tables", [P, CN], F32)
        self.SM = sb("small", [P, 512], F32)
        self.arena_n = (212863 - 48 * 1024 - 8192 - 16384 - 4096 - 1024 - CN * 4 - 2048 - 1056) // 4 // 8 * 8
        self.arena = sb("arena", [P, self.arena_n], F32)
        self.top = 0
        self.PS = nc.alloc_psum_tensor("ps", [P, 8 * 512], F32)
        self.s_start = nc.alloc_semaphore("loaded_start")
        self.s_tables = nc.alloc_semaphore("loaded_tables")
        self.s_set = nc.alloc_semaphore("constants_set")
        self.s_out = nc.alloc_semaphore("stored")
        self.unit = 0
        self.scope = 0

    def V(self, method, *args, after=(), **kw):
        self.dve.wait(self.last_v, *after)
        self.last_v = self.dve.done(method(*args, **kw))
        return self.last_v

    def A(self, out, in_, func, after=(), **kw):
        self.act.wait(*after)
        return self.act.done(self.act.e.activation(out, in_, func, **kw))

    def bank(self, b, n=512, nb=1):
        return self.PS[:, b * 512:b * 512 + (n if nb == 1 else nb * 512)]

    def mem(self, *shape):
        n = int(np.prod(shape))
        v = self.arena[:, self.top:self.top + n]
        self.top += n
        assert self.top <= self.arena_n, (self.top, self.arena_n)
        if len(shape) == 1:
            return v
        names = "abcd"[:len(shape)]
        return v.rearrange(f"p ({' '.join(names)}) -> p {' '.join(names)}", **dict(zip(names, shape)))

    def c(self, name):
        o, n = COFF[name]
        return self.C[:, o:o + n]

    def event(self, name, val):
        return Token(self.ev[name], val)

    def split_next(self):
        m = self.unit + AHEAD
        i = m % RING
        n = self.scope + m
        use = self.scope_use + m // RING
        self.act.e.wait_ge(self.s_load[i], use * 16 + 16)
        self.act.e.wait_ge(self.s_mm, n + 1)
        self.act.e.activation(self.whi[i][:, :, :], self.raw[i][:, :, :], ACT.Copy).then_inc(self.s_hi, 1)
        self.dve.e.wait_ge(self.s_hi, n + 1)
        self.dve.e.tensor_tensor(self.wlo[i][:, :, :], self.raw[i][:, :, :], self.whi[i][:, :, :].bitcast(F32),
                                 ALU.subtract).then_inc(self.s_lo, 1)

    def products(self, jobs, ahi, alo, after=()):
        self.split_next()
        i = self.unit % RING
        n = self.scope + self.unit
        self.pe.wait(*after)
        self.pe.e.wait_ge(self.s_lo, n + (RING + 1))
        hi, lo = self.whi[i], self.wlo[i]
        for out, kk, kt, t, start in jobs:
            w = out.shape[1]
            a_h, a_l = ahi[:, kt, t * P:(t + 1) * P], alo[:, kt, t * P:(t + 1) * P]
            mm = self.pe.e.matmul
            mm(out, a_h, hi[:, kk, 0:w], start=start, stop=False, skip_group_check=True)
            mm(out, a_h, lo[:, kk, 0:w], start=False, stop=False, skip_group_check=True)
            last = mm(out, a_l, hi[:, kk, 0:w], start=False, stop=True, skip_group_check=True)
        last.then_inc(self.s_mm, 1)
        self.unit += 1
        return Token(self.s_mm, n + (RING + 1))

    def gemm(self, *args, **kw):
        return self.drain(self.gemm_steps(*args, **kw))

    def drain(self, steps):
        while True:
            try:
                next(steps)
            except StopIteration as end:
                return end.value

    def gemm_steps(self, banks, nk, kt0=0, width=512, toks=None, after=(), first=True):
        for u in range(nk // 2):
            need = [toks[kt0 + 2 * u + 1]] if toks else []
            jobs = [(self.bank(banks[t], width), kk, kt0 + 2 * u + kk, t, first and u == 0 and kk == 0)
                    for kk in range(2) for t in range(NT)]
            tok = self.products(jobs, self.AHI, self.ALO, after=[*need, *(after if u == 0 else ())])
            yield 2.6
        return tok

    def rstd(self, out, ss, n, eps, tok):
        self.dve.wait(tok)
        t = self.dve.done(self.dve.e.tensor_scalar(out, ss, 1.0 / n, eps, ALU.mult, ALU.add))
        return self.power(out, t)

    def power(self, x, tok):
        self.pool.wait(tok)
        half = self.minus_half[:, 0:x.shape[1]]
        return self.pool.done(self.pool.e.tensor_tensor(x, x, half, ALU.pow))

    def turn(self, cols, banks, gain=None, kt0=0, ready=None):
        toks, left = [None] * kt0, {}
        for k, src in enumerate(cols):
            b = banks[k % len(banks)]
            self.pe.wait(ready[k] if isinstance(ready, list) else ready, left.get(b))
            for t in range(NT):
                ins = self.pe.e.transpose(self.bank(b)[:, t * P:(t + 1) * P], src[t], self.c("ident"))
            tp = self.pe.done(ins)
            self.act.wait(tp)
            ps = self.bank(b, S)
            scale = gain[:, k:k + 1] if gain is not None else 1.0
            th = self.act.done(self.act.e.activation(self.AHI[:, kt0 + k, :], ps, ACT.Copy, scale=scale))
            self.dve.wait(th)
            if gain is None:
                ins = self.dve.e.tensor_tensor(self.ALO[:, kt0 + k, :], ps, self.AHI[:, kt0 + k, :].bitcast(F32),
                                               ALU.subtract)
            else:
                ins = self.dve.e.scalar_tensor_tensor(self.ALO[:, kt0 + k, :], ps, scale,
                                                      self.AHI[:, kt0 + k, :].bitcast(F32), ALU.mult, ALU.subtract)
            left[b] = self.dve.done(ins)
            toks.append(left[b])
        return toks

    def norm_turn(self, src, gain, banks, halves, slot=0, junk=None):
        toks = self.turn([[src[:, t, k * P:(k + 1) * P] for t in range(NT)] for k in range(8)], banks, gain,
                         ready=[halves[k // 4] for k in range(8)])
        rs, ss = (self.SM[:, o:o + NT] for o in (72 + 4 * slot, 74 + 4 * slot))
        ta = None
        for t in range(NT):
            out = self.XN[:, t, :] if junk is None else junk
            ta = self.A(out, src[:, t, :], ACT.Square, after=[*halves, ta], accum_out=ss[:, t:t + 1])
        self.rs[slot] = [rs[:, t:t + 1] for t in range(NT)]
        self.t_rs[slot] = self.rstd(rs, ss, D, EPS, ta)
        return toks

    def add_half(self, h, banks, scale, tok):
        self.dve.wait(tok)
        for t in range(NT):
            x = self.X[:, t, h * 512:(h + 1) * 512]
            ins = self.dve.e.scalar_tensor_tensor(x, self.bank(banks[t]), scale, x, ALU.mult, ALU.add)
        return self.dve.done(ins)

    def project(self, nk, toks, after=()):
        halves = []
        for h in range(2):
            tok = self.gemm([2 * h, 2 * h + 1], nk, toks=toks, after=after)
            halves.append(self.add_half(h, [2 * h, 2 * h + 1], 1.0, tok))
        return halves

    def ffn_in(self, j, toks=None):
        after = [] if toks else [self.event("h_ready", 2 * j)]
        for u in range(4):
            need = [toks[2 * u + 1]] if toks else []
            jobs = [(self.bank(4 + t), kk, 2 * u + kk, t, u == 0 and kk == 0) for kk in range(2) for t in range(NT)]
            tok = self.products(jobs, self.AHI, self.ALO, after=[*need, *(after if u == 0 else ())])
        if toks:
            self.act.wait(self.t_rs[0])
            self.dve.wait(self.t_rs[0])
        for t in range(NT):
            self.act.wait(tok)
            self.act.e.activation(self.SG[:, t, :], self.bank(4 + t, 256), ACT.Silu,
                                  scale=self.rs[0][t]).then_inc(self.ev["silu"], 1)
            self.dve.wait(self.event("silu", 2 * j + (t + 1)))
            self.dve.e.scalar_tensor_tensor(self.H[:, t, :], self.bank(4 + t)[:, 256:512], self.rs[0][t],
                                            self.SG[:, t, :], ALU.mult, ALU.mult).then_inc(self.ev["h_ready"], 1)

    def ffn_turn(self, j, first=False):
        self.pe.wait(self.event("h_ready", 2 * j + 2))
        if not first:
            self.pe.wait(self.event("ht_lo", 2 * j))
        for kk in range(2):
            for t in range(NT):
                ins = self.pe.e.transpose(self.bank(6 + kk)[:, t * P:(t + 1) * P],
                                          self.H[:, t, kk * P:(kk + 1) * P], self.c("ident"))
            ins.then_inc(self.ev["h_turned"], 1)
        for kk in range(2):
            self.act.wait(self.event("h_turned", 2 * j + (kk + 1)))
            self.act.e.activation(self.HHI[:, kk, :], self.bank(6 + kk, S), ACT.Copy).then_inc(self.ev["ht_hi"], 1)
            self.dve.wait(self.event("ht_hi", 2 * j + (kk + 1)))
            self.dve.e.tensor_tensor(self.HLO[:, kk, :], self.bank(6 + kk, S), self.HHI[:, kk, :].bitcast(F32),
                                     ALU.subtract).then_inc(self.ev["ht_lo"], 1)

    def ffn_out(self, j):
        toks = []
        for h in range(2):
            jobs = [(self.bank(2 * t + h), kk, kk, t, False) for kk in range(2) for t in range(NT)]
            toks.append(self.products(jobs, self.HHI, self.HLO,
                                      after=[self.event("ht_lo", 2 * j + 2)] if h == 0 else ()))
        return toks

    def loop(self, count, per, body):
        for e in self.engines:
            e.seen = {}
        outer, outer_use, n0, counts = self.scope, self.scope_use, self.unit, [e.n for e in self.engines]
        assert per % RING == 0
        with self.nc.Fori(0, count, engines=self.compute) as i:
            self.scope, self.scope_use = outer + i * per, outer_use + i * (per // RING)
            body(i)
            assert self.unit == n0 + per and counts == [e.n for e in self.engines]
        self.scope, self.scope_use, self.unit = outer, outer_use, n0 + count * per
        for e in self.engines:
            e.seen = {}

    def ffn(self, gain, jb, halves):
        toks = self.norm_turn(self.X, gain, [6, 7, 0, 1, 2, 3], halves)
        self.ffn_in(jb, toks)
        self.pe.wait(toks)
        for b in range(4):
            self.pe.e.matmul(self.bank(b), self.zero[:, 0:P], self.zero[:, :], start=True, stop=False,
                             skip_group_check=True)
        self.ffn_turn(jb, first=jb == 0)

        def body(i):
            for u in range(2):
                j = i * 2 + (jb + 1 + u)
                self.ffn_in(j)
                self.ffn_out(j - 1)
                self.ffn_turn(j)

        self.loop((NJ - 1) // 2, 12, body)
        toks = self.ffn_out(jb + NJ - 1)
        return [self.add_half(h, [h, 2 + h], 0.5, toks[h]) for h in range(2)]

    def column_group(self, dst, g, col, width, banks, before, toks=(), func=None):
        tok = yield from self.gemm_steps(
            banks, 8, width=width, after=[*toks, self.event("z_act", before + 2), self.event("z_dve", before + 2)])
        cols = slice(col, col + width) if isinstance(col, int) else bass.ds(col, width)
        self.act.wait(tok)
        self.act.e.activation(dst[:, 0, cols], self.bank(banks[0], width), func or ACT.Copy,
                              scale=self.rs[0][0]).then_inc(self.ev["z_act"], 1)
        if func is None:
            self.dve.wait(tok)
            self.dve.e.tensor_scalar(dst[:, 1, cols], self.bank(banks[1], width), self.rs[0][1], None,
                                     ALU.mult).then_inc(self.ev["z_dve"], 1)
        else:
            self.act.e.activation(dst[:, 1, cols], self.bank(banks[1], width), func,
                                  scale=self.rs[0][1]).then_inc(self.ev["z_dve"], 1)
        return [self.event("z_act", g + 3), self.event("z_dve", g + 3)]

    def column_loop(self, dst, count, toks):
        for e, n in ((self.act, "z_act"), (self.dve, "z_dve")):
            e.e.sem_inc(self.ev[n], 2)
        self.pe.wait(toks)
        self.act.wait(self.t_rs[0])
        self.dve.wait(self.t_rs[0])

        def body(i):
            for u in range(2):
                g = i * 2 + u
                self.drain(self.column_group(dst, g, g * 512, 512, [2 * u, 2 * u + 1], g - 1))

        self.loop(count, 8, body)
        return [self.event("z_act", 2 * count + 2), self.event("z_dve", 2 * count + 2)]

    def weave(self, *threads, pace=(1.0, 1.0)):
        clocks = [[0.0, n, t] for n, t in enumerate(threads)]
        while clocks:
            now = min(clocks, key=lambda c: (c[0], c[1]))
            try:
                now[0] += next(now[2]) * pace[now[1]]
            except StopIteration:
                clocks.remove(now)

    def head_norm(self, x, nh, hd, tmp, sm, ready, gain=None):
        e = self.dve
        e.wait(ready)
        x3 = x.rearrange("p (h d) -> p h d", h=nh)
        t = e.done(e.e.tensor_tensor(tmp, x, x, ALU.mult))
        e.wait(t)
        t = e.done(e.e.tensor_reduce(sm, tmp.rearrange("p (h d) -> p h d", h=nh), AX, ALU.add))
        t = self.rstd(sm, sm, hd, EPS, t)
        yield 1.5 + nh * hd / 500
        e.wait(t)
        t = e.done(e.e.tensor_tensor(x3, x3, sm.unsqueeze(2).to_broadcast([P, nh, hd]), ALU.mult))
        if gain is not None:
            e.wait(t)
            t = e.done(e.e.tensor_tensor(x, x, gain, ALU.mult))
        return t

    def rope(self, x, nh, half, cos, sin, tmp, ready):
        e = self.dve
        e.wait(ready)
        x1, x2 = x[:, :, 0:half], x[:, :, half:2 * half]
        cb, sb = (a.unsqueeze(1).to_broadcast([P, nh, half]) for a in (cos, sin))
        v = tmp[:, 0:3 * nh * half].rearrange("p (a h d) -> p a h d", a=3, h=nh)
        e.e.tensor_tensor(v[:, 0], x2, sb, ALU.mult)
        e.e.tensor_tensor(v[:, 1], x1, sb, ALU.mult)
        e.e.tensor_tensor(v[:, 2], x2, cb, ALU.mult)
        t = e.done(e.e.tensor_tensor(x1, x1, cb, ALU.mult))
        e.wait(t)
        e.e.tensor_tensor(x1, x1, v[:, 0], ALU.subtract)
        return e.done(e.e.tensor_tensor(x2, v[:, 2], v[:, 1], ALU.add))

    def turn_plain(self, dst, src, n, b, ready, gain=None, free=None, on=None):
        self.pe.wait(ready, free)
        for k in range(n):
            ins = self.pe.e.transpose(self.bank(b)[:, k * P:(k + 1) * P], src[:, k * P:(k + 1) * P], self.c("ident"))
        tp = self.pe.done(ins)
        e = on or self.act
        e.wait(tp)
        v = self.bank(b, n * P).rearrange("p (k c) -> p k c", k=n)
        if e is self.act:
            return e.done(e.e.activation(dst, v, ACT.Copy, scale=gain if gain is not None else 1.0))
        if gain is not None:
            return e.done(e.e.tensor_scalar(dst, v, gain, None, ALU.mult))
        return e.done(e.e.tensor_copy(dst, v))

    def softmax_pv(self, nh, hd, SB, nk, v_of, out, PT, tok, free, banks_t, bank_o, res, small=32):
        dve, act, pe = self.dve, self.act, self.pe
        mx, sm = self.SM[:, small:small + nh], self.SM[:, small + 16:small + 16 + nh]
        dve.wait(tok)
        t = dve.done(dve.e.tensor_reduce(mx, SB, AX, ALU.max))
        dve.wait(t)
        t = dve.done(dve.e.tensor_scalar(mx, mx, -1.0, None, ALU.mult))
        act.wait(t)
        te = []
        for h in range(nh):
            te.append(act.done(act.e.activation(SB[:, h, :], SB[:, h, :], ACT.Exp, bias=mx[:, h:h + 1],
                                                accum_out=sm[:, h:h + 1])))
            yield 0.45
        dve.wait(te[-1])
        tr = dve.done(dve.e.reciprocal(sm, sm))
        nkt = nk // P
        per = 4
        todo = [(h, k) for h in range(nh) for k in range(nkt)]
        left, ready = {}, {}
        for g in range(0, len(todo), per):
            b = banks_t[(g // per) % len(banks_t)]
            part = todo[g:g + per]
            pe.wait(te[part[-1][0]], left.get(b), free)
            for n, (h, k) in enumerate(part):
                ins = pe.e.transpose(self.bank(b)[:, n * P:(n + 1) * P], SB[:, h, k * P:(k + 1) * P], self.c("ident"))
            tp = pe.done(ins)
            e = dve if (g // per) % 2 else act
            e.wait(tp)
            dst = PT[:, g * P:(g + len(part)) * P]
            if e is act:
                left[b] = act.done(act.e.activation(dst, self.bank(b, len(part) * P), ACT.Copy))
            else:
                left[b] = dve.done(dve.e.tensor_copy(dst, self.bank(b, len(part) * P)))
            for h, k in part:
                ready[h, k] = left[b]
            yield 0.8
        for h in range(nh):
            for k in range(nkt):
                pe.wait(ready[h, k])
                n = todo.index((h, k))
                ins = pe.e.matmul(self.bank(bank_o)[:, h * hd:(h + 1) * hd], PT[:, n * P:(n + 1) * P], v_of(h, k),
                                  start=(k == 0), stop=(k == nkt - 1), skip_group_check=True)
            if h < nh - 1 and h % 4 == 3:
                yield 0.8
        tp = pe.done(ins)
        dve.wait(tp, tr)
        o3 = self.bank(bank_o, nh * hd).rearrange("p (h d) -> p h d", h=nh)
        self.last_v = dve.done(dve.e.tensor_tensor(out.rearrange("p (h d) -> p h d", h=nh), o3,
                                                   sm.unsqueeze(2).to_broadcast([P, nh, hd]), ALU.mult))
        res[:] = [self.last_v, tp]
        yield 0.8



    def load(self, name, dst, src):
        assert name not in self.loaded
        self.loaded[name] = True
        self.nc.scalar.dma_start(dst, src).then_inc(self.dma[name], 16)
        return Token(self.dma[name], self.layer_no * 16 + (self.dma_base[name] + 16))

    def attention(self, par, rows, t_z, banks):
        Z = self.Z
        act, pe = self.act, self.pe
        v = self.dve.e
        even, odd, bt = banks
        QT, KT, SB, PT = self.mem(2, S), self.mem(2, S), self.mem(4, S), self.mem(8 * P)
        for t_ in range(NT):
            self.last_v = yield from self.head_norm(Z[:, t_, ZQ:ZQ + 1024], 16, HD, SB.rearrange("p h k -> p (h k)"),
                                                    self.SM[:, 112:128], [self.last_v, t_z, par],
                                                    rows[:, R_GQ:R_GQ + 1024])
            yield 2
        tmp = SB.rearrange("p h k -> p (h k)")
        LF, LN, CS, pos, aux = self.mem(NT, 4), self.mem(NT, 4), self.mem(NT, 2, 8), self.mem(NT), self.mem(80)
        f = aux[:, 0:8].rearrange("p (t h) -> p t h", t=NT)
        ab = aux[:, 8:16].rearrange("p (t h) -> p t h", t=NT)
        fb = rows[:, R_FB:R_FB + 4].unsqueeze(1).to_broadcast([P, NT, 4])
        self.V(v.tensor_tensor, f, Z[:, :, ZF:ZF + 4], fb, ALU.add, after=[t_z, par])
        t = self.V(v.scalar_tensor_tensor, ab, f, -1.0, f, ALU.mult, ALU.max)
        t = self.A(ab, ab, ACT.Exp, after=[t], scale=-1.0)
        t = self.A(ab, ab, ACT.Ln, after=[t], bias=1.0)
        yield 2
        self.V(v.scalar_tensor_tensor, LF, f, 0.0, ab, ALU.min, ALU.subtract, after=[t])
        self.V(v.tensor_scalar, LF, LF, float(HD) ** 0.5, None, ALU.mult)
        t_lf = self.V(v.tensor_scalar, LN, LF, -1.0, None, ALU.mult)
        self.V(v.tensor_copy, pos, self.POS)
        ang, n = (aux[:, o:o + 32].rearrange("p (t a d) -> p t a d", t=NT, a=2) for o in (16, 48))
        for t_ in range(NT):
            for a in range(2):
                self.V(v.tensor_scalar, ang[:, t_, a, :], self.c("inv"), pos[:, t_:t_ + 1], None, ALU.mult)
        yield 1
        to_int = float(1.5 * 2 ** 23)
        for a, quarter in ((0, 0.25), (1, 0.0)):
            self.V(v.tensor_scalar, n[:, :, a, :], ang[:, :, a, :], float(1 / (2 * np.pi)), quarter, ALU.mult, ALU.add)
        self.V(v.tensor_scalar, n, n, to_int, None, ALU.add)
        self.V(v.tensor_scalar, n, n, to_int, None, ALU.subtract)
        for part in TWO_PI:
            self.V(v.scalar_tensor_tensor, ang, n, -part, ang, ALU.mult, ALU.add)
        self.V(v.tensor_scalar, ang[:, :, 0, :], ang[:, :, 0, :], float(np.pi / 2), None, ALU.add)
        t = self.V(v.tensor_scalar, ang, ang, PI_IN, -PI_IN, ALU.min, ALU.max)
        t_cs = self.A(CS, ang, ACT.Sin, after=[t])
        yield 2
        scale = float(HD) ** -0.5
        free = None
        for fox in (True, False):
            off = 0 if fox else 256
            tq, t_r = [], self.last_v
            if not fox:
                for t_ in range(NT):
                    for src in (ZQ + off, ZK + off):
                        self.last_v = t_r = self.rope(Z[:, t_, src:src + 256].rearrange("p (h d) -> p h d", h=4), 4, 8,
                                                      CS[:, t_, 0, :], CS[:, t_, 1, :], tmp,
                                                      [self.last_v, t_cs, free])
                    yield 1.2
            for t_ in range(NT):
                for src, dst in ((ZQ, QT), (ZK, KT)):
                    b = banks[len(tq) % 2]
                    tq.append(self.turn_plain(dst[:, :, t_ * P:(t_ + 1) * P], Z[:, t_, src + off:src + off + 256], 2,
                                              b, [t_r, free], free=tq[-2:]))
                    yield 0.5
            for qt in range(NT):
                nk = P * (qt + 1)
                qs = slice(qt * P, (qt + 1) * P)
                pe.wait(tq, t_lf, free, self.last_v)
                for h in range(4):
                    hp, po = h // 2, HD * (h % 2)
                    out = self.bank((even, odd)[h % 2])[:, hp * S:hp * S + nk]
                    ins = pe.e.matmul(out, QT[po:po + HD, hp, qs], KT[po:po + HD, hp, 0:nk], start=True, stop=not fox,
                                      skip_group_check=True)
                    if fox:
                        for st in range(qt + 1):
                            cum = self.c("cum")[:, st * S:(st + 1) * S]
                            pe.e.matmul(out, cum[:, qs], LF[:, st, h:h + 1].to_broadcast([P, nk]), start=False,
                                        stop=False, skip_group_check=True)
                            ins = pe.e.matmul(out, LN[:, st, h:h + 1].to_broadcast([P, P]), cum[:, 0:nk],
                                              start=False, stop=st == qt, skip_group_check=True)
                    if h < 3:
                        yield 0.5
                tp = pe.done(ins)
                for g in range(2):
                    ps = self.bank((even, odd)[g]).rearrange("p (s k) -> p s k", s=2)
                    dst = SB[:, g::2, :]
                    mask = self.c("causal").unsqueeze(1).to_broadcast([P, 2, P])
                    t_s = self.V(v.scalar_tensor_tensor, dst[:, :, nk - P:nk], ps[:, :, nk - P:nk], scale, mask,
                                 ALU.mult, ALU.add, after=[tp, free])
                    if qt:
                        t_s = self.V(v.tensor_scalar, dst[:, :, 0:P], ps[:, :, 0:P], scale, None, ALU.mult)
                yield 1
                res = []
                yield from self.softmax_pv(4, HD, SB[:, :, 0:nk], nk,
                                           lambda h, k: Z[:, k, ZV + off + h * HD:ZV + off + (h + 1) * HD],
                                           Z[:, qt, ZQ + off:ZQ + off + 256], PT, t_s, free, [bt, odd], even, res)
                self.t_att, free = res

    def rwkv(self, par, rows, lora, t_z, banks, base):
        Z, act, pe = self.Z, self.act, self.pe
        v = self.dve.e
        B0, B1, B2, B3, B4 = banks
        side_top, self.top = self.top, base
        shared = self.mem(2560)
        ZS = shared[:, 0:ZR]
        T1, T2, T4, T5, T7 = (shared[:, i * 512:(i + 1) * 512] for i in range(5))
        L, LT = T2[:, 0:288], T4[:, 0:384].rearrange("p (k c) -> p k c", k=3)
        MK = shared[:, 0:2048].rearrange("p (h a c) -> p h a c", h=8, a=4)
        T3, T6, T8 = (self.mem(512) for _ in range(3))
        TA = self.mem(4, 4, P)
        RHS, ST = self.mem(512), self.mem(4, P)
        assert self.top == base + RWKV_WORDS
        self.top = side_top
        xn = self.XN.rearrange("p a b -> p (a b)")
        ZS2 = xn[:, 0:ZR]
        TI, TIT = (xn[:, i * 512:(i + 1) * 512].rearrange("p (h c) -> p h c", h=8) for i in range(2))
        G, GN = [T6, xn[:, 1024:1536]], xn[:, 1536:2048]
        XG = [x.rearrange("p a b -> p (a b)")[:, 0:256].rearrange("p (h c) -> p h c", h=4) for x in (self.H, self.SG)]
        U, WCM = rows[:, 0:512], rows[:, 512:1536].rearrange("p (c h d) -> p c h d", c=2, h=4)
        sm, sm3, WC, MU = self.SM[:, 0:8], self.SM[:, 16:24], self.SM[:, 24:32], self.SM[:, 64:72]
        bonus = [self.SM[:, 8:16], self.SM[:, 56:64]]
        act.wait(t_z)
        shifted = [self.load("d_shift1", ZS2[1:P, :], Z[0:P - 1, 1, 0:ZR]),
                   self.load("d_shift1_row", ZS2[0:1, :], Z[P - 1:P, 0, 0:ZR])]
        t = self.V(v.memset, ZS[0:1, :], 0.0, after=[t_z])
        act.wait(t)
        shifted.append(self.load("d_shift0", ZS[1:P, :], Z[0:P - 1, 0, 0:ZR]))
        mu = rows[:, R_MU:R_MU + ZR]
        yield 8
        pool = self.pool
        pool.wait(*shifted, par, t_z)
        t_shift = None
        for out, a, b, op in ((ZS2, ZS2, Z[:, 1, 0:ZR], ALU.subtract), (ZS2, ZS2, mu, ALU.mult),
                              (Z[:, 1, 0:ZR], Z[:, 1, 0:ZR], ZS2, ALU.add)):
            pool.wait(t_shift)
            t_shift = pool.done(pool.e.tensor_tensor(out, a, b, op))
        zt = Z[:, 0, 0:ZR]
        self.V(v.tensor_tensor, ZS, ZS, zt, ALU.subtract, after=[*shifted, par])
        self.V(v.tensor_tensor, ZS, ZS, mu, ALU.mult)
        self.V(v.tensor_tensor, zt, zt, ZS, ALU.add)
        yield 6
        self.V(v.memset, ST, 0.0)
        later, t_y = iter(()), None
        decay = -float(np.exp(-0.5))
        h3 = lambda x: x.rearrange("p (h d) -> p h d", h=8)
        bc = lambda s: s.unsqueeze(2).to_broadcast([P, 8, HD])
        for t_ in range(NT):
            r, k, val = (Z[:, t_, i * 512:(i + 1) * 512] for i in range(3))
            zl = Z[:, t_, 3 * 512:ZR]
            t0 = [self.last_v, t_shift if t_ else None]
            self.A(L[:, 0:64], zl[:, 0:64], ACT.Tanh, after=t0)
            self.A(L[:, 64:128], zl[:, 64:128], ACT.Copy)
            ta = self.A(L[:, 128:288], zl[:, 128:288], ACT.Sigmoid)
            yield 1.5
            pe.wait(ta, t0)
            for i, w in enumerate((128, 128, 32)):
                ins = pe.e.transpose(self.bank(B0)[0:w, i * P:(i + 1) * P], L[:, i * P:i * P + w], self.c("ident"))
            tp = pe.done(ins)
            self.A(LT[:, 0:2, :], self.bank(B0, 256).rearrange("p (k c) -> p k c", k=2), ACT.Copy, after=[tp])
            ta = self.A(LT[0:32, 2, :], self.bank(B0)[0:32, 256:384], ACT.Copy)
            yield 2.5
            pe.wait(ta, lora)
            W = self.LORA
            pe.e.matmul(self.bank(B1), LT[0:64, 0, :], W[0:64, 0, :], start=True, stop=True)
            pe.e.matmul(self.bank(B2), LT[64:128, 0, :], W[64:128, 0, :], start=True, stop=True)
            pe.e.matmul(self.bank(B3), LT[:, 1, :], W[:, 1, :], start=True, stop=False)
            tp = pe.done(pe.e.matmul(self.bank(B3), LT[0:32, 2, :], W[0:32, 2, :], start=False, stop=True))
            yield 3.5
            self.V(v.tensor_tensor, T1, self.bank(B1), rows[:, R_W0:R_W0 + 512], ALU.add, after=[tp])
            t = self.V(v.tensor_tensor, T5, self.bank(B2), rows[:, R_A0:R_A0 + 512], ALU.add)
            self.A(T1, T1, ACT.Sigmoid, after=[t])
            t_a = self.A(T5, T5, ACT.Sigmoid)
            t_g = self.A(G[t_], self.bank(B3), ACT.Copy)
            yield 2.5
            t_ld = self.V(v.tensor_scalar, T1, T1, decay, None, ALU.mult, after=[t_a])
            yield 1
            pe.wait(t_ld)
            tp = pe.done(pe.e.matmul(self.bank(B1), self.c("cum64"), T1, start=True, stop=True))
            for hp in range(4):
                ins = pe.e.matmul(self.bank(B2)[:, 2 * hp:2 * hp + 2], T1[:, hp * P:(hp + 1) * P], self.c("ones64"),
                                  start=True, stop=True, skip_group_check=True)
            tw = pe.done(ins)
            t_cx = self.V(v.tensor_tensor, T4, self.bank(B1), T1, ALU.subtract, after=[tp])
            self.A(T2, self.bank(B1), ACT.Exp, after=[tp, t_cx])
            self.A(T3, self.bank(B1), ACT.Exp, scale=-1.0)
            self.A(T4, T4, ACT.Exp)
            t_e = self.A(WC, self.bank(B2, 8), ACT.Exp, after=[tw])
            yield 2
            self.V(v.tensor_tensor, T7, k, rows[:, R_KK:R_KK + 512], ALU.mult, after=t0)
            self.V(v.tensor_tensor, T8, T7, T7, ALU.mult)
            self.V(v.tensor_reduce, sm, h3(T8), AX, ALU.add)
            t = self.V(v.tensor_scalar, sm, sm, 1e-24, None, ALU.max)
            t = self.power(sm, t)
            self.V(v.tensor_tensor, h3(T7), h3(T7), bc(sm), ALU.mult, after=[t])
            self.V(v.scalar_tensor_tensor, T8, T5, -1.0, rows[:, R_KA:R_KA + 512], ALU.add, ALU.mult)
            self.V(v.scalar_tensor_tensor, k, T8, 1.0, k, ALU.add, ALU.mult)
            yield 6
            self.V(v.tensor_tensor, T2, r, T2, ALU.mult, after=[t_e])
            t_at = self.V(v.scalar_tensor_tensor, T4, T7, -1.0, T4, ALU.mult, ALU.mult)
            self.V(v.tensor_tensor, T8, k, T3, ALU.mult)
            self.V(v.tensor_tensor, T7, T7, T5, ALU.mult)
            t_bt = self.V(v.tensor_tensor, T3, T7, T3, ALU.mult)
            for c in range(2):
                wc = WC.rearrange("p (h c) -> p c h", c=2)[:, c, :].unsqueeze(2).to_broadcast([P, 4, P])
                pool.wait(t_e)
                t_wcm = pool.done(pool.e.tensor_tensor(WCM[:, c], wc, self.c("bd").unsqueeze(1).to_broadcast(
                    [P, 4, P]), ALU.mult))
            yield 4.5
            tt = [self.turn_plain(TA[:, i], src, 4, b, t_bt, free=[t_g, t_e, t_cx, t_y])
                  for i, (src, b) in enumerate(((T4, B0), (T2, B4), (T3, B3), (T8, B1)))]
            self.V(v.tensor_tensor, GN, r, k, ALU.mult, after=[t_shift])
            self.V(v.tensor_tensor, GN, GN, rows[:, R_RK:R_RK + 512], ALU.mult)
            t_bonus = self.V(v.tensor_reduce, bonus[t_], h3(GN), AX, ALU.add)
            yield 2.5
            chunks = [slice(0, HD), slice(HD, P)]
            t_mk = []
            for n, h0 in enumerate((0, 1, 4, 5)):
                po = HD * (h0 % 2)
                pe.wait(tt)
                for i in range(2):
                    hp = h0 // 2 + i
                    for co in chunks:
                        for a in range(2):
                            out = self.bank(banks[n])[co, i * 256 + a * P:i * 256 + (a + 1) * P]
                            ins = pe.e.matmul(out, TA[po:po + HD, 2 + a, hp, co], TA[po:po + HD, 0:2, hp, co],
                                              start=True, stop=True, skip_group_check=True)
                tp = pe.done(ins)
                mask = self.c("mask4").unsqueeze(1).to_broadcast([P, 2, 256])
                t_mk.append(self.V(v.tensor_tensor, MK[:, h0:h0 + 3:2].rearrange("p h a c -> p h (a c)"),
                                   self.bank(banks[n]).rearrange("p (h x) -> p h x", h=2), mask, ALU.mult,
                                   after=[tp]))
                yield 1.8
            b4 = lambda n: self.c(n).unsqueeze(1).to_broadcast([P, 4, HD])
            p4 = lambda b: self.bank(b, 4 * HD).rearrange("p (h c) -> p h c", h=4)
            for g in range(2):
                nb = (B4, B0)[g]
                pe.wait(t_mk)
                for i in range(4):
                    for co in chunks:
                        ins = pe.e.matmul(p4(nb)[co, i, :], TA[HD * g:HD * (g + 1), 0, i, co],
                                          TA[HD * g:HD * (g + 1), 2, i, co], start=True, stop=True,
                                          skip_group_check=True)
                tp = pe.done(ins)
                self.V(v.tensor_tensor, TIT[:, g::2, :], MK[:, g::2, 0, :], b4("lowT0"), ALU.mult)
                self.V(v.tensor_tensor, TIT[:, g::2, :], TIT[:, g::2, :], b4("ident64"), ALU.add)
                self.V(v.tensor_tensor, TI[:, g::2, :], p4(nb), b4("low0"), ALU.mult, after=[tp])
                self.V(v.tensor_tensor, TI[:, g::2, :], TI[:, g::2, :], b4("ident64"), ALU.add)
                yield 1.5
            ready = [self.last_v, self.last_v]
            xb, tb = (B1, B3), (B2, B4)
            for lv in range(1, 6):
                tx = []
                for g in range(2):
                    pe.wait(ready[g])
                    for i in range(4):
                        for co in chunks:
                            ins = pe.e.matmul(p4(xb[g])[co, i, :], MK[co, 2 * i + g, 0, :], TI[co, 2 * i + g, :],
                                              start=True, stop=True, skip_group_check=True)
                    tp = pe.done(ins)
                    tx.append(self.V(v.tensor_tensor, XG[g], p4(xb[g]), b4(f"low{lv}"), ALU.mult, after=[tp]))
                    next(later, None)
                    yield 0.9
                ready = []
                for g in range(2):
                    pe.wait(tx[g])
                    for i in range(4):
                        h = 2 * i + g
                        for co in chunks:
                            ins = pe.e.matmul(p4(xb[g])[co, i, :], XG[g][co, i, :], TIT[co, h, :], start=True,
                                              stop=True, skip_group_check=True)
                            if lv < 5:
                                ins = pe.e.matmul(p4(tb[g])[co, i, :], TIT[co, h, :], XG[g][co, i, :], start=True,
                                                  stop=True, skip_group_check=True)
                    tp = pe.done(ins)
                    t = self.V(v.tensor_tensor, TIT[:, g::2, :], TIT[:, g::2, :], p4(xb[g]), ALU.add, after=[tp])
                    if lv < 5:
                        t = self.V(v.tensor_tensor, TI[:, g::2, :], TI[:, g::2, :], p4(tb[g]), ALU.add)
                    ready.append(t)
                    next(later, None)
                    yield 1.6
            y = self.bank(B4)
            t_s = self.last_v
            for c, co in enumerate(chunks):
                pe.wait(t_s)
                for hp in range(4):
                    cols = slice(hp * P, (hp + 1) * P)
                    pe.e.matmul(self.bank(B0)[co, cols], TA[:, 0, hp, co], ST[:, hp, :], start=hp == 0, stop=False,
                                skip_group_check=True)
                for h in range(8):
                    hc = slice(h * HD, (h + 1) * HD)
                    ins = pe.e.matmul(self.bank(B0)[co, hc], MK[co, h, 2, :], val[co, hc], start=False, stop=True,
                                      skip_group_check=True)
                t = self.A(RHS[co, :], self.bank(B0)[co, :], ACT.Copy, after=[pe.done(ins)])
                for hp in range(4):
                    cols = slice(hp * P, (hp + 1) * P)
                    pe.e.matmul(y[co, cols], TA[:, 1, hp, co], ST[:, hp, :], start=hp == 0, stop=False,
                                skip_group_check=True)
                yield 2.5
                pe.wait(t)
                for h in range(8):
                    hc = slice(h * HD, (h + 1) * HD)
                    ins = pe.e.matmul(self.bank(B1)[co, hc], TIT[co, h, :], RHS[co, hc], start=True, stop=True,
                                      skip_group_check=True)
                t = self.A(U[co, :], self.bank(B1)[co, :], ACT.Copy, after=[pe.done(ins)])
                yield 1.6
                pe.wait(t)
                for hp in range(4):
                    cols = slice(hp * P, (hp + 1) * P)
                    pe.e.matmul(self.bank(B2)[:, cols], T3[co, cols], U[co, cols], start=True, stop=False,
                                skip_group_check=True)
                    ins = pe.e.matmul(self.bank(B2)[:, cols], T8[co, cols], val[co, cols], start=False, stop=True,
                                      skip_group_check=True)
                self.V(v.tensor_tensor, ST, ST, self.bank(B2).rearrange("p (h c) -> p h c", h=4), ALU.add,
                       after=[pe.done(ins)])
                t_s = self.V(v.tensor_tensor, ST, ST, WCM[:, c], ALU.mult, after=[t_wcm])
                for h in range(8):
                    hc = slice(h * HD, (h + 1) * HD)
                    pe.e.matmul(y[co, hc], MK[co, h, 1, :], U[co, hc], start=False, stop=False,
                                skip_group_check=True)
                    ins = pe.e.matmul(y[co, hc], MK[co, h, 3, :], val[co, hc], start=False, stop=True,
                                      skip_group_check=True)
                tp = pe.done(ins)
                yield 3
            t_y = self.A(r, y, ACT.Copy, after=[tp, t_bonus, t_at])
            later = self.group_norm(r, val, rows, GN, MU, sm3, bonus[t_], G[t_], [t_y, t_g])
        for _ in later:
            yield 1.5

    def group_norm(self, r, val, rows, tmp, MU, ss, bonus, gate, ready):
        v = self.dve.e
        h3 = lambda x: x.rearrange("p (h d) -> p h d", h=8)
        bc = lambda s: s.unsqueeze(2).to_broadcast([P, 8, HD])
        self.V(v.tensor_reduce, MU, h3(r), AX, ALU.add, after=ready)
        self.V(v.tensor_scalar, MU, MU, 1.0 / HD, None, ALU.mult)
        yield
        self.V(v.tensor_tensor, h3(r), h3(r), bc(MU), ALU.subtract)
        yield
        self.V(v.tensor_tensor, tmp, r, r, ALU.mult)
        yield
        self.V(v.tensor_reduce, ss, h3(tmp), AX, ALU.add)
        t = self.rstd(ss, ss, HD, GN_EPS, self.last_v)
        self.V(v.tensor_tensor, h3(tmp), h3(val), bc(bonus), ALU.mult)
        yield
        self.V(v.tensor_tensor, h3(r), h3(r), bc(ss), ALU.mult, after=[t])
        yield
        self.V(v.tensor_tensor, r, r, rows[:, R_LW:R_LW + 512], ALU.mult)
        yield
        self.V(v.tensor_tensor, r, r, rows[:, R_LB:R_LB + 512], ALU.add)
        yield
        self.V(v.tensor_tensor, r, r, tmp, ALU.add)
        yield
        self.t_rwkv = self.V(v.tensor_tensor, r, r, gate, ALU.mult)

    def memory_kv(self, par, banks):
        pv, act = self.PV, self.act
        self.KT = self.mem(4, S)
        K, VV = self.mem(NT, 512), self.mem(NT, 512)
        MEM = self.arena[:, self.top - 2048:self.top].rearrange("p (t d) -> p t d", t=NT)
        kt = self.KT.rearrange("p h k -> p (h k)")
        self.VV = VV
        act.wait(self.t_att)
        t_mem = self.load("d_mem", MEM, self.a["mem"].rearrange("(t p) d -> p t d", p=P))
        yield 4
        toks = self.norm_turn(MEM, pv[:, PV_MEM:PV_MEM + 8], banks, [t_mem, t_mem], slot=1, junk=kt)
        rs = self.rs[1]
        yield 6
        b = banks[:2]
        tok = yield from self.gemm_steps(b, 8, toks=toks, after=[toks])
        t_k = [self.A(K[:, t, :], self.bank(b[t]), ACT.Copy, after=[tok, self.t_rs[1]], scale=rs[t])
               for t in range(NT)][-1]
        tok = yield from self.gemm_steps(b, 8, after=[t_k])
        self.t_v = [self.A(VV[:, t, :], self.bank(b[t]), ACT.Copy, after=[tok], scale=rs[t]) for t in range(NT)][-1]
        self.t_kt = []
        tmp, sm = self.Z[:, 0, ZK:ZK + 512], self.SM[:, 116:120]
        for t_ in range(NT):
            self.last_v = t = yield from self.head_norm(K[:, t_, :], 4, P, tmp, sm, [t_k, self.last_v])
            yield 1
            self.t_kt.append(self.turn_plain(self.KT[:, :, t_ * P:(t_ + 1) * P], K[:, t_, :], 4, banks[2], t,
                                             gain=pv[:, PV_XK:PV_XK + 1], free=self.t_kt[-1:]))

    def cross_attention(self, halves):
        mark = self.top
        pe, v, pv = self.pe, self.dve.e, self.PV
        Q = O = self.mem(NT, 512)
        QT = self.mem(4, S)
        buffers = [(self.mem(512), self.mem(4, S), self.mem(8 * P)) for _ in range(NT)]
        assert self.top <= mark + RWKV_WORDS
        toks = self.norm_turn(self.X, pv[:, PV_X:PV_X + 8], [4, 5, 6, 7], halves)
        tok = self.gemm([0, 1], 8, toks=toks)
        t_q = [self.A(Q[:, t, :], self.bank(t), ACT.Copy, after=[tok, self.t_rs[0]], scale=self.rs[0][t])
               for t in range(NT)]

        def tile(t):
            tmp, SB, PT = buffers[t]
            tn = yield from self.head_norm(Q[:, t, :], 4, P, tmp, self.SM[:, 4 * t:4 * t + 4],
                                           [t_q[t], *toks, self.last_v])
            self.last_v = tn
            yield 1
            tq = self.turn_plain(QT[:, :, t * P:(t + 1) * P], Q[:, t, :], 4, 4 + 2 * t, tn,
                                 gain=pv[:, PV_XQ:PV_XQ + 1])
            yield 1
            pe.wait(tq, self.t_kt)
            for h in range(4):
                ins = pe.e.matmul(self.bank(4 + 2 * t + h // 2)[:, (h % 2) * S:(h % 2 + 1) * S],
                                  QT[:, h, t * P:(t + 1) * P], self.KT[:, h, :], start=True, stop=True,
                                  skip_group_check=True)
            ts = self.V(v.tensor_scalar, SB.rearrange("p h k -> p (h k)"), self.bank(4 + 2 * t, nb=2),
                        float(P) ** -0.5, None, ALU.mult, after=[pe.done(ins)])
            yield 2
            yield from self.softmax_pv(4, P, SB, S, lambda h, k: self.VV[:, k, h * P:(h + 1) * P], O[:, t, :], PT,
                                       ts, [self.t_v, ts], [2 + t, 4 + 2 * t], t, [], small=32 + 4 * t)

        self.weave(tile(0), tile(1))
        toks = self.turn([[O[:, t, k * P:(k + 1) * P] for t in range(NT)] for k in range(4)], [4, 5, 6, 7],
                         ready=self.last_v)
        self.top = mark
        return self.project(4, toks, after=[self.last_v])

    def block1(self):
        a = self.a
        self.top = 0
        self.XN, self.H, self.SG = self.mem(NT, D), self.mem(NT, 256), self.mem(NT, 256)
        rows, self.LORA, pv, self.Z = self.mem(R_N), self.mem(3, 512), self.mem(48), self.mem(NT, ZN)
        self.PV = pv
        fixed = self.top

        def sources(first):
            return [[self.Z[:, t, first + k * P:first + (k + 1) * P] for t in range(NT)] for k in range(4)]

        def side(par, t_rows, toks, mark):
            widths = [512, 512, ZN - 6 * 512]
            for n, w in enumerate(widths):
                g = 4 + n
                t_z = yield from self.column_group(self.Z, g, 512 * g, w, [0, 1], g)
            yield from self.attention(t_rows, rows, t_z, [0, 1, 2])
            self.top = mark
            yield from self.memory_kv(par, [0, 1, 2])
            self.t_turned = self.turn(sources(ZQ), [2], ready=(self.t_att, self.t_kt))
            yield 3
            yield from self.gemm_steps([0, 1], 4, toks=self.t_turned, after=[self.t_v])

        def layer(l):
            par = self.load("d_par", pv[:, 0:PV_N], a["pv1"][bass.ds(l, 1)].rearrange("a p n -> p (a n)"))
            t_rows = self.load("d_rows", rows, a["rows1"][bass.ds(l, 1)].rearrange("a b n -> (a b) n").to_broadcast(
                [P, R_N]))
            lora = self.load("d_lora", self.LORA, a["lora"][bass.ds(l, 1)].rearrange("a k p n -> p (a k) n"))
            halves = self.ffn(pv[:, PV_FFN1:PV_FFN1 + 8], 0, [par, par])
            toks = self.norm_turn(self.X, pv[:, PV_MIX:PV_MIX + 8], [4, 5, 6, 7], halves)
            t_z = self.column_loop(self.Z, 2, [*halves, *toks])
            for e in self.engines:
                e.wait(Token(self.s_tables, 32))
            self.top = fixed + RWKV_WORDS
            rec = self.rwkv(t_rows, rows, lora, [*t_z, *toks], [3, 4, 5, 6, 7], fixed)
            self.weave(rec, side(par, t_rows, toks, fixed + RWKV_WORDS),
                       pace=(1.0, 1.25))
            self.gemm([2, 3], 4, toks=self.t_turned, after=[self.t_kt, self.t_turned])
            toks = self.turn(sources(0), [4, 5, 6, 7], kt0=4, ready=(self.t_rwkv,))
            halves = []
            for h in range(2):
                tok = self.gemm([2 * h, 2 * h + 1], 4, kt0=4, toks=toks, first=False)
                halves.append(self.add_half(h, [2 * h, 2 * h + 1], 1.0, tok))
            self.top = fixed
            halves = self.cross_attention(halves)
            self.ffn(pv[:, PV_FFN2:PV_FFN2 + 8], NJ, halves)

        self.layers(UNITS1, layer)

    def layers(self, per, layer):
        base = self.done_units
        sems = [self.pe.sem.num, self.act.sem.num, self.dve.sem.num, self.pool.sem.num] + [s.num for s in
                                                                                           self.ev.values()]
        lo, hi = min(sems), max(sems)
        assert hi - lo + 1 == len(sems)
        with self.nc.Fori(0, DEPTH, engines=self.compute) as l:
            for e in self.engines:
                e.n, e.seen = 0, {}
            self.last_v = None
            self.unit, self.scope = 0, base + l * per
            self.scope_use = base // RING + l * (per // RING)
            self.layer_no = l
            self.loaded = {}
            layer(l)
            assert self.unit == per, (self.unit, per)
            self.nc.multi_engine_barrier(list(self.compute), sems_to_clear=range(lo, hi + 1))
        self.done_units += DEPTH * per
        for name in self.loaded:
            self.dma_base[name] += 16 * DEPTH
        for e in self.engines:
            e.n, e.seen = 0, {}
        self.last_v = None

    def block2(self):
        a = self.a
        pe = self.pe
        v = self.dve.e
        self.top = 0
        self.XN = self.mem(NT, D)
        Pm, rows, PW, pv, band = self.mem(NT, PN), self.mem(Q_N), self.mem(4, P), self.mem(24), self.mem(4, NT, S)
        rest = self.top
        t_band = self.load_band(band)

        def col(t, name, n=512, skip=0):
            return Pm[:, t, PC[name] + skip:PC[name] + skip + n]

        def by_feature(t, name):
            return col(t, name, 1024).rearrange("p (k s) -> p k s", k=4)

        merged = [col(t, "mg", D) for t in range(NT)]
        ZT, BG, CV = by_feature(0, "cx"), by_feature(1, "cx"), by_feature(0, "cb")
        POT = col(1, "mg", 1024, 2 * D).rearrange("p (k s) -> p k s", k=4)

        def conv_and_pool(ready, par, t_rows, t_pw, b):
            left = None
            for g2 in range(2):
                pe.wait(ready["pu"], t_band, left)
                for g in range(2 * g2, 2 * g2 + 2):
                    for s in range(NT):
                        ins = pe.e.matmul(self.bank(b)[:, (g % 2) * S:(g % 2 + 1) * S],
                                          col(s, "pu")[:, g * P:(g + 1) * P], band[:, g, s, :], start=s == 0,
                                          stop=s == 1, skip_group_check=True)
                tp = pe.done(ins)
                left = self.A(POT[:, 2 * g2:2 * g2 + 2, :], self.bank(b).rearrange("p (k s) -> p k s", k=2), ACT.Copy,
                              after=[tp])
            yield 4
            for t in range(NT):
                pe.wait(left, t_pw)
                for g in range(4):
                    ins = pe.e.matmul(self.bank(b)[:, g * P:(g + 1) * P], POT[:, g, t * P:(t + 1) * P], PW[:, g, :],
                                      start=True, stop=True, skip_group_check=True)
                tp = pe.done(ins)
                left = self.V(v.tensor_tensor, col(t, "pu"), self.bank(b), rows[:, Q_PS:Q_PS + 512], ALU.mult,
                              after=[tp, t_rows, *ready["pg"]])
                self.t_pool = self.V(v.tensor_tensor, col(t, "pu"), col(t, "pu"), col(t, "pg"), ALU.mult)
                yield 1.5
            yield 0
            t_in = []
            for t in range(NT):
                self.V(v.tensor_tensor, col(t, "cc"), col(t, "cc"), col(t, "cx"), ALU.mult, after=[ready["cg"]])
                t_in = self.V(v.tensor_tensor, col(t, "cb"), col(t, "cb"), col(t, "cg"), ALU.mult)
            yield 2
            for dst, src in ((ZT, "cc"), (BG, "cb")):
                for t in range(NT):
                    left = self.turn_plain(dst[:, :, t * P:(t + 1) * P], col(t, src), 4, b, [t_in, left])
                    yield 1.5
            for k in range(4):
                w = [pv[:, PW_CONV + 3 * k + j:PW_CONV + 3 * k + j + 1] for j in range(3)]
                self.V(v.tensor_scalar, CV[:, k, :], ZT[:, k, :], w[2], None, ALU.mult, after=[left, par])
                for j in (1, 2):
                    y = CV[:, k, j:]
                    self.V(v.scalar_tensor_tensor, y, ZT[:, k, 0:S - j], w[2 - j], y, ALU.mult, ALU.add)
            self.t_conv = self.V(v.tensor_tensor, CV, CV, BG, ALU.mult)
            self.t_branch = left
            yield 3

        def side(toks, par, t_rows, t_pw):
            silu = {"pg", "cg", "ag"}
            ready = {}
            extras = conv_and_pool(ready, par, t_rows, t_pw, 2)
            names = ["pu", "pg", "cb", "cc", "cx", "cg", "ag"] + ["mg"] * 6
            for n, name in enumerate(names):
                g = 5 + n
                func = ACT.Silu if name in silu else ACT.Sigmoid if name == "mg" else None
                ready[name] = yield from self.column_group(Pm, g, P2 + 512 * n, 512, [0, 1], g, func=func)
                if n:
                    yield next(extras, 0)
            t1 = self.A(self.AHI[:, 0:4, :], CV, ACT.Copy, after=[self.t_conv, *ready["mg"]])
            t1 = self.V(v.tensor_tensor, self.ALO[:, 0:4, :], CV, self.AHI[:, 0:4, :].bitcast(F32), ALU.subtract,
                        after=[t1])
            left = ready["mg"]
            for h in range(2):
                tok = yield from self.gemm_steps([0, 1], 4, toks=[t1] * 4, after=[left])
                left = self.merge(merged, col, 0, h, [0, 1], tok)
                yield 0
            toks = self.turn([[col(t, "pu")[:, k * P:(k + 1) * P] for t in range(NT)] for k in range(4)],
                             [2], kt0=4, ready=(self.t_pool, self.t_branch))
            yield 3
            for h in range(2):
                tok = yield from self.gemm_steps([0, 1], 4, kt0=4, toks=toks, after=[left])
                left = self.merge(merged, col, 2, h, [0, 1], tok)
            self.t_side = left

        def layer(l):
            par = self.load("d_par", pv[:, 0:PW_N], a["pv2"][bass.ds(l, 1)].rearrange("a p n -> p (a n)"))
            t_rows = self.load("d_rows", rows, a["rows2"][bass.ds(l, 1)].rearrange("a b n -> (a b) n").to_broadcast(
                [P, Q_N]))
            t_pw = self.load("d_lora", PW, a["poolw"][bass.ds(l, 1)].rearrange("a g p n -> p (a g) n"))
            toks = self.norm_turn(self.X, pv[:, PW_NORM:PW_NORM + 8], [4, 5, 6, 7], [par, par])
            self.column_loop(Pm, 2, toks)
            t_q = self.drain(self.column_group(Pm, 4, PC["ik"], 72, [0, 1], 4))
            self.top = rest
            self.weave(self.sparse_attention(Pm, col, rows, t_rows, [*t_q, *toks], [3, 4, 5, 6, 7]),
                       side(toks, par, t_rows, t_pw), pace=(1.8, 1.0))
            for t in range(NT):
                t1 = self.V(v.tensor_tensor, col(t, "q"), col(t, "q"), col(t, "ag"), ALU.mult, after=[self.t_side])
            toks = self.turn([[col(t, "q")[:, k * P:(k + 1) * P] for t in range(NT)] for k in range(4)],
                             [4, 5, 6, 7], ready=t1)
            ready = []
            for h in range(2):
                banks = [2 * h, 2 * h + 1]
                tok = self.gemm(banks, 4, toks=toks, after=[t1])
                ready += [self.merge(merged, col, 1, h, banks, tok)] * 4
            toks = self.turn([[merged[t][:, k * P:(k + 1) * P] for t in range(NT)] for k in range(8)], [4, 5, 6, 7],
                             ready=ready)
            self.project(8, toks, after=[ready[-1]])

        self.layers(UNITS2, layer)

    def merge(self, merged, col, branch, h, banks, tok):
        v = self.dve.e
        for t in range(NT):
            g = col(t, "mg", 512, branch * D + h * 512)
            last = self.V(v.tensor_tensor, g, self.bank(banks[t]), g, ALU.mult, after=[tok])
            if branch:
                m = merged[t][:, h * 512:(h + 1) * 512]
                last = self.V(v.tensor_tensor, m, m, g, ALU.add)
        return last

    def load_band(self, band):
        self.nc.gpsimd.dma_start(band.rearrange("p g s t -> p (g s t)"), self.a["band"]).then_inc(self.s_tables, 16)
        return Token(self.s_tables, 32 + 16)

    def sparse_attention(self, Pm, col, rows, t_rows, t_p, banks):
        dve, act, pe = self.dve, self.act, self.pe
        v = self.dve.e
        bt, s_banks = banks[0], banks[1:]
        xn = self.XN.rearrange("p a b -> p (a b)")
        QT, KT = (xn[:, i * 1024:(i + 1) * 1024].rearrange("p (h k) -> p h k", h=4) for i in range(2))
        IQT, IKT, SB, PT = self.mem(4, S), self.mem(S), self.mem(8, S), self.mem(16 * P)
        score, M2, SC = self.mem(S), self.mem(S), self.SM[:, 128:384]
        tmp = SB.rearrange("p a b -> p (a b)")
        IK2 = self.SM[:, 384:512]
        sm = self.SM[:, 0:16]
        cos, sin = (self.c(n).rearrange("p (t d) -> p t d", t=NT) for n in ("cos2", "sin2"))
        tq = []
        h8 = lambda x: x.rearrange("p (h d) -> p h d", h=8)
        for t in range(NT):
            t1 = self.rope(h8(col(t, "iq")), 8, 32, cos[:, t, :], sin[:, t, :], tmp, [self.last_v, t_p])
            self.last_v = t1
            yield 2
            tq.append(self.turn_plain(IQT[:, :, t * P:(t + 1) * P], col(t, "iq"), 4, s_banks[0], t1, free=tq[-1:]))
            ik = col(t, "ik", 64)
            t1 = self.rope(ik.unsqueeze(1), 1, 32, cos[:, t, :], sin[:, t, :], tmp, [self.last_v])
            self.last_v = t1
            for c in range(2):
                t1 = self.V(v.tensor_copy, IK2[:, c * 64:(c + 1) * 64], ik, after=tq)
            yield 1.5
            tq.append(self.turn_plain(IKT[:, t * P:(t + 1) * P].unsqueeze(1), IK2, 1, s_banks[1], t1))
        for t in range(NT):
            x = col(t, "q", 1024)
            t1 = yield from self.head_norm(x, 16, HD, tmp[:, 0:1024], sm, [self.last_v, t_rows],
                                           rows[:, Q_GQ:Q_GQ + 1024])
            t1 = self.rope(x.rearrange("p (h d) -> p h d", h=16), 16, 32, cos[:, t, :], sin[:, t, :], tmp,
                           [t1, self.last_v])
            self.last_v = t1
            yield 6
            for name, dst, b in (("q", QT, s_banks[2]), ("k", KT, s_banks[3])):
                tq.append(self.turn_plain(dst[:, :, t * P:(t + 1) * P], col(t, name), 4, b, t1, free=tq[-2:]))
            yield 1
        free = None
        last = t1

        def scores(A, B):
            pe.wait(tq, free, last)
            for h in range(8):
                bk, slot, po = s_banks[2 * (h // 4) + h % 2], (h // 2) % 2, HD * (h % 2)
                ins = pe.e.matmul(self.bank(bk)[:, slot * S:slot * S + nk], A[po:po + HD, h // 2, qs],
                                  B(h)[po:po + HD, 0:nk], start=True, stop=True, skip_group_check=True)
            return pe.done(ins)

        for qt in range(NT):
            nk = P * (qt + 1)
            qs = slice(qt * P, (qt + 1) * P)
            tp = scores(IQT, lambda h: IKT)
            yield 2
            act.wait(free, last)
            for n, bk in enumerate(s_banks):
                h0 = 4 * (n // 2) + n % 2
                t1 = self.A(SB[:, h0:h0 + 3:2, 0:nk], self.bank(bk).rearrange("p (s k) -> p s k", s=2)[:, :, 0:nk],
                            ACT.Relu, after=[tp], scale=HD ** -0.5)
            iw = col(qt, "iw", 8)
            sc = score[:, 0:nk]
            self.V(v.tensor_scalar, sc, SB[:, 0, 0:nk], iw[:, 0:1], None, ALU.mult, after=[t1])
            for h in range(1, 8):
                self.V(v.scalar_tensor_tensor, sc, SB[:, h, 0:nk], iw[:, h:h + 1], sc, ALU.mult, ALU.add)
            yield 4
            self.V(v.tensor_scalar, sc, sc, 8 ** -0.5, None, ALU.mult)
            self.V(v.tensor_tensor, sc[:, nk - P:nk], sc[:, nk - P:nk], self.c("causal"), ALU.add)
            top8 = self.SM[:, 104:112]
            work = [sc, SC[:, 0:nk]]
            for n in range(8):
                self.V(v.max, top8, work[n % 2])
                self.V(v.match_replace, work[1 - n % 2], top8, work[n % 2], TAKEN)
                yield 1
            m2 = M2[:, 0:nk]
            self.V(v.tensor_scalar, m2, sc, -2e38, NEG, ALU.is_gt, ALU.mult)
            t_m = self.V(v.tensor_tensor, m2[:, nk - P:nk], m2[:, nk - P:nk], self.c("causal"), ALU.add)
            last = t1
            tp = scores(QT, lambda h: KT[:, h // 2, :])
            yield 2
            for n, bk in enumerate(s_banks):
                h0 = 4 * (n // 2) + n % 2
                t1 = self.V(v.scalar_tensor_tensor, SB[:, h0:h0 + 3:2, 0:nk],
                            self.bank(bk).rearrange("p (s k) -> p s k", s=2)[:, :, 0:nk], HD ** -0.5,
                            m2.unsqueeze(1).to_broadcast([P, 2, nk]), ALU.mult, ALU.add, after=[tp, t_m])
            yield 2
            res = []
            yield from self.softmax_pv(8, HD, SB[:, :, 0:nk], nk, lambda h, k: col(k, "v")[:, h * HD:(h + 1) * HD],
                                       col(qt, "q"), PT, t1, [free, t1], [bt, *s_banks[1:]], s_banks[0], res)
            last, free = res

    def build(self):
        nc, a = self.nc, self.a
        self.POS = nc.alloc_sbuf_tensor("positions", [P, NT], I32)[:, :]
        n = COFF["ident"][1]
        assert COFF["ident"][0] == 0
        nc.scalar.dma_start(self.C[:, 0:n], a["consts"][:, 0:n]).then_inc(self.s_start, 16)
        x = a["x"].rearrange("(t p) d -> p t d", p=P)
        nc.sync.dma_start(self.X[:, 0, :], x[:, 0, :]).then_inc(self.s_start, 16)
        nc.scalar.dma_start(self.X[:, 1, :], x[:, 1, :]).then_inc(self.s_start, 16)
        nc.gpsimd.dma_start(self.C[:, n:], a["consts"][:, n:]).then_inc(self.s_tables, 16)
        nc.gpsimd.dma_start(self.POS, a["pos"]).then_inc(self.s_tables, 16)
        self.done_units = 0
        nc.tensor.sem_inc(self.s_mm, RING)
        nc.vector.sem_inc(self.s_lo, RING)
        nc.vector.memset(self.zero[:, :], 0.0)
        nc.vector.memset(self.minus_half[:, :], -0.5)
        z = nc.vector.memset(self.SM[:, :], 0.0)
        z.then_inc(self.s_set, 1)
        for e in self.engines:
            e.e.wait_ge(self.s_start, 48)
            e.e.wait_ge(self.s_set, 1)
        with nc.Fori(0, STREAM // RING, engines=(nc.sync.engine,)) as i:
            for u in range(RING):
                nc.sync.wait_ge(self.s_lo, i * RING + (u + 1))
                nc.sync.dma_start(self.raw[u][:, :, :],
                                  a["stream"][bass.ds(i * RING + u, 1)].rearrange("a p (k n) -> p (a k) n", k=2)
                                  ).then_inc(self.s_load[u], 16)
        self.unit = -AHEAD
        self.scope, self.scope_use = 0, 0
        for _ in range(AHEAD):
            self.split_next()
            self.unit += 1
        self.block1()
        self.block2()
        nc.sync.wait_ge(self.s_load[RING - 1], 16 * (STREAM // RING))
        nc.vector.drain().then_inc(self.s_out, 1)
        nc.scalar.wait_ge(self.s_out, 1)
        nc.scalar.dma_start(a["out"].rearrange("(t p) d -> p t d", p=P), self.X[:, :, :]).then_inc(self.s_out, 16)
        nc.scalar.wait_ge(self.s_out, 17)


def two_pi_parts():
    rest, parts = 2 * np.pi, []
    for bits in (2.0 ** 6, 2.0 ** 17):
        parts.append(float(np.floor(rest * bits) / bits))
        rest -= parts[-1]
    return parts + [float(np.float32(rest))]


TWO_PI = two_pi_parts()
PI_IN = float(np.nextafter(np.float32(np.pi), np.float32(0)))


def units(w, cols=None):
    k, n = w.shape
    pad = -n % 512
    if pad:
        w = np.concatenate([w, np.zeros((k, pad), w.dtype)], 1)
    return w.reshape(k // 256, 2, P, (n + pad) // 512, 512).transpose(3, 0, 2, 1, 4).reshape(-1, P, 1024)


def ffn_units(w_in, w_out):
    both = np.stack([w_in[:, :FFN].reshape(D, NJ, 256), w_in[:, FFN:].reshape(D, NJ, 256)], 2)
    both = both.reshape(4, 2, P, NJ, 512).transpose(3, 0, 2, 1, 4).reshape(NJ, 4, P, 1024)
    out = w_out.reshape(NJ, 2, P, 2, 512).transpose(0, 3, 2, 1, 4).reshape(NJ, 2, P, 1024)
    seq = [both[0]]
    for j in range(1, NJ):
        seq += [both[j], out[j - 1]]
    return np.concatenate(seq + [out[NJ - 1]])


def kernel(**inputs):
    import concourse.bacc as bacc
    from concourse.bass_utils import run_bass_kernel_spmd as run

    n = {k: np.asarray(v) for k, v in inputs.items()}
    seq, pv1, rows1, lora, pv2, rows2, poolw = [], [], [], [], [], [], []
    for l in range(DEPTH):
        w = n["mix_w_in"][l]
        f0, m0, r0 = 0, 772, 1540
        w = np.concatenate([w[:, r0:], w[:, 0:256], w[:, m0:m0 + 256], w[:, 256:512], w[:, m0 + 256:m0 + 512],
                            w[:, 512:768], w[:, m0 + 512:m0 + 768], w[:, 768:772]], 1)
        w_o = n["mix_w_out"][l]
        w_o = units(np.concatenate([w_o[:256], w_o[768:], w_o[256:768]]))
        seq += [ffn_units(n["ffn1_w_in"][l], n["ffn1_w_out"][l]), units(w), units(n["xattn_w_kv"][l]),
                w_o[[0, 1, 4, 5, 2, 3, 6, 7]], units(n["xattn_w_q"][l]), units(n["xattn_w_out"][l]),
                ffn_units(n["ffn2_w_in"][l], n["ffn2_w_out"][l])]
        pv1.append(np.concatenate([n[k][l].reshape(8, P).T for k in
                                   ("ffn1_norm", "mix_norm", "xattn_norm", "xattn_mem_norm", "ffn2_norm")]
                                  + [n[k][l].reshape(P, 1) for k in ("xattn_q_gain", "xattn_k_gain")], 1))
        four = lambda g: [n[g][l]] * 4
        rows1.append(np.concatenate([n["rwkv_mu"][l], n["rwkv_w0"][l], n["rwkv_a0"][l], n["rwkv_k_k"][l],
                                     n["rwkv_k_a"][l], n["rwkv_r_k"][l].reshape(-1), n["rwkv_ln_w"][l],
                                     n["rwkv_ln_b"][l], *four("fox_q_gain"), *four("moba_q_gain"),
                                     *four("fox_k_gain"), *four("moba_k_gain"), n["fox_f_bias"][l]])[None])
        g2 = n["rwkv_g2"][l]
        lora.append(np.stack([np.concatenate([n["rwkv_w2"][l], n["rwkv_a2"][l]]), g2[:P],
                              np.concatenate([g2[P:], np.zeros((P - 32, 512), g2.dtype)])]))
    for l in range(DEPTH):
        w = n["w_in_2"][l]
        q0, i0, p0, c0 = 2048, 4608, 4680, 0
        rest = np.concatenate([w[:, p0:p0 + 1024], w[:, c0:q0], w[:, q0 + 1536:q0 + 2048], w[:, p0 + 1024:]], 1)
        seq += [units(np.concatenate([w[:, q0:q0 + 1536], w[:, i0 - 512:i0]], 1)), units(w[:, i0:p0]), units(rest),
                units(n["w_out_conv_2"][l]), units(n["w_out_pool_2"][l]), units(n["w_out_attn_2"][l]),
                units(n["w_o_2"][l])]
        pv2.append(np.concatenate([n["norm_g_2"][l].reshape(8, P).T,
                                   n["conv_w_2"][l].reshape(3, 4, P).transpose(2, 1, 0).reshape(P, 12)], 1))
        rows2.append(np.concatenate([np.tile(n["q_norm_g_2"][l], 8), np.tile(n["k_norm_g_2"][l], 8),
                                     n["pool_scale_2"][l]])[None])
        poolw.append(n["pool_w_2"][l])
    stream = np.concatenate(seq + [np.zeros((RING, P, 1024), np.float32)])
    assert stream.shape[0] == STREAM, (stream.shape, STREAM)
    arrays = {"stream": stream, "pv1": np.stack(pv1), "rows1": np.stack(rows1), "lora": np.stack(lora),
              "pv2": np.stack(pv2), "rows2": np.stack(rows2), "poolw": np.stack(poolw),
              "consts": np.concatenate([v for k, v in CONST.items() if k != "band"], 1), "band": CONST["band"],
              "x": n["x"][0], "mem": n["mem"][0], "pos": n["positions"].reshape(NT, P).T}
    arrays = {k: np.ascontiguousarray(v) for k, v in arrays.items()}
    nc = bacc.Bacc("TRN2", target_bir_lowering=False, num_devices=1)
    aps = {k: nc.dram_tensor(k, list(v.shape), I32 if k == "pos" else F32, kind="ExternalInput").ap()
           for k, v in arrays.items()}
    aps["out"] = nc.dram_tensor("out", [S, D], F32, kind="ExternalOutput").ap()
    Program(nc, aps).build()
    r = run(nc, [arrays], core_ids=[0])
    return r.results[0]["out"].reshape(1, S, D)
```
